# Optimizing a Trainium2 kernel written in Bass

```python
import jax, jax.numpy as jnp
from jax import lax
import numpy as np

D_MODEL = 1024
BATCH = 1
SEQ = 512
DEPTH = 1
DEC_BATCH = 8
DEC_SEQ = 4
PAST_LEN = 4096
PAGE_SIZE = 128

D_CONV = D_MODEL // 2
D_ATTN = D_MODEL - D_CONV
HEAD_DIM = 64
N_HEADS = D_ATTN // HEAD_DIM
N_KV = 2
GQA_R = N_HEADS // N_KV
N_BR = 3
CONV_W = 3
BLK = 64
N_SEL = 16
WINDOW = 512
WIN_QB = 128
NW = WINDOW // WIN_QB
SEL_QC = 32
CMP_HID = HEAD_DIM
D_FF = ((8 * D_MODEL // 3) + 127) // 128 * 128
KV_W = 2 * N_KV * HEAD_DIM
D_IN = 3 * D_CONV + D_ATTN + 3 * KV_W + N_BR * N_HEADS
ALPHA = (2.0 * DEPTH) ** 0.25
BETA = (8.0 * DEPTH) ** -0.25
SCALE = HEAD_DIM ** -0.5
LN_EPS = 1e-5
NEG = -1e30
FORCE = 1e4

kernel_name = 'hybrid_shortconv_nsa_macaron_deepnorm_step'

def layer_norm(x, g, b):
    xf = x.astype(jnp.float32)
    mu = xf.mean(-1, keepdims=True)
    var = jnp.square(xf - mu).mean(-1, keepdims=True)
    return ((xf - mu) * lax.rsqrt(var + LN_EPS) * g + b).astype(x.dtype)

def post_ln(x, sub, g, b):
    return layer_norm(ALPHA * x + sub, g, b)

def swiglu(x, w_gate, w_up, w_down):
    return (jax.nn.silu(x @ w_gate) * (x @ w_up)) @ w_down

def masked_softmax(s, mask):
    s = jnp.where(mask, s.astype(jnp.float32), NEG)
    return jnp.where(mask, jax.nn.softmax(s, axis=-1), 0.0)

def project(h, w_in, b_in):
    n, t = h.shape[:2]
    z = h @ w_in + b_in
    sizes = [D_CONV, D_CONV, D_CONV, D_ATTN, KV_W, KV_W, KV_W]
    cuts = []
    acc = 0
    for s in sizes:
        acc += s
        cuts.append(acc)
    cb, cc, ch, q, kv_cmp, kv_sel, kv_win, g = jnp.split(z, cuts, axis=-1)
    kvshape = (n, t, 2, N_KV, HEAD_DIM)
    gates = jax.nn.sigmoid(g.astype(jnp.float32)).reshape(n, t, N_BR, N_HEADS).astype(h.dtype)
    return (cb, cc, ch, q.reshape(n, t, N_HEADS, HEAD_DIM), kv_cmp.reshape(kvshape),
            kv_sel.reshape(kvshape), kv_win.reshape(kvshape), gates)

def short_conv(u, prev, w_conv):
    t = u.shape[1]
    ext = jnp.concatenate([prev, u], axis=1)
    z = sum(ext[:, i:i + t] * w_conv[i] for i in range(CONV_W))
    return z, ext[:, -(CONV_W - 1):]

def compress(kv, w1, w2, pe):
    n, L = kv.shape[:2]
    nb = L // BLK
    blk = kv[:, :nb * BLK].reshape(n, nb, BLK, 2, N_KV, HEAD_DIM) + pe[:, :, None, :]
    hid = jax.nn.silu(jnp.einsum('nbpcgd,cpdh->nbcgh', blk, w1))
    return jnp.einsum('nbcgh,chd->nbcgd', hid, w2)

def cmp_attn(q, q_pos, kc):
    n, tq = q.shape[:2]
    nb = kc.shape[1]
    qg = q.reshape(n, tq, N_KV, GQA_R, HEAD_DIM)
    s = jnp.einsum('nqgrd,nbgd->ngrqb', qg, kc[:, :, 0]) * SCALE
    blk_end = (jnp.arange(nb) + 1) * BLK - 1
    p = masked_softmax(s, blk_end[None, :] <= q_pos[:, None])
    o = jnp.einsum('ngrqb,nbgd->nqgrd', p.astype(kc.dtype), kc[:, :, 1])
    return o.reshape(n, tq, N_HEADS, HEAD_DIM), p.sum(axis=2)

def select_blocks(imp, q_pos, n_blocks):
    n_cand = max(n_blocks, N_SEL)
    imp = jnp.pad(imp, ((0, 0), (0, 0), (0, 0), (0, n_cand - imp.shape[-1])))
    j = jnp.arange(n_cand)[None, :]
    cur = (q_pos // BLK)[:, None]
    score = jnp.where(j > cur, NEG, imp)
    score = jnp.where((j == 0) | (j == cur) | (j == cur - 1), FORCE, score)
    _, idx = lax.top_k(score, N_SEL)
    return idx

def to_blocks(kv):
    n, t = kv.shape[:2]
    nb = -(-t // BLK)
    kv = jnp.pad(kv, ((0, 0), (0, nb * BLK - t), (0, 0), (0, 0), (0, 0)))
    return kv.reshape(n, nb, BLK, 2, N_KV, HEAD_DIM)

def gather_blocks(new_blocks, idx, n_past_blk, pool_blocks=None, page_table=None):
    n = new_blocks.shape[0]
    nidx = jnp.arange(n)[:, None, None, None]
    gidx = jnp.arange(N_KV)[None, :, None, None]
    j_new = jnp.clip(idx - n_past_blk, 0, new_blocks.shape[1] - 1)
    out = new_blocks[nidx, j_new, :, :, gidx]
    if pool_blocks is not None:
        bpp = PAGE_SIZE // BLK
        jp = jnp.clip(idx, 0, n_past_blk - 1)
        page = jnp.take_along_axis(page_table, (jp // bpp).reshape(n, -1), axis=1).reshape(jp.shape)
        past = pool_blocks[page * bpp + jp % bpp, :, :, gidx]
        out = jnp.where((idx < n_past_blk)[..., None, None, None], past, out)
    return out

def sel_attn(q, q_pos, g, idx):
    n, tq = q.shape[:2]
    qg = q.reshape(n, tq, N_KV, GQA_R, HEAD_DIM)
    k = g[..., 0, :]
    v = g[..., 1, :]
    s = jnp.einsum('nqgrd,ngqspd->ngrqsp', qg, k) * SCALE
    kpos = idx[..., None] * BLK + jnp.arange(BLK)
    mask = (kpos <= q_pos[:, None, None])[:, :, None]
    p = masked_softmax(s.reshape(n, N_KV, GQA_R, tq, -1), mask.reshape(n, N_KV, 1, tq, -1))
    o = jnp.einsum('ngrqk,ngqkd->nqgrd', p.astype(v.dtype), v.reshape(n, N_KV, tq, -1, HEAD_DIM))
    return o.reshape(n, tq, N_HEADS, HEAD_DIM)

def win_attn(q, k, v, q_pos, k_pos):
    n, tq = q.shape[:2]
    qg = q.reshape(n, tq, N_KV, GQA_R, HEAD_DIM)
    s = jnp.einsum('nqgrd,nkgd->ngrqk', qg, k) * SCALE
    d = q_pos[:, None] - k_pos[None, :]
    p = masked_softmax(s, (d >= 0) & (d < WINDOW) & (k_pos[None, :] >= 0))
    o = jnp.einsum('ngrqk,nkgd->nqgrd', p.astype(v.dtype), v)
    return o.reshape(n, tq, N_HEADS, HEAD_DIM)

def win_prompt(q, kv):
    n, t = q.shape[:2]
    nqb = t // WIN_QB
    kvp = jnp.pad(kv, ((0, 0), (WINDOW, 0), (0, 0), (0, 0), (0, 0)))
    kvb = kvp.reshape(n, nqb + NW, WIN_QB, 2, N_KV, HEAD_DIM)
    band = jnp.concatenate([kvb[:, o:o + nqb] for o in range(NW + 1)], axis=2)
    kp = jnp.arange(-WINDOW, t).reshape(nqb + NW, WIN_QB)
    kp = jnp.concatenate([kp[o:o + nqb] for o in range(NW + 1)], axis=1)
    qp = jnp.arange(t).reshape(nqb, WIN_QB)

    def one(args):
        qb, kb, qpb, kpb = args
        return win_attn(qb, kb[:, :, 0], kb[:, :, 1], qpb, kpb)

    o = lax.map(one, (q.reshape(n, nqb, WIN_QB, N_HEADS, HEAD_DIM).swapaxes(0, 1),
                      band.swapaxes(0, 1), qp, kp))
    return o.swapaxes(0, 1).reshape(n, t, N_HEADS, HEAD_DIM)

def merge(gates, o_cmp, o_sel, o_win, y_conv, w_out):
    n, t = y_conv.shape[:2]
    o = (gates[:, :, 0, :, None] * o_cmp + gates[:, :, 1, :, None] * o_sel
         + gates[:, :, 2, :, None] * o_win)
    return jnp.concatenate([o.reshape(n, t, D_ATTN), y_conv], axis=-1) @ w_out

def mix_prompt(h, w_in, b_in, w_conv, cmp_w1, cmp_w2, cmp_pe, w_out):
    n, t = h.shape[:2]
    cb, cc, ch, q, kv_cmp, kv_sel, kv_win, gates = project(h, w_in, b_in)
    z, conv_state = short_conv(cc * ch, jnp.zeros((n, CONV_W - 1, D_CONV), h.dtype), w_conv)
    y_conv = cb * z
    q_pos = jnp.arange(t)
    o_cmp, imp = cmp_attn(q, q_pos, compress(kv_cmp, cmp_w1, cmp_w2, cmp_pe))
    idx = select_blocks(imp, q_pos, -(-t // BLK))
    blocks = to_blocks(kv_sel)
    nc = t // SEL_QC

    def sel_chunk(args):
        qc, pc, ic = args
        return sel_attn(qc, pc, gather_blocks(blocks, ic, 0), ic)

    o_sel = lax.map(sel_chunk, (q.reshape(n, nc, SEL_QC, N_HEADS, HEAD_DIM).swapaxes(0, 1),
                                q_pos.reshape(nc, SEL_QC),
                                idx.reshape(n, N_KV, nc, SEL_QC, N_SEL).transpose(2, 0, 1, 3, 4)))
    o_sel = o_sel.swapaxes(0, 1).reshape(n, t, N_HEADS, HEAD_DIM)
    o_win = win_prompt(q, kv_win)
    out = merge(gates, o_cmp, o_sel, o_win, y_conv, w_out)
    return out, kv_cmp, kv_sel, kv_win[:, -min(WINDOW, t):], conv_state

def mix_sample(h, cmp_pool, sel_pool, win_buf, conv_buf, page_table,
               w_in, b_in, w_conv, cmp_w1, cmp_w2, cmp_pe, w_out):
    n, s = h.shape[:2]
    past = page_table.shape[1] * PAGE_SIZE
    cb, cc, ch, q, kv_cmp, kv_sel, kv_win, gates = project(h, w_in, b_in)
    z, conv_state = short_conv(cc * ch, conv_buf, w_conv)
    y_conv = cb * z
    q_pos = past + jnp.arange(s)
    past_cmp = cmp_pool[page_table].reshape(n, past, 2, N_KV, HEAD_DIM)
    ctx_cmp = jnp.concatenate([past_cmp, kv_cmp], axis=1)
    o_cmp, imp = cmp_attn(q, q_pos, compress(ctx_cmp, cmp_w1, cmp_w2, cmp_pe))
    idx = select_blocks(imp, q_pos, -(-(past + s) // BLK))
    pool_blocks = sel_pool.reshape(-1, BLK, 2, N_KV, HEAD_DIM)
    g = gather_blocks(to_blocks(kv_sel), idx, past // BLK, pool_blocks, page_table)
    o_sel = sel_attn(q, q_pos, g, idx)
    ctx_win = jnp.concatenate([win_buf, kv_win], axis=1)
    k_pos = jnp.arange(past - win_buf.shape[1], past + s)
    o_win = win_attn(q, ctx_win[:, :, 0], ctx_win[:, :, 1], q_pos, k_pos)
    out = merge(gates, o_cmp, o_sel, o_win, y_conv, w_out)
    return out, kv_cmp, kv_sel, ctx_win[:, -min(WINDOW, past + s):], conv_state

def setup_inputs(seed: int = 0) -> dict:
    key = jax.random.key(seed)
    ks = iter(jax.random.split(key, 40))

    def nrm(shape, scale):
        return jax.random.normal(next(ks), shape, jnp.float32) * scale

    n_pages = PAST_LEN // PAGE_SIZE
    n_phys = (5 * DEC_BATCH * n_pages + 3) // 4
    win_rows = min(WINDOW, PAST_LEN)
    d = D_MODEL
    inp = {}
    inp['x_prompt'] = nrm((BATCH, SEQ, d), 1.0)
    inp['x_sample'] = nrm((DEC_BATCH, DEC_SEQ, d), 1.0)
    inp['cache_cmp_kv'] = nrm((DEPTH, n_phys, PAGE_SIZE, 2, N_KV, HEAD_DIM), 1.0)
    inp['cache_sel_kv'] = nrm((DEPTH, n_phys, PAGE_SIZE, 2, N_KV, HEAD_DIM), 1.0)
    inp['state_win_kv'] = nrm((DEPTH, DEC_BATCH, win_rows, 2, N_KV, HEAD_DIM), 1.0)
    inp['state_conv'] = nrm((DEPTH, DEC_BATCH, CONV_W - 1, D_CONV), 1.0)
    perm = jax.random.permutation(next(ks), n_phys)
    inp['page_table'] = perm[:DEC_BATCH * n_pages].reshape(DEC_BATCH, n_pages).astype(jnp.int32)
    inp['ffa_gate'] = nrm((DEPTH, d, D_FF), d ** -0.5)
    inp['ffa_up'] = nrm((DEPTH, d, D_FF), d ** -0.5)
    inp['ffa_down'] = nrm((DEPTH, D_FF, d), BETA * D_FF ** -0.5)
    inp['ln1_g'] = 1.0 + nrm((DEPTH, d), 0.02)
    inp['ln1_b'] = nrm((DEPTH, d), 0.02)
    inp['w_in'] = nrm((DEPTH, d, D_IN), d ** -0.5)
    inp['b_in'] = nrm((DEPTH, D_IN), 0.02)
    inp['w_conv'] = nrm((DEPTH, CONV_W, D_CONV), CONV_W ** -0.5)
    inp['cmp_w1'] = nrm((DEPTH, 2, BLK, HEAD_DIM, CMP_HID), (BLK * HEAD_DIM) ** -0.5)
    inp['cmp_w2'] = nrm((DEPTH, 2, CMP_HID, HEAD_DIM), CMP_HID ** -0.5)
    inp['cmp_pe'] = nrm((DEPTH, BLK, 2, HEAD_DIM), 0.1)
    inp['w_out'] = nrm((DEPTH, d, d), BETA * d ** -0.5)
    inp['ln2_g'] = 1.0 + nrm((DEPTH, d), 0.02)
    inp['ln2_b'] = nrm((DEPTH, d), 0.02)
    inp['ffb_gate'] = nrm((DEPTH, d, D_FF), d ** -0.5)
    inp['ffb_up'] = nrm((DEPTH, d, D_FF), d ** -0.5)
    inp['ffb_down'] = nrm((DEPTH, D_FF, d), BETA * D_FF ** -0.5)
    inp['ln3_g'] = 1.0 + nrm((DEPTH, d), 0.02)
    inp['ln3_b'] = nrm((DEPTH, d), 0.02)
    return inp

def reference(x_prompt, x_sample, cache_cmp_kv, cache_sel_kv, state_win_kv, state_conv, page_table,
              ffa_gate, ffa_up, ffa_down, ln1_g, ln1_b, w_in, b_in, w_conv, cmp_w1, cmp_w2, cmp_pe,
              w_out, ln2_g, ln2_b, ffb_gate, ffb_up, ffb_down, ln3_g, ln3_b):
    yp, ys = x_prompt, x_sample
    pc, psl, pw, pcv, sc, ssl, sw, scv = [], [], [], [], [], [], [], []
    for l in range(DEPTH):
        yp = post_ln(yp, 0.5 * swiglu(yp, ffa_gate[l], ffa_up[l], ffa_down[l]), ln1_g[l], ln1_b[l])
        ys = post_ln(ys, 0.5 * swiglu(ys, ffa_gate[l], ffa_up[l], ffa_down[l]), ln1_g[l], ln1_b[l])
        mp, a, b, c, e = mix_prompt(yp, w_in[l], b_in[l], w_conv[l], cmp_w1[l], cmp_w2[l], cmp_pe[l], w_out[l])
        pc.append(a); psl.append(b); pw.append(c); pcv.append(e)
        ms, a, b, c, e = mix_sample(ys, cache_cmp_kv[l], cache_sel_kv[l], state_win_kv[l], state_conv[l],
                                    page_table, w_in[l], b_in[l], w_conv[l], cmp_w1[l], cmp_w2[l],
                                    cmp_pe[l], w_out[l])
        sc.append(a); ssl.append(b); sw.append(c); scv.append(e)
        yp = post_ln(yp, mp, ln2_g[l], ln2_b[l])
        ys = post_ln(ys, ms, ln2_g[l], ln2_b[l])
        yp = post_ln(yp, 0.5 * swiglu(yp, ffb_gate[l], ffb_up[l], ffb_down[l]), ln3_g[l], ln3_b[l])
        ys = post_ln(ys, 0.5 * swiglu(ys, ffb_gate[l], ffb_up[l], ffb_down[l]), ln3_g[l], ln3_b[l])
    return (yp, ys, jnp.stack(pc), jnp.stack(psl), jnp.stack(pw), jnp.stack(pcv),
            jnp.stack(sc), jnp.stack(ssl), jnp.stack(sw), jnp.stack(scv))


_drawn_inputs = setup_inputs


def setup_inputs(seed=0):
    import zlib

    import numpy as np

    out = dict(_drawn_inputs(seed))
    spreads = {}
    factors = {'cache_cmp_kv': 3.346,
     'cache_sel_kv': 5.694,
     'cmp_pe': 6.684,
     'ln2_g': 2.789,
     'ln2_b': 2.91,
     'ln3_g': 2.86,
     'ln3_b': 2.806}
    for name, (base, spread) in spreads.items():
        noise = np.random.default_rng([zlib.crc32(name.encode()), seed]).standard_normal(out[name].shape)
        drawn = base * np.exp(spread * noise) if base else spread * noise
        out[name] = __import__('jax').numpy.asarray(drawn.astype(out[name].dtype))
    for name, factor in factors.items():
        out[name] = (out[name] * factor).astype(out[name].dtype)
    return out
```

```python
from contextlib import ExitStack

import concourse.bass as bass
from concourse import mybir

F32 = mybir.dt.float32
F32R = mybir.dt.float32r
BF16 = mybir.dt.bfloat16
I32 = mybir.dt.int32
ALU = mybir.AluOpType
ACT = mybir.ActivationFunctionType
AX = mybir.AxisListType.X
DS = bass.ds

D = 1024
SEQ = 512
NB = 8
NQ = 4
NS = NB * NQ
T = SEQ + NS
HALF = T // 2
KC = D // 128
FF = 2816
FT = FF // 128
FH = FT // 2
DC = 512
HD = 64
G = 2
R = 4
NH = G * R
BR = 3
BLK = 64
PAGE = 128
NPG = 32
NPHYS = 320
NBLK = NPG * 2
KVW = 256
QT = SEQ // 128
CH = 4
PC = NPG // CH
WIN = 512
N_SEL = 16
ALPHA = 2.0 ** 0.25
SCALE = HD ** -0.5
EPS = 1e-5
NEG = -1e30
ZC = 3 * DC // 128
ZR = 11
Q0, KV0, G0 = 0, 4, 10
OFF_Q = 3 * DC
OFF_KV = OFF_Q + NH * HD
OFF_G = OFF_KV + 3 * KVW
OB = 130

R_LN = 0
R_BC, R_BQ, R_BKV, R_BG = 48, 60, 64, 70
R_WC = 71
R_ALL = 83


USES = {"ffa": (0, 0), "proj": (FT, FT), "out": (FT + 12, FT + 11), "ffb": (FT + 16, FT + 15)}
FILLS = {"ffa": (0, 0), "proj": (FT, FT), "out": (FT + 24, FT + 22), "ffb": (FT + 36, FT + 34)}
PER_FILL = {"ffa": 1, "proj": 2, "out": 3, "ffb": 1}
NT = ZC + ZR


C_NCM, C_CSUM, C_M1, C_M2, C_CNT, C_NNM, C_NSUM, C_PNM, C_PSUM = 0, 2, 4, 20, 36, 38, 42, 46, 62
C_REC, C_GS, C_MX, C_KEY, C_LO, C_HI, C_Q = 78, 80, 82, 114, 115, 117, 119
C_F = 120


class Steps:

    def __init__(self, eng, sem):
        self.eng, self.sem, self.n, self.i = eng, sem, 0, None

    def __call__(self, ins):
        ins.then_inc(self.sem, 1)
        self.n += 1
        return ins

    def settle(self):
        if self.i is None:
            self.eng.wait_ge(self.sem, self.n)
        else:
            i, first, per, start = self.i
            self.eng.wait_ge(self.sem, (i - first) * per + self.n)

    def enter(self, i, first, per):
        self.i = (i, first, per, self.n)

    def leave(self, times):
        _, _, per, start = self.i
        assert self.n - start == per, (self.n - start, per)
        self.i = None
        self.n = start + per * times


def trunk(nc, x_prompt, x_sample, cache_cmp, cache_sel, state_win, state_conv, page_table,
          ffa_gate, ffa_up, ffa_down, ln1_g, ln1_b, w_in, b_in, w_conv, cmp_w1, cmp_w2, cmp_pe,
          w_out, ln2_g, ln2_b, ffb_gate, ffb_up, ffb_down, ln3_g, ln3_b,
          y_prompt, y_sample, p_cmp, p_sel, p_win, p_conv, s_cmp, s_sel, s_win, s_conv):
    ctx = ExitStack()
    with ctx:
        def sb(name, shape, dt=F32, stack=ctx):
            return stack.enter_context(nc.sbuf_tensor(name, shape, dt))

        def sem(name):
            return ctx.enter_context(nc.semaphore(name))

        ident = sb("ident", [128, 128])
        identb = sb("identb", [128, 128], BF16)
        causal = sb("causal", [128, 128], BF16)
        mean_w = sb("mean_w", [128, 128])
        eps = sb("eps", [128, 1])
        par = sb("par", [128, 96])
        x = sb("x", [128, KC, T])
        pages_sb = sb("pages_sb", [1, NB * NPG], I32)
        kc_all = sb("kc_all", [128, NB, NBLK])
        vc_all = sb("vc_all", [64, NB, 128])
        w2 = sb("w2", [128, HD])
        pe_sb = sb("pe_sb", [64, 2, HD])
        hid_bias = sb("hid_bias", [128, 1])
        same = sb("same", [128, 128])
        fold = sb("fold", [128, NS])
        win_mask = sb("win_mask", [128, 128], BF16)
        new_mask = sb("new_mask", [128, 2, NS], BF16)
        qbd = sb("qbd", [128, NB, NS])
        qn = [sb(f"qn{n}", [128, NS]) for n in range(2)]
        gate_p = sb("gate_p", [128, QT, BR * NH])
        blk_neg = sb("blk_neg", [128, QT, 8])
        blk_ok = sb("blk_ok", [128, QT, 8])
        diag = sb("diag", [64, R, G])
        selneg = sb("selneg", [128, 2, NBLK], BF16)
        selt = sb("selt", [128, NB, 16], BF16)
        small = sb("small", [128, 160])
        u1 = ExitStack()
        xh = sb("xh", [128, KC, T], F32R, u1)
        xl = sb("xl", [128, KC, T], F32R, u1)
        u1.close()
        up = ExitStack()
        w1p = sb("w1p", [128, 2, HD, HD], F32, up)
        up.close()
        page0 = sb("page0", [128, 2 * KC * T])
        ring = ExitStack()
        graw = [sb(f"graw{n}", [128, KC, 128], F32, ring) for n in range(2)]
        ghi = [sb(f"ghi{n}", [128, KC, 128], F32R, ring) for n in range(2)]
        glo = [sb(f"glo{n}", [128, KC, 128], F32R, ring) for n in range(2)]
        ring.close()
        mid = ExitStack()
        cb = sb("cb", [128, NB, 2, OB], F32, mid)
        po = sb("po", [128, QT, R, 128], F32, mid)
        pcs = sb("pcs", [128, 2, NBLK], F32, mid)
        pct = sb("pct", [64, 2, 128], F32, mid)
        ocs = sb("ocs", [128, 2, 128], F32, mid)
        imp = sb("imp", [128, 2, NBLK], F32, mid)
        rest = sb("rest", [128, 2, NBLK], F32, mid)
        gt = sb("gt", [128, 2, NBLK], F32, mid)
        eq = sb("eq", [128, 2, NBLK], F32, mid)
        pre = sb("pre", [128, 2, NBLK], F32, mid)
        one = sb("one", [128, NBLK], F32, mid)
        gate_s = sb("gate_s", [128, BR * R, NS], F32, mid)
        pnew = sb("pnew", [128, 4, NS], F32, mid)
        mid.close()
        in_ring = sb("in_ring", [128, 6 * KC * 128])
        ffn = ExitStack()
        hh = sb("hh", [128, FH, T], F32R, ffn)
        hl = sb("hl", [128, FH, T], F32R, ffn)
        draw = [sb(f"draw{n}", [128, FH, 128], F32, ffn) for n in range(2)]
        dhi = [sb(f"dhi{n}", [128, FH, 128], F32R, ffn) for n in range(2)]
        dlo = [sb(f"dlo{n}", [128, FH, 128], F32R, ffn) for n in range(2)]
        sg = sb("sg", [128, T], F32, ffn)
        ht = sb("ht", [128, T], F32, ffn)
        ffn.close()
        first = ExitStack()
        xin = sb("xin", [128, QT + 1, D], F32, first)
        prow = sb("prow", [128, 128], F32, first)
        w1 = sb("w1", [128, 2, HD, HD], F32, first)
        cpage = [sb(f"cpage{n}", [128, NPG, KVW], F32, first) for n in range(2)]
        hid = [sb(f"hid{n}", [128, 2, NPG, G], F32, first) for n in range(2)]
        first.close()
        norm = ExitStack()
        sq = sb("sq", [128, KC, T], F32, norm)
        csum = sb("csum", [128, T], F32, norm)
        rstd = sb("rstd", [128, T], F32, norm)
        yout = sb("yout", [128, QT + 1, D], F32, norm)
        norm.close()
        zr = sb("zr", [128, ZR, T])
        kvtok = sb("kvtok", [128, QT + 1, 6, 128])
        yconv = sb("yconv", [128, 4, T])
        conv = ExitStack()
        zc = sb("zc", [128, ZC, T], F32, conv)
        conv.close()
        page1 = sb("page1", [128, NPG, KVW])
        pr = ExitStack()
        crow = sb("crow", [NB * 2, DC], F32, pr)
        ctok = sb("ctok", [NS, 2, DC], F32, pr)
        sext = sb("sext", [128, 4, NB, NQ + 2], F32, pr)
        kcp = sb("kcp", [128, 8], F32, pr)
        vcp = sb("vcp", [8, 128], F32, pr)
        hidp = sb("hidp", [128, 2, QT, G], F32, pr)
        vbd = sb("vbd", [64, R, G, HD], F32, pr)
        ptp = sb("ptp", [64, QT, 128], F32, pr)
        pnt = sb("pnt", [NS, 4, 128], F32, pr)
        rep8 = sb("rep8", [8, NH, 8], F32, pr)
        pr.close()
        fin = ExitStack()
        neg_row = sb("neg_row", [16, NS], F32, fin)
        neg_rep = sb("neg_rep", [16, CH, NS], F32, fin)
        neg_all = sb("neg_all", [128, 16], F32, fin)
        chunk_w = sb("chunk_w", [128, 16], F32, fin)
        comb = sb("comb", [128, 2, 2, OB], F32, fin)
        ofin = sb("ofin", [128, 2, 2, 128], F32, fin)
        os_all = sb("os_all", [128, BR, 2, 4, R, NQ], F32, fin)
        os_sum = sb("os_sum", [128, R, NB, NQ], F32, fin)
        fin.close()
        kt = sb("kt", [128, NPG + CH, 128])
        win = [sb(f"win{n}", [128, CH, KVW]) for n in range(2)]
        qs = sb("qs", [128, SEQ])
        two = ExitStack()
        pp = [sb(f"pp{n}", [128, SEQ], F32, two) for n in range(2)]
        two.close()
        pw = sb("pw", [128, PC + 1, 128])
        two = ExitStack()
        ppt = [sb(f"ppt{n}", [128, SEQ], F32, two) for n in range(2)]
        two.close()
        pwt = sb("pwt", [128, PC + 1, 128])
        onew = page0[:, NPG * KVW:NPG * KVW + 512]
        gate_sel = [win[0][0:BR * NH].rearrange("p a (b m) -> p (a b) m", m=128),
                    win[1][0:BR * NH].rearrange("p a (b m) -> p (a b) m", m=128)]
        pages = (page0[:, 0:NPG * KVW].rearrange("p (a c) -> p a c", c=KVW), page1[:])

        ps = ctx.enter_context(nc.psum_tensor("ps", [128, 8, 512], F32))

        dma_x, dma_par = sem("dma_x"), sem("dma_par")
        prow_clear, const_ready = sem("prow_clear"), sem("const_ready")
        dve_step, act_step, pool_step = sem("dve_step"), sem("act_step"), sem("pool_step")
        par_in_psum, par_ready = sem("par_in_psum"), sem("par_ready")
        xt_in_psum, xt_hi, xt_done = sem("xt_in_psum"), sem("xt_hi"), sem("xt_done")
        dma_w = [sem("dma_w0"), sem("dma_w1")]
        w_hi, w_lo = [sem("w_hi0"), sem("w_hi1")], [sem("w_lo0"), sem("w_lo1")]
        w_used = [sem("w_used0"), sem("w_used1")]
        sg_ready, ht_ready, hh_ready, hl_ready = sem("sg_ready"), sem("ht_ready"), sem("hh_ready"), sem("hl_ready")
        dma_d = [sem("dma_d0"), sem("dma_d1")]
        d_hi, d_lo = [sem("d_hi0"), sem("d_hi1")], [sem("d_lo0"), sem("d_lo1")]
        d_used, y_added = [sem("d_used0"), sem("d_used1")], [sem("y_added0"), sem("y_added1")]
        csum_ready, mean_ready, centered = sem("csum_ready"), sem("mean_ready"), sem("centered")
        sq_ready, var_ready, std_ready = sem("sq_ready"), sem("var_ready"), sem("std_ready")
        scaled, normed, norm_hi, norm_lo = sem("scaled"), sem("normed"), sem("norm_hi"), sem("norm_lo")
        z_out = [sem("z_out0"), sem("z_out1")]
        tok_in_psum, tok_out = sem("tok_in_psum"), sem("tok_out")
        stored = sem("stored")
        names = ("dma_first", "dma_cpage0", "dma_cpage1", "hid_in_psum0", "hid_in_psum1", "hid_ready0",
                 "hid_ready1", "kc_in_psum0", "kc_in_psum1", "kc_ready0", "kc_ready1", "bias_in_psum", "bias_ready", "qbd_ready", "scmp_in_psum", "ncm_ready", "ecmp_ready", "pcs_ready",
                 "imp_in_psum", "pct_ready", "ocs_in_psum", "ocs_ready", "sel_ready", "selt_in_psum", "selt_ready",
                 "snew_in_psum", "nnm_ready", "pnew_ready", "pnewt_in_psum", "pnewt_ready", "onew_in_psum",
                 "onew_ready", "gates_in_psum", "gates_ready", "dma_conv", "prev_in_psum", "u_ready",
                 "conv_ready", "ctok_in_psum", "ctok_ready", "dma_w1p", "hidp_in_psum", "hidp_ready",
                 "kcp_in_psum", "kcp_ready", "rep_in_psum", "vbd_ready", "sp_in_psum", "sp_shifted", "ep_ready",
                 "pp_ready", "ptp_in_psum", "ptp_ready", "op_in_psum", "op_ready", "qs_ready", "scores", "negmax",
                 "probs", "probs_t", "pt_copied", "pv", "o_added", "dma_page0", "dma_page1", "dma_win0", "dma_win1",
                 "qn_ready", "kt_in_psum", "kt_by_act", "kt_by_dve", "s_scores", "s_negmax", "s_probs",
                 "s_probs_t", "s_pt_act", "s_pt_dve", "s_pv0", "s_pv1", "s_o", "masks_ready", "state_stored", "waited", "m_in_psum", "m_ready", "mb_in_psum",
                 "mdiff_ready", "mw_ready", "cb_scaled", "comb_in_psum", "diff_ready", "wts_ready", "ofin_ready",
                 "ofin_in_psum", "os_ready", "pt_in_psum", "at_hi", "at_lo", "out_added", "y_in_psum", "y_by_act",
                 "y_by_dve", "dma_y")
        q = {name: sem(name) for name in names}

        block = ctx.enter_context(nc.Block())


        @block.sync
        def _(sp):
            sp.dma_start(xin[:, 0:QT, :], x_prompt[0].rearrange("(t p) d -> p t d", p=128)).then_inc(dma_x, 16)
            sp.dma_start(xin[0:NS, QT, :], x_sample.rearrange("n q d -> (n q) d")).then_inc(dma_x, 16)
            sp.wait_ge(prow_clear, 1)
            rows = [(R_LN + 8 * n, a[0].rearrange("(a b) -> a b", b=128))
                    for n, a in enumerate((ln1_g, ln1_b, ln2_g, ln2_b, ln3_g, ln3_b))]
            rows.append((R_BC, b_in[0, 0:OFF_Q].rearrange("(a b) -> a b", b=128)))
            rows.append((R_BKV, b_in[0, OFF_KV:OFF_G].rearrange("(a b) -> a b", b=128)))
            rows.append((R_WC, w_conv[0].rearrange("i (a b) -> (i a) b", b=128)))
            for row, src in rows:
                sp.dma_start(prow[row:row + src.shape[0], :], src).then_inc(dma_par, 16)
            for g in range(G):
                sp.dma_start(prow[R_BQ:R_BQ + R, g * HD:g * HD + HD],
                             b_in[0, OFF_Q + g * R * HD:OFF_Q + (g + 1) * R * HD].rearrange("(r d) -> r d", d=HD)
                             ).then_inc(dma_par, 16)
            sp.dma_start(prow[R_BG:R_BG + 1, 0:BR * NH],
                         b_in[0, OFF_G:OFF_G + BR * NH].rearrange("(a b) -> a b", a=1)).then_inc(dma_par, 16)

            sp.dma_start(pages_sb[:], page_table.rearrange("(a n) g -> a (n g)", a=1)).then_inc(q["dma_first"], 16)
            for c in range(2):
                for h in range(2):
                    sp.dma_start(w1[h * BLK:(h + 1) * BLK, c, :, :], cmp_w1[0, c]).then_inc(q["dma_first"], 16)
            sp.dma_start(w2[:], cmp_w2[0].rearrange("c h d -> (c h) d")).then_inc(q["dma_first"], 16)
            sp.dma_start(pe_sb[:], cmp_pe[0]).then_inc(q["dma_first"], 16)

            def page_loads(dst, n, pool, landed):
                with sp.Fori(0, NPG // 8) as j:
                    _, numbers = nc.values_load_multi_w_load_instructions(
                        pages_sb[0:1, DS(n * NPG + j * 8, 8)], engines=[sp.engine], min_val=0, max_val=NPHYS - 1,
                        skip_runtime_bounds_check_because="the DMA itself checks its bounds")
                    for k, page in enumerate(numbers):
                        sp.dma_start(dst[:, DS(j * 8 + k, 1), :], pool[0, DS(page, 1)].rearrange("o p c g d -> p o (c g d)")
                                     ).then_inc(landed, 16)

            with sp.Fori(0, NB // 2) as i:
                for b in range(2):
                    free = sp.snap(i)
                    sp.wait_ge(q["dma_first"], 16 * 7)
                    sp.wait_ge(q[f"hid_in_psum{b}"], free)
                    page_loads(cpage[b], i * 2 + b, cache_cmp, q[f"dma_cpage{b}"])

            def ffn_loads(n, gate, up, down_w):
                phase = ("ffa", "ffb")[n]
                for half in range(2):
                    with sp.Fori(0, FH) as i:
                        for s, w in enumerate((gate, up)):
                            col = sp.snap((i + half * FH) * 128)
                            free = sp.snap(i + (USES[phase][s] + half * FH))
                            sp.wait_ge(w_lo[s], free)
                            sp.dma_start(graw[s][:], w[0].rearrange("(k p) f -> p k f", p=128)[:, :, DS(col, 128)]
                                         ).then_inc(dma_w[s], 16)
                    with sp.Fori(0, KC // 2) as i:
                        for s in range(2):
                            col = sp.snap((2 * i + s) * 128)
                            free = sp.snap(i + (2 * n + half) * (KC // 2))
                            sp.wait_ge(d_lo[s], free)
                            sp.dma_start(draw[s][:], down_w[0, half * FH * 128:(half + 1) * FH * 128, :].rearrange(
                                "(k p) f -> p k f", p=128)[:, :, DS(col, 128)]).then_inc(dma_d[s], 16)

            ffn_loads(0, ffa_gate, ffa_up, ffa_down)

            w_in_k = w_in[0].rearrange("(k p) f -> p k f", p=128)
            for t in range(NT):
                s = t % 2
                sp.wait_ge(w_lo[s], USES["proj"][s] + t // 2)
                for part in range(2):
                    if ZC <= t < ZC + R:
                        c0 = OFF_Q + (part * R + t - ZC) * HD
                        dst, src = graw[s][:, :, part * HD:(part + 1) * HD], w_in_k[:, :, c0:c0 + HD]
                    else:
                        wide = BR * NH if t == NT - 1 else 128
                        k = slice(part * KC // 2, (part + 1) * KC // 2)
                        dst, src = graw[s][:, k, 0:wide], w_in_k[:, k, t * 128:t * 128 + wide]
                    sp.dma_start(dst, src).then_inc(dma_w[s], 16)

            sp.dma_start(crow[:], state_conv[0].rearrange("n i d -> (n i) d")).then_inc(q["dma_conv"], 16)
            sp.wait_ge(w_used[0], USES["proj"][0] + NT // 2 + 1)
            for c in range(2):
                for h in range(2):
                    sp.dma_start(w1p[h * BLK:(h + 1) * BLK, c, :, :], cmp_w1[0, c]).then_inc(q["dma_w1p"], 16)
            n_stored = 0
            for n in range(NB):
                sp.dma_start(s_win[0, n, 0:WIN - NQ].rearrange("p c g d -> p (c g d)"),
                             state_win[0, n, NQ:WIN].rearrange("p c g d -> p (c g d)")).then_inc(stored, 16)
                n_stored += 1
            sp.wait_ge(tok_out, QT + 1)
            for j, (prompt, sample) in enumerate(((p_cmp, s_cmp), (p_sel, s_sel), (p_win, s_win))):
                for t in range(QT):
                    sp.dma_start(prompt[0, 0, t * 128:(t + 1) * 128].rearrange("p c g d -> p (c g d)"),
                                 kvtok[:, t, 2 * j:2 * j + 2, :]).then_inc(stored, 16)
                    n_stored += 1
                if j < 2:
                    sp.dma_start(sample[0].rearrange("n q c g d -> (n q) (c g d)"),
                                 kvtok[0:NS, QT, 2 * j:2 * j + 2, :]).then_inc(stored, 16)
                    n_stored += 1
                else:
                    for n in range(NB):
                        sp.dma_start(sample[0, n, WIN - NQ:WIN].rearrange("q c g d -> q (c g d)"),
                                     kvtok[n * NQ:(n + 1) * NQ, QT, 2 * j:2 * j + 2, :]).then_inc(stored, 16)
                        n_stored += 1

            def sample_loads(b, i):
                page_loads(pages[b], i * 2 + b, cache_sel, q[f"dma_page{b}"])
                sp.dma_start(win[b][:], state_win[0, DS(i * 2 + b, 1)].rearrange("o (c p) k g d -> p (o c) (k g d)", p=128)
                             ).then_inc(q[f"dma_win{b}"], 16)

            sp.wait_ge(q["hidp_in_psum"], 1)
            sample_loads(0, 0)
            sp.wait_ge(q["ctok_ready"], 1)
            sp.dma_start(p_conv[0, 0], ctok[NS - 2:NS, 0, :]).then_inc(q["state_stored"], 16)
            for n in range(NB):
                sp.dma_start(s_conv[0, n], ctok[n * NQ + 2:n * NQ + 4, 1, :]).then_inc(q["state_stored"], 16)
            sp.wait_ge(q["conv_ready"], 1)
            sample_loads(1, 0)
            sp.wait_ge(stored, 16 * n_stored)
            with sp.Fori(1, NB // 2) as i:
                for b in range(2):
                    free = sp.snap(i)
                    sp.wait_ge(q["dma_first"], 16 * 7)
                    sp.wait_ge(q[f"s_pv{b}"], free)
                    sample_loads(b, i)

            w_o = w_out[0]
            sp.wait_ge(q["at_hi"], R)
            sp.wait_ge(q["pt_in_psum"], R)
            for t in range(KC):
                s = t % 2
                sp.wait_ge(w_lo[s], USES["out"][s] + t // 2)
                cols = slice(t * 128, (t + 1) * 128)
                for g in range(G):
                    sp.dma_start(graw[s][g * HD:(g + 1) * HD, 0:R, :],
                                 w_o[g * R * HD:(g + 1) * R * HD, cols].rearrange("(r d) n -> d r n", d=HD)
                                 ).then_inc(dma_w[s], 16)
                sp.dma_start(graw[s][:, R:KC, :], w_o[DC:D, cols].rearrange("(k p) n -> p k n", p=128)
                             ).then_inc(dma_w[s], 16)

            ffn_loads(1, ffb_gate, ffb_up, ffb_down)

            for t in range(QT + 1):
                sp.wait_ge(q["y_by_act"], t + 1)
                sp.wait_ge(q["y_by_dve"], t + 1)
                if t < QT:
                    sp.dma_start(y_prompt[0, t * 128:(t + 1) * 128, :], yout[:, t, :]).then_inc(stored, 16)
                else:
                    sp.dma_start(y_sample.rearrange("n q d -> (n q) d"), yout[0:NS, t, :]).then_inc(stored, 16)
                n_stored += 1
            sp.wait_ge(q["state_stored"], 16 * (NB + 1))
            sp.wait_ge(stored, 16 * n_stored)

        @block.gpsimd
        def _(pool):
            steps = Steps(pool, pool_step)
            pool.memset(prow[:], 0.0).then_inc(prow_clear, 1)
            steps(pool.memset(ident[:], 0.0))
            steps(pool.memset(causal[:], 0.0))
            pool.memset(mean_w[:], 1.0 / D).then_inc(const_ready, 1)
            pool.memset(eps[:], EPS).then_inc(const_ready, 1)
            for tile in (qbd, win_mask):
                pool.memset(tile[:], 0.0)
            pool.memset(new_mask[:], NEG)
            steps(pool.memset(blk_neg[:], 0.0))
            steps(pool.memset(blk_ok[:], 1.0))
            steps(pool.memset(diag[:], 1.0))
            steps.settle()
            pool.affine_select(out=ident[:], in_=ident[:], compare_op=ALU.not_equal, fill=1.0, base=0,
                               pattern=[[-1, 128]], channel_multiplier=1).then_inc(const_ready, 1)
            pool.affine_select(out=causal[:], in_=causal[:], compare_op=ALU.is_ge, fill=NEG, base=0,
                               pattern=[[-1, 128]], channel_multiplier=1).then_inc(const_ready, 1)
            pool.wait_ge(const_ready, 4)
            pool.tensor_copy(identb[:], ident[:]).then_inc(const_ready, 1)
            for tile, fill in ((blk_neg, NEG), (blk_ok, 0.0)):
                pool.affine_select(out=tile[:], in_=tile[:], compare_op=ALU.is_ge, fill=fill, base=1 - BLK,
                                   pattern=[[128, QT], [-BLK, 2], [-PAGE, QT]], channel_multiplier=1)
            steps(pool.affine_select(out=diag[:], in_=diag[:], compare_op=ALU.is_ge, fill=0.0, base=0,
                                     pattern=[[-8, R], [-8 * R, G]], channel_multiplier=1))
            steps.settle()
            pool.affine_select(out=diag[:], in_=diag[:], compare_op=ALU.is_ge, fill=0.0, base=7,
                               pattern=[[8, R], [8 * R, G]], channel_multiplier=-1).then_inc(const_ready, 1)

        @block.tensor
        def _(pe):
            def product(out, hi, lo, xhi, xlo, chunks):
                last = None
                for k in range(chunks):
                    for a, b in ((hi, xhi), (hi, xlo), (lo, xhi)):
                        for h in range(2):
                            last = nc.tensor.matmul(
                                out[:, h, 0:HALF], a[:, k, :], b[:, k, h * HALF:(h + 1) * HALF],
                                start=(k == 0 and a is hi and b is xhi),
                                stop=(k == chunks - 1 and a is lo))
                return last

            pe.wait_ge(const_ready, 5)
            pe.wait_ge(dma_par, 16 * 12)
            nc.tensor.transpose(ps[:, 7, 0:128], prow[:], ident[:]).then_inc(par_in_psum, 1)
            pe.wait_ge(dma_x, 32)
            for k in range(KC):
                if k >= 2:
                    pe.wait_ge(xt_done, k - 1)
                b = 2 * (k % 2)
                for t in range(QT):
                    nc.tensor.transpose(ps[:, b, t * 128:(t + 1) * 128], xin[:, t, k * 128:(k + 1) * 128], ident[:])
                nc.tensor.transpose(ps[:, b + 1, 0:NS], xin[0:NS, QT, k * 128:(k + 1) * 128],
                                    ident[0:NS, 0:NS]).then_inc(xt_in_psum, 1)

            def hidden(src, w, out_bank, wide):
                for d in range(HD):
                    for c in range(2):
                        for h in range(2):
                            last = nc.tensor.matmul(ps[c * HD:(c + 1) * HD, out_bank + h, 0:wide],
                                                    w[h * BLK:(h + 1) * BLK, c, d, :], src(h, c, d),
                                                    start=(d == 0), stop=(d == HD - 1))
                return last

            def hidden_cached(b, i):
                pe.wait_ge(q[f"dma_cpage{b}"], (i + 1) * (NPG * 16))
                pe.wait_ge(q[f"hid_ready{b}"], i)
                pe.sem_inc(q["waited"], 1)
                hidden(lambda h, c, d: cpage[b][h * BLK:(h + 1) * BLK, :, :].rearrange(
                    "p a (c g d) -> p a c g d", c=2, g=G)[:, :, c, :, d], w1, 2 * b, NPG * G
                       ).then_inc(q[f"hid_in_psum{b}"], 1)

            def compressed(b, i):
                pe.wait_ge(q[f"hid_ready{b}"], i + 1)
                pe.wait_ge(q[f"kc_ready{b}"], i)
                pe.sem_inc(q["waited"], 1)
                for g in range(G):
                    nc.tensor.matmul(ps[g * HD:(g + 1) * HD, 4 + b, 0:NBLK], w2[0:HD, :], hid[b][0:HD, :, :, g],
                                     start=True, stop=True)
                for g in range(G):
                    last = nc.tensor.matmul(ps[0:NBLK, 6 + b, g * HD:(g + 1) * HD],
                                            hid[b][HD:128, :, :, g].rearrange("p h a -> p (h a)"), w2[HD:128, :],
                                            start=True, stop=True)
                last.then_inc(q[f"kc_in_psum{b}"], 1)

            def ffn_products(n):
                uses = USES[("ffa", "ffb")[n]]
                for half in range(2):
                    before = n * FT + half * FH
                    with pe.Fori(0, FH) as i:
                        for s, (done, bank) in enumerate(((sg_ready, 0), (ht_ready, 2))):
                            pe.wait_ge(w_lo[s], i + (uses[s] + half * FH + 1))
                            pe.wait_ge(done, i + before)
                            product(ps[:, bank:bank + 2, :], ghi[s], glo[s], xh, xl, KC).then_inc(w_used[s], 1)
                    pe.wait_ge(hl_ready, before + FH)
                    with pe.Fori(0, KC // 2) as i:
                        for s in range(2):
                            use = (2 * n + half) * (KC // 2)
                            pe.wait_ge(d_lo[s], i + (use + 1))
                            pe.wait_ge(y_added[s], i + use)
                            product(ps[:, 4 + 2 * s:6 + 2 * s, :], dhi[s], dlo[s], hh, hl, FH
                                    ).then_inc(d_used[s], 1)

            def norm_products(n):
                for j, ready in enumerate((csum_ready, csum_ready)):
                    for h in range(2):
                        pe.wait_ge(csum_ready, 4 * n + 2 * j + h + 1)
                        nc.tensor.matmul(ps[:, 2 * j + h, 0:HALF], mean_w[:], csum[:, h * HALF:(h + 1) * HALF],
                                         start=True, stop=True).then_inc((mean_ready, var_ready)[j], 1)

            pe.wait_ge(q["dma_first"], 16 * 7)
            pe.wait_ge(par_ready, 1)
            for d in range(HD):
                for c in range(2):
                    last = nc.tensor.matmul(ps[c * HD:(c + 1) * HD, 7, 0:1], w1[0:BLK, c, d, :], pe_sb[:, c, d:d + 1],
                                            start=(d == 0), stop=(d == HD - 1))
            last.then_inc(q["bias_in_psum"], 1)
            pe.wait_ge(xt_done, KC)
            hidden_cached(0, 0)
            pe.wait_ge(q["bias_ready"], 1)
            with pe.Fori(0, NB // 2 - 1) as i:
                hidden_cached(1, i)
                compressed(0, i)
                hidden_cached(0, i + 1)
                compressed(1, i)
            hidden_cached(1, NB // 2 - 1)
            compressed(0, NB // 2 - 1)
            compressed(1, NB // 2 - 1)
            for b in range(2):
                pe.wait_ge(q[f"kc_ready{b}"], NB // 2)
            ffn_products(0)
            norm_products(0)

            pe.wait_ge(norm_lo, KC)
            with pe.Fori(0, NT // 2) as i:
                for s in range(2):
                    pe.wait_ge(w_lo[s], i + (USES["proj"][s] + 1))
                    pe.wait_ge(z_out[s], i)
                    product(ps[:, 2 * s:2 * s + 2, :], ghi[s], glo[s], xh, xl, KC).then_inc(w_used[s], 1)
            pe.wait_ge(w_lo[0], USES["proj"][0] + NT // 2 + 1)
            pe.wait_ge(z_out[0], NT // 2)
            product(ps[:, 0:2, :], ghi[0], glo[0], xh, xl, KC).then_inc(w_used[0], 1)

            pe.wait_ge(z_out[0], NT // 2 + 1)
            pe.wait_ge(z_out[1], NT // 2)
            for t in range(QT + 1):
                if t >= 2:
                    pe.wait_ge(tok_out, t - 1)
                w = 128 if t < QT else NS
                for j in range(6):
                    last = nc.tensor.transpose(ps[0:w, 4 + 2 * (t % 2) + j // 4, (j % 4) * 128:(j % 4 + 1) * 128],
                                               zr[:, KV0 + j, t * 128:t * 128 + w], ident[:])
                last.then_inc(tok_in_psum, 1)

            pe.wait_ge(q["qbd_ready"], 1)
            pe.wait_ge(q["masks_ready"], 1)
            for n in range(NB):
                last = nc.tensor.matmul(ps[32 * (n % 4):32 * (n % 4) + 32, 0, n // 4 * NBLK:(n // 4 + 1) * NBLK],
                                        qbd[:, n, :], kc_all[:, n, :], start=True, stop=True)
            last.then_inc(q["scmp_in_psum"], 1)
            for br in range(2):
                for nh in range(2):
                    out = ps[:, 1, (2 * br + nh) * NS:(2 * br + nh + 1) * NS]
                    nc.tensor.matmul(out, qbd[:, 4 * nh:4 * nh + 4, :].rearrange("p n r -> p (n r)"),
                                     zr[:, KV0 + 2 + 2 * br, SEQ:T], start=True, stop=False)
                    last = nc.tensor.matmul(out, identb[:], new_mask[:, nh, :], start=False, stop=True)
            last.then_inc(q["snew_in_psum"], 1)
            for k in range(BR * R):
                br, r = k // R, k % R
                nc.tensor.matmul(ps[:, 2, k * NS:(k + 1) * NS], gate_sel[k // 8][:, k % 8, :],
                                 zr[0:BR * NH, G0, SEQ:T], start=True, stop=True)
            for t in range(QT):
                nc.tensor.transpose(ps[:, 3, t * 32:t * 32 + BR * NH], zr[0:BR * NH, G0, t * 128:(t + 1) * 128],
                                    ident[0:BR * NH, 0:BR * NH])
            pe.wait_ge(q["dma_conv"], 16)
            for t in range(4):
                last = nc.tensor.transpose(ps[:, 3, 128 + t * 16:144 + t * 16], crow[:, t * 128:(t + 1) * 128],
                                           ident[0:16, 0:16])
            last.then_inc(q["gates_in_psum"], 1)

            pe.wait_ge(q["dma_w1p"], 16 * 4)
            pe.wait_ge(tok_out, QT + 1)
            hidden(lambda h, c, d: kvtok[h * BLK:(h + 1) * BLK, 0:QT, c, :].rearrange(
                "p a (g d) -> p a g d", g=G)[:, :, :, d], w1p, 6, QT * G).then_inc(q["hidp_in_psum"], 1)

            pe.wait_ge(q["pcs_ready"], 1)
            nc.tensor.matmul(ps[:, 4, 0:128], same[:], pcs[:].rearrange("p n b -> p (n b)"), start=True, stop=True)
            for nh in range(2):
                last = nc.tensor.transpose(ps[0:NBLK, 5, nh * 128:(nh + 1) * 128], pcs[:, nh, :], ident[:])
            last.then_inc(q["imp_in_psum"], 1)

            pe.wait_ge(q["hidp_ready"], 1)
            for g in range(G):
                nc.tensor.matmul(ps[g * HD:(g + 1) * HD, 6, 0:8], w2[0:HD, :], hidp[0:HD, :, :, g],
                                 start=True, stop=True)
            for g in range(G):
                last = nc.tensor.matmul(ps[0:8, 7, g * HD:(g + 1) * HD],
                                        hidp[HD:128, :, :, g].rearrange("p h a -> p (h a)"), w2[HD:128, :],
                                        start=True, stop=True)
            last.then_inc(q["kcp_in_psum"], 1)

            pe.wait_ge(q["pct_ready"], 1)
            for n in range(NB):
                last = nc.tensor.matmul(ps[32 * (n % 4):32 * (n % 4) + 32, 0, n // 4 * 128:(n // 4 + 1) * 128],
                                        pct[:, n // 4, 32 * (n % 4):32 * (n % 4) + 32], vc_all[:, n, :],
                                        start=True, stop=True)
            last.then_inc(q["ocs_in_psum"], 1)

            pe.wait_ge(q["pnew_ready"], 1)
            for k in range(4):
                last = nc.tensor.transpose(ps[0:NS, 1, k * 128:(k + 1) * 128], pnew[:, k, :], ident[:])
            last.then_inc(q["pnewt_in_psum"], 1)

            pe.wait_ge(q["sel_ready"], 1)
            for n in range(NB):
                for c in range(CH):
                    last = nc.tensor.matmul(ps[32 * c:32 * c + 32, 5, n * 16:(n + 1) * 16],
                                            identb[:, 32 * (n % 4):32 * (n % 4) + 32],
                                            selneg[:, n // 4, c * 16:(c + 1) * 16], start=True, stop=True)
            last.then_inc(q["selt_in_psum"], 1)

            pe.wait_ge(q["kcp_ready"], 1)
            nc.tensor.matmul(ps[0:64, 7, 0:128], rep8[:].rearrange("p x b -> p (x b)"), vcp[:],
                             start=True, stop=True).then_inc(q["rep_in_psum"], 1)
            pe.wait_ge(q["gates_ready"], 1)
            for g in range(G):
                for t in range(QT):
                    for r in range(R):
                        last = nc.tensor.matmul(ps[:, 2 + g, (t * R + r) * 8:(t * R + r + 1) * 8],
                                                zr[g * HD:(g + 1) * HD, r, t * 128:(t + 1) * 128],
                                                kcp[g * HD:(g + 1) * HD, :], start=True, stop=True)
            last.then_inc(q["sp_in_psum"], 1)

            pe.wait_ge(q["pnewt_ready"], 1)
            for k in range(4):
                last = nc.tensor.matmul(ps[:, 4, k * 128:(k + 1) * 128], pnt[:, k, :],
                                        kvtok[0:NS, QT, 3 + 2 * (k // 2), :], start=True, stop=True)
            last.then_inc(q["onew_in_psum"], 1)

            pe.wait_ge(q["pp_ready"], 1)
            for t in range(QT):
                last = nc.tensor.transpose(ps[0:64, 6, t * 128:(t + 1) * 128], pp[0][:, t * 64:(t + 1) * 64], ident[:])
            last.then_inc(q["ptp_in_psum"], 1)
            pe.wait_ge(q["ptp_ready"], 1)
            pe.wait_ge(q["vbd_ready"], 1)
            pe.wait_ge(q["ocs_ready"], 1)
            for t in range(QT):
                last = nc.tensor.matmul(ps[:, t, :], ptp[:, t, :], vbd[:].rearrange("p r g d -> p (r g d)"),
                                        start=True, stop=True)
            last.then_inc(q["op_in_psum"], 1)
            pe.wait_ge(q["u_ready"], 1)
            pe.wait_ge(q["selt_ready"], 1)
            for k, c0 in enumerate((SEQ - NS, SEQ)):
                for t in range(4):
                    last = nc.tensor.transpose(ps[0:NS, 5 + 2 * k, t * 128:(t + 1) * 128],
                                               zc[:, 4 + t, c0:c0 + NS], ident[:])
            last.then_inc(q["ctok_in_psum"], 1)

            units = [(br, t, g) for br in range(2) for t in range(QT) for g in range(G)]
            U = len(units)
            for name in ("op_ready", "ctok_ready", "onew_ready", "conv_ready"):
                pe.wait_ge(q[name], 1)
            def prompt_head(r):
                pe.wait_ge(q["qs_ready"], r + 1)
                for j in range(U + 3):
                    if j < U:
                        br, t, g = units[j]
                        gp = slice(g * HD, (g + 1) * HD)
                        if j >= 3:
                            pe.wait_ge(q["probs"], r * U + (j - 2))
                        nc.tensor.matmul(ps[:, j % 3, 0:(t + 1) * 128], qs[gp, t * 128:(t + 1) * 128],
                                         zr[gp, KV0 + 2 + 2 * br, 0:(t + 1) * 128], start=True, stop=True)
                        nc.tensor.matmul(ps[:, j % 3, t * 128:(t + 1) * 128], identb[:], causal[:],
                                         start=False, stop=True, skip_group_check=True).then_inc(q["scores"], 1)
                    if 2 <= j < U + 2:
                        k = j - 2
                        br, t, g = units[k]
                        pe.wait_ge(q["probs"], r * U + (k + 1))
                        if k >= 2:
                            pe.wait_ge(q["pt_copied"], r * U + (k - 1))
                        for m in range(t + 1):
                            last = nc.tensor.transpose(ps[:, 3 + k % 2, m * 128:(m + 1) * 128],
                                                       pp[k % 2][:, m * 128:(m + 1) * 128], ident[:])
                        last.then_inc(q["probs_t"], 1)
                    if j >= 3:
                        k = j - 3
                        br, t, g = units[k]
                        pe.wait_ge(q["pt_copied"], r * U + (k + 1))
                        if k >= 2:
                            pe.wait_ge(q["o_added"], r * U + (k - 1))
                        for m in range(t + 1):
                            last = nc.tensor.matmul(ps[:, 5 + k % 2, 0:HD], ppt[k % 2][:, m * 128:(m + 1) * 128],
                                                    kvtok[:, m, 3 + 2 * br, g * HD:(g + 1) * HD],
                                                    start=(m == 0), stop=(m == t))
                        last.then_inc(q["pv"], 1)

            def keys_t(b, i, n):
                pe.wait_ge(q[f"dma_page{b}"], (i + 1) * (NPG * 16))
                pe.wait_ge(q[f"dma_win{b}"], (i + 1) * 16)
                for m in range(9):
                    if m % 2 == 0:
                        pe.wait_ge(q["kt_by_act"], n * 5 + m // 2)
                    else:
                        pe.wait_ge(q["kt_by_dve"], n * 4 + m // 2)
                    for k in range(4):
                        src = pages[b][:, 4 * m + k, 0:128] if m < 8 else win[b][:, k, 0:128]
                        last = nc.tensor.transpose(ps[:, m % 2, k * 128:(k + 1) * 128], src, ident[:])
                    last.then_inc(q["kt_in_psum"], 1)

            def scores_s(b, n):
                pe.wait_ge(q["kt_by_act"], n * 5 + 5)
                pe.wait_ge(q["kt_by_dve"], n * 4 + 4)
                pe.wait_ge(q["qn_ready"], n + 1)
                pe.wait_ge(q["s_probs"], n)
                for h in range(2):
                    nc.tensor.matmul(ps[:, 2 + h, :], identb[:],
                                     selt[:, DS(n, 1), h * 8:(h + 1) * 8].rearrange("p o (k u) -> p (o k) u", u=1)
                                     .broadcast_to([128, 8, BLK]), start=True, stop=True, skip_group_check=True)
                nc.tensor.matmul(ps[:, 4, 0:128], identb[:], win_mask[:], start=True, stop=True,
                                 skip_group_check=True)
                for h in range(2):
                    for c in range(CH):
                        nc.tensor.matmul(ps[32 * c:32 * c + 32, 2 + h, :], qn[b][:],
                                         kt[:, c * 8 + h * 4:c * 8 + h * 4 + 4, :].rearrange("p k t -> p (k t)"),
                                         start=False, stop=True, skip_group_check=True)
                for c in range(CH):
                    last = nc.tensor.matmul(ps[32 * c:32 * c + 32, 4, 0:128], qn[b][:], kt[:, NPG + c, :],
                                            start=False, stop=True, skip_group_check=True)
                last.then_inc(q["s_scores"], 1)

            def values_s(b, n):
                pe.wait_ge(q["s_probs"], n + 1)
                pe.wait_ge(q["s_o"], n)
                pe.wait_ge(q["s_pt_act"], n)
                pe.wait_ge(q["s_pt_dve"], n)
                for k in range(PC + 1):
                    last = nc.tensor.transpose(ps[:, 5 + k // 4, k % 4 * 128 if k < 8 else 256:(k % 4 * 128 if k < 8 else 256) + 128],
                                               pw[:, k, :], ident[:])
                last.then_inc(q["s_probs_t"], 1)
                pe.wait_ge(q["s_pt_act"], n + 1)
                pe.wait_ge(q["s_pt_dve"], n + 1)
                for k in range(PC):
                    for c in range(CH):
                        nc.tensor.matmul(ps[32 * c:32 * c + 32, 7, 0:128], pwt[:, k, 32 * c:32 * c + 32],
                                         pages[b][:, c * PC + k, 128:256], start=(k == 0), stop=(k == PC - 1))
                for c in range(CH):
                    last = nc.tensor.matmul(ps[32 * c:32 * c + 32, 7, 128:256], pwt[:, PC, 32 * c:32 * c + 32],
                                            win[b][:, c, 128:256], start=True, stop=True)
                last.then_inc(q[f"s_pv{b}"], 1)

            with pe.Fori(0, R) as r:
                prompt_head(r)
                keys_t(0, r, r * 2)
                scores_s(0, r * 2)
                pe.wait_ge(q["o_added"], (r + 1) * U)
                keys_t(1, r, r * 2 + 1)
                values_s(0, r * 2)
                scores_s(1, r * 2 + 1)
                values_s(1, r * 2 + 1)

            pe.wait_ge(q["s_o"], NB)
            nc.tensor.transpose(ps[0:16, 0, 0:128], cb[:, :, :, OB - 1].rearrange("p n b -> p (n b)"), ident[:]
                                ).then_inc(q["m_in_psum"], 1)
            pe.wait_ge(q["m_ready"], 1)
            nc.tensor.transpose(ps[:, 1, 0:16], neg_rep[:].rearrange("p c r -> p (c r)"), ident[0:16, 0:16]
                                ).then_inc(q["mb_in_psum"], 1)
            pe.wait_ge(q["cb_scaled"], 1)
            for n in range(NB):
                last = nc.tensor.matmul(ps[32 * (n % 4):32 * (n % 4) + 32, 2 + n // 4, 0:2 * OB], fold[:],
                                        cb[:, n, :, :].rearrange("p b o -> p (b o)"), start=True, stop=True)
            last.then_inc(q["comb_in_psum"], 1)
            pe.wait_ge(q["ofin_ready"], 1)
            for nh in range(2):
                nc.tensor.transpose(ps[:, 4, nh * 128:(nh + 1) * 128], ocs[:, nh, :], ident[:])
                for br in range(2):
                    last = nc.tensor.transpose(ps[:, 5 + br, nh * 128:(nh + 1) * 128], ofin[:, nh, br, :], ident[:])
            last.then_inc(q["ofin_in_psum"], 1)
            pe.wait_ge(q["mb_in_psum"], 1)
            for r in range(R):
                if r >= 2:
                    pe.wait_ge(q["at_lo"], r - 1)
                for t in range(QT):
                    last = nc.tensor.transpose(ps[:, r % 2, t * 128:(t + 1) * 128], po[:, t, r, :], ident[:])
                last.then_inc(q["pt_in_psum"], 1)

            pe.wait_ge(q["at_lo"], R + 1)
            for t in range(KC):
                s = t % 2
                pe.wait_ge(w_lo[s], USES["out"][s] + t // 2 + 1)
                if t >= 2:
                    pe.wait_ge(q["out_added"], t - 1)
                product(ps[:, 2 * s:2 * s + 2, :], ghi[s], glo[s], xh, xl, KC).then_inc(w_used[s], 1)
            norm_products(1)
            pe.wait_ge(norm_lo, 2 * KC)
            ffn_products(1)
            norm_products(2)
            pe.wait_ge(normed, 3 * KC)
            for t in range(QT + 1):
                if t >= 2:
                    pe.wait_ge(q["y_by_act"], t - 1)
                    pe.wait_ge(q["y_by_dve"], t - 1)
                w = 128 if t < QT else NS
                for k in range(KC):
                    last = nc.tensor.transpose(ps[0:w, 4 + 2 * (t % 2) + k // 4, k % 4 * 128:(k % 4 + 1) * 128],
                                               x[:, k, t * 128:t * 128 + w], ident[:])
                last.then_inc(q["y_in_psum"], 1)

        @block.scalar
        def _(act):
            def split_w(s, use, fills):
                act.wait_ge(dma_w[s], fills)
                act.wait_ge(w_used[s], use)
                act.activation(ghi[s][:], graw[s][:], ACT.Copy).then_inc(w_hi[s], 1)

            def split_d(s, use):
                act.wait_ge(dma_d[s], use * 16 + 16)
                act.wait_ge(d_used[s], use)
                act.activation(dhi[s][:], draw[s][:], ACT.Copy).then_inc(d_hi[s], 1)

            for k in range(KC):
                act.wait_ge(xt_in_psum, k + 1)
                b = 2 * (k % 2)
                act.activation(xh[:, k, 0:SEQ], ps[:, b, :], ACT.Copy)
                act.activation(xh[:, k, SEQ:T], ps[:, b + 1, 0:NS], ACT.Copy).then_inc(xt_hi, 1)

            def ffn_gates(n):
                phase = ("ffa", "ffb")[n]
                uses, fills = USES[phase], FILLS[phase]
                for half in range(2):
                    before = n * FT + half * FH

                    def copy_h(j):
                        act.wait_ge(ht_ready, j + (before + 1))
                        act.activation(hh[:, DS(j, 1), :], ht[:], ACT.Copy).then_inc(hh_ready, 1)

                    def tile(i, first):
                        split_w(0, i + (uses[0] + half * FH), (i + (fills[0] + half * FH + 1)) * 16)
                        if not first:
                            copy_h(i - 1)
                        split_w(1, i + (uses[1] + half * FH), (i + (fills[1] + half * FH + 1)) * 16)
                        act.wait_ge(w_used[0], i + (uses[0] + half * FH + 1))
                        act.wait_ge(ht_ready, i + before)
                        act.activation(sg[:].rearrange("p (h t) -> p h t", h=2), ps[:, 0:2, 0:HALF], ACT.Silu
                                       ).then_inc(sg_ready, 1)

                    tile(0, True)
                    with act.Fori(1, FH) as i:
                        tile(i, False)
                    use = (2 * n + half) * (KC // 2)
                    split_d(0, use)
                    copy_h(FH - 1)
                    with act.Fori(0, KC // 2 - 1) as i:
                        split_d(1, i + use)
                        split_d(0, i + (use + 1))
                    split_d(1, use + KC // 2 - 1)

            def norm_scale(n, split):
                for h in range(2):
                    act.wait_ge(centered, 2 * n + h + 1)
                    hs = slice(h * HALF, (h + 1) * HALF)
                    act.activation(sq[:, :, hs], x[:, :, hs], ACT.Square).then_inc(sq_ready, 1)
                for h in range(2):
                    hs = slice(h * HALF, (h + 1) * HALF)
                    act.wait_ge(var_ready, 2 * n + h + 1)
                    act.activation(rstd[:, hs], ps[:, 2 + h, 0:HALF], ACT.Sqrt, bias=eps[:]).then_inc(std_ready, 1)
                for k in range(KC):
                    act.wait_ge(scaled, KC * n + k + 1)
                    act.activation(x[:, k, :], x[:, k, :], ACT.Identity,
                                   scale=par[:, R_LN + 16 * n + k:R_LN + 16 * n + k + 1],
                                   bias=par[:, R_LN + 16 * n + 8 + k:R_LN + 16 * n + 9 + k]).then_inc(normed, 1)
                if split:
                    for k in range(KC):
                        act.wait_ge(normed, KC * n + k + 1)
                        act.activation(xh[:, k, :], x[:, k, :], ACT.Copy).then_inc(norm_hi, 1)

            steps = Steps(act, act_step)
            act.wait_ge(par_ready, 1)
            act.wait_ge(q["bias_ready"], 1)
            with act.Fori(0, NB // 2) as i:
                for b in range(2):
                    act.wait_ge(q[f"hid_in_psum{b}"], i + 1)
                    act.wait_ge(q[f"kc_in_psum{b}"], i)
                    act.activation(hid[b][:].rearrange("p h a g -> p h (a g)"), ps[:, 2 * b:2 * b + 2, 0:NPG * G],
                                   ACT.Silu, bias=hid_bias[:]).then_inc(q[f"hid_ready{b}"], 1)
            ffn_gates(0)
            norm_scale(0, True)

            def z_tile(t, s, i):
                split_w(s, i + USES["proj"][s], (i * 2 + (FILLS["proj"][s] + 2)) * 16)

            def z_split(s, i):
                split_w(s, i + USES["proj"][s], (i * 2 + (FILLS["proj"][s] + 2)) * 16)

            def z_result(dst, col, s, i, func=ACT.Identity):
                act.wait_ge(w_used[s], i + (USES["proj"][s] + 1))
                act.activation(dst.rearrange("p o (h t) -> p (o h) t", h=2), ps[:, 2 * s:2 * s + 2, 0:HALF], func,
                               bias=par[:, DS(col, 1)]).then_inc(z_out[s], 1)

            z_split(0, 0)
            with act.Fori(0, ZC // 2) as i:
                z_split(1, i)
                z_result(zc[:, DS(i * 2, 1), :], i * 2 + R_BC, 0, i)
                z_split(0, i + 1)
                z_result(zc[:, DS(i * 2 + 1, 1), :], i * 2 + (R_BC + 1), 1, i)
            with act.Fori(ZC // 2, NT // 2) as i:
                z_split(1, i)
                z_result(zr[:, DS(i * 2 - ZC, 1), :], i * 2 + R_BC, 0, i)
                z_split(0, i + 1)
                z_result(zr[:, DS(i * 2 - (ZC - 1), 1), :], i * 2 + (R_BC + 1), 1, i)
            z_result(zr[:, G0:G0 + 1, :], R_BG, 0, NT // 2, ACT.Sigmoid)

            act.wait_ge(q["ncm_ready"], 1)
            for nh in range(2):
                last = act.activation(pcs[:, nh, :], ps[:, 0, nh * NBLK:(nh + 1) * NBLK], ACT.Exp,
                                      bias=small[:, C_NCM + nh:C_NCM + nh + 1],
                                      accum_out=small[:, C_CSUM + nh:C_CSUM + nh + 1])
            last.then_inc(q["ecmp_ready"], 1)
            act.wait_ge(q["nnm_ready"], 1)
            for k in range(4):
                last = act.activation(pnew[:, k, :], ps[:, 1, k * NS:(k + 1) * NS], ACT.Exp,
                                      bias=small[:, C_NNM + k:C_NNM + k + 1],
                                      accum_out=small[:, C_NSUM + k:C_NSUM + k + 1])
            last.then_inc(q["pnew_ready"], 1)
            act.wait_ge(q["hidp_in_psum"], 1)
            act.activation(hidp[:].rearrange("p h a g -> p h (a g)"), ps[:, 6:8, 0:QT * G], ACT.Silu,
                           bias=hid_bias[:]).then_inc(q["hidp_ready"], 1)
            act.wait_ge(q["sp_shifted"], 1)
            act.activation(pp[0][:, 0:256], pp[0][:, 0:256], ACT.Exp).then_inc(q["ep_ready"], 1)
            act.wait_ge(q["op_in_psum"], 1)
            act.activation(po[:].rearrange("p t r d -> p t (r d)"), ps[:, 0:4, :], ACT.Copy).then_inc(q["op_ready"], 1)

            units = [(br, t, g) for br in range(2) for t in range(QT) for g in range(G)]
            U = len(units)
            def prompt_head(r):
                act.wait_ge(q["o_added"], r * U)
                act.wait_ge(q["s_pv0"], r)
                act.wait_ge(q["s_pv1"], r)
                for j in range(U + 2):
                    if j < U:
                        br, t, g = units[j]
                        act.wait_ge(q["negmax"], r * U + (j + 1))
                        act.wait_ge(q["probs_t"], r * U + max(j - 1, 0))
                        act.activation(pp[j % 2][:, 0:(t + 1) * 128], ps[:, j % 3, 0:(t + 1) * 128], ACT.Exp,
                                       bias=small[:, C_PNM + j:C_PNM + j + 1],
                                       accum_out=small[:, C_PSUM + j:C_PSUM + j + 1]).then_inc(q["probs"], 1)
                    if j >= 2:
                        k = j - 2
                        br, t, g = units[k]
                        act.wait_ge(q["probs_t"], r * U + (k + 1))
                        act.wait_ge(q["pv"], r * U + max(k - 1, 0))
                        act.activation(ppt[k % 2][:, 0:(t + 1) * 128], ps[:, 3 + k % 2, 0:(t + 1) * 128], ACT.Copy
                                       ).then_inc(q["pt_copied"], 1)

            def keys_s(n):
                for m in range(0, 9, 2):
                    act.wait_ge(q["kt_in_psum"], n * 9 + (m + 1))
                    if m == 0:
                        act.wait_ge(q["s_scores"], n)
                    act.activation(kt[:, 4 * m:4 * m + 4, :].rearrange("p k t -> p (k t)"), ps[:, 0, :], ACT.Copy
                                   ).then_inc(q["kt_by_act"], 1)

            def probs_s(b, n):
                act.wait_ge(q["s_negmax"], n + 1)
                act.wait_ge(q["s_probs_t"], n)
                act.activation(pw[:, 0:PC, :].rearrange("p k t -> p (k t)"), ps[:, 2:4, :].rearrange("p b t -> p (b t)"),
                               ACT.Exp, bias=cb[:, DS(n, 1), 0, OB - 1], accum_out=cb[:, DS(n, 1), 0, OB - 2])
                act.activation(pw[:, PC, :], ps[:, 4, 0:128], ACT.Exp, bias=cb[:, DS(n, 1), 1, OB - 1],
                               accum_out=cb[:, DS(n, 1), 1, OB - 2]).then_inc(q["s_probs"], 1)

            def probs_t_s(b, i, n):
                act.wait_ge(q["s_probs_t"], n + 1)
                act.activation(pwt[:, 4:8, :].rearrange("p k t -> p (k t)"), ps[:, 6, :], ACT.Copy)
                act.activation(pwt[:, 8, :], ps[:, 7, 256:384], ACT.Copy).then_inc(q["s_pt_act"], 1)

            act.wait_ge(q["state_stored"], 16 * (NB + 1))
            with act.Fori(0, R) as r:
                prompt_head(r)
                act.wait_ge(q["pv"], (r + 1) * U)
                keys_s(r * 2)
                probs_s(0, r * 2)
                keys_s(r * 2 + 1)
                probs_t_s(0, r, r * 2)
                probs_s(1, r * 2 + 1)
                probs_t_s(1, r, r * 2 + 1)

            act.wait_ge(q["mdiff_ready"], 1)
            act.activation(chunk_w[:], chunk_w[:], ACT.Exp).then_inc(q["mw_ready"], 1)
            act.wait_ge(q["diff_ready"], 1)
            act.activation(small[:, C_F:C_F + 8], small[:, C_F:C_F + 8], ACT.Exp).then_inc(q["wts_ready"], 1)

            act.wait_ge(q["os_ready"], 1)
            for r in range(R):
                act.wait_ge(q["pt_in_psum"], r + 1)
                act.activation(xh[:, r, 0:SEQ], ps[:, r % 2, :], ACT.Copy)
                act.activation(xh[:, r, SEQ:T], os_sum[:, r, :, :].rearrange("p n q -> p (n q)"), ACT.Copy
                               ).then_inc(q["at_hi"], 1)
            act.activation(xh[:, R:KC, :], yconv[:], ACT.Copy).then_inc(q["at_hi"], 1)

            for t in range(KC):
                s = t % 2
                split_w(s, USES["out"][s] + t // 2, (FILLS["out"][s] + 3 * (t // 2 + 1)) * 16)
            norm_scale(1, True)
            ffn_gates(1)
            norm_scale(2, False)
            for t in range(QT + 1):
                w = 128 if t < QT else NS
                act.wait_ge(q["y_in_psum"], t + 1)
                act.activation(yout[0:w, t, 0:512], ps[0:w, 4 + 2 * (t % 2), :], ACT.Copy).then_inc(q["y_by_act"], 1)

        @block.vector
        def _(dve):
            steps = Steps(dve, dve_step)
            def split_w(s, use):
                dve.wait_ge(w_hi[s], use + 1)
                dve.tensor_tensor(glo[s][:], graw[s][:], ghi[s][:].bitcast(F32), ALU.subtract).then_inc(w_lo[s], 1)

            def split_d(s, use):
                dve.wait_ge(d_hi[s], use + 1)
                dve.tensor_tensor(dlo[s][:], draw[s][:], dhi[s][:].bitcast(F32), ALU.subtract).then_inc(d_lo[s], 1)

            dve.wait_ge(const_ready, 6)
            F = C_F
            by_head = ident[:].rearrange("p (x r q) -> p x q r", r=R, q=NQ)
            steps(dve.tensor_reduce(small[:, F:F + 32].rearrange("p (x q) -> p x q", q=NQ), by_head, AX, ALU.add))
            dve.tensor_reduce(fold[:], ident[:].rearrange("p (c r) -> p r c", c=CH), AX, ALU.add)
            steps.settle()
            dve.tensor_copy(same[:].rearrange("p (x r q) -> p x r q", r=R, q=NQ),
                            small[:, F:F + 32].rearrange("p (x o q) -> p x o q", o=1, q=NQ).broadcast_to([128, 8, R, NQ]))
            steps(dve.tensor_reduce(small[:, 0:NQ], ident[:, 0:NS].rearrange("p (x q) -> p q x", q=NQ), AX, ALU.add))
            steps(dve.tensor_reduce(small[:, 16:32].rearrange("p (n q) -> p n q", q=NQ),
                                    ident[:].rearrange("p (n x q) -> p n q x", n=4, q=NQ), AX, ALU.add))
            steps.settle()
            for k in range(NQ):
                steps(dve.tensor_reduce(small[:, 4 + k:5 + k], small[:, k:NQ], AX, ALU.add))
                steps(dve.tensor_reduce(small[:, 32:48].rearrange("p (n k) -> p n k", k=NQ)[:, :, k],
                                        small[:, 16:32].rearrange("p (n q) -> p n q", q=NQ)[:, :, k:NQ], AX, ALU.add))
            steps.settle()
            dve.tensor_scalar(win_mask[:, 0:NQ], small[:, 4:8], NEG, None, ALU.mult)
            for nh in range(2):
                last = dve.tensor_scalar(new_mask[:, nh, 16 * nh:16 * nh + 16], small[:, 32:48], -1.0, -NEG,
                                         ALU.add, ALU.mult)
            last.then_inc(q["masks_ready"], 1)

            dve.wait_ge(par_in_psum, 1)
            dve.tensor_copy(par[:], ps[:, 7, 0:96]).then_inc(par_ready, 1)
            for k in range(KC):
                dve.wait_ge(xt_hi, k + 1)
                b = 2 * (k % 2)
                for bank, w, cols in ((b, SEQ, slice(0, SEQ)), (b + 1, NS, slice(SEQ, T))):
                    dve.tensor_tensor(xl[:, k, cols], ps[:, bank, 0:w], xh[:, k, cols].bitcast(F32), ALU.subtract)
                    last = dve.tensor_scalar(x[:, k, cols], ps[:, bank, 0:w], ALPHA, None, ALU.mult)
                last.then_inc(xt_done, 1)
            dve.wait_ge(xt_done, KC)
            dve.wait_ge(q["bias_in_psum"], 1)
            dve.tensor_copy(hid_bias[:], ps[:, 7, 0:1]).then_inc(q["bias_ready"], 1)
            with dve.Fori(0, NB // 2) as i:
                for b in range(2):
                    dve.wait_ge(q[f"kc_in_psum{b}"], i + 1)
                    dve.tensor_copy(kc_all[:, DS(i * 2 + b, 1), :], ps[:, 4 + b:5 + b, 0:NBLK])
                    dve.tensor_copy(vc_all[:, DS(i * 2 + b, 1), :], ps[0:NBLK, 6 + b:7 + b, 0:128]
                                    ).then_inc(q[f"kc_ready{b}"], 1)

            def ffn_values(n):
                uses = USES[("ffa", "ffb")[n]]
                for half in range(2):
                    before = n * FT + half * FH

                    def gated(j):
                        dve.wait_ge(w_used[1], j + (uses[1] + half * FH + 1))
                        dve.wait_ge(sg_ready, j + (before + 1))
                        dve.wait_ge(hh_ready, j + before)
                        dve.wait_ge(hl_ready, j + before)
                        dve.tensor_tensor(ht[:].rearrange("p (h t) -> p h t", h=2), ps[:, 2:4, 0:HALF],
                                          sg[:].rearrange("p (h t) -> p h t", h=2), ALU.mult).then_inc(ht_ready, 1)
                        dve.wait_ge(ht_ready, j + (before + 1))
                        dve.wait_ge(hh_ready, j + (before + 1))
                        dve.tensor_tensor(hl[:, DS(j, 1), :], ht[:], hh[:, DS(j, 1), :].bitcast(F32),
                                          ALU.subtract).then_inc(hl_ready, 1)

                    split_w(0, uses[0] + half * FH)
                    split_w(1, uses[1] + half * FH)
                    with dve.Fori(1, FH) as i:
                        split_w(0, i + (uses[0] + half * FH))
                        gated(i - 1)
                        split_w(1, i + (uses[1] + half * FH))
                    use = (2 * n + half) * (KC // 2)
                    split_d(0, use)
                    gated(FH - 1)

                    def add_y(s, i):
                        dve.wait_ge(d_used[s], i + (use + 1))
                        xt = x[:, DS(i * 2 + s, 1), :].rearrange("p o (h t) -> p (o h) t", h=2)
                        dve.scalar_tensor_tensor(xt, ps[:, 4 + 2 * s:6 + 2 * s, 0:HALF], 0.5, xt, ALU.mult, ALU.add
                                                 ).then_inc(y_added[s], 1)

                    with dve.Fori(0, KC // 2 - 1) as i:
                        split_d(1, i + use)
                        add_y(0, i)
                        split_d(0, i + (use + 1))
                        add_y(1, i)
                    split_d(1, use + KC // 2 - 1)
                    add_y(0, KC // 2 - 1)
                    add_y(1, KC // 2 - 1)

            def norm_values(n, split):
                for h in range(2):
                    hs = slice(h * HALF, (h + 1) * HALF)
                    dve.tensor_reduce(csum[:, hs], x[:, :, hs].rearrange("p k t -> p t k"), AX, ALU.add
                                      ).then_inc(csum_ready, 1)
                for h in range(2):
                    hs = slice(h * HALF, (h + 1) * HALF)
                    dve.wait_ge(mean_ready, 2 * n + h + 1)
                    dve.tensor_tensor(x[:, :, hs], x[:, :, hs],
                                      ps[:, h:h + 1, 0:HALF].broadcast_to([128, KC, HALF]), ALU.subtract
                                      ).then_inc(centered, 1)
                for h in range(2):
                    hs = slice(h * HALF, (h + 1) * HALF)
                    dve.wait_ge(sq_ready, 2 * n + h + 1)
                    dve.tensor_reduce(csum[:, hs], sq[:, :, hs].rearrange("p k t -> p t k"), AX, ALU.add
                                      ).then_inc(csum_ready, 1)
                dve.wait_ge(std_ready, 2 * n + 2)
                steps(dve.reciprocal(rstd[:], rstd[:]))
                dve.wait_ge(centered, 2 * n + 2)
                steps.settle()
                for k in range(KC):
                    dve.tensor_tensor(x[:, k, :], x[:, k, :], rstd[:], ALU.mult).then_inc(scaled, 1)
                if split:
                    for k in range(KC):
                        dve.wait_ge(norm_hi, KC * n + k + 1)
                        dve.tensor_tensor(xl[:, k, :], x[:, k, :], xh[:, k, :].bitcast(F32), ALU.subtract
                                          ).then_inc(norm_lo, 1)
                        steps(dve.tensor_scalar(x[:, k, :], x[:, k, :], ALPHA, None, ALU.mult))
                    steps.settle()

            ffn_values(0)
            dve.wait_ge(y_added[0], 2 * (KC // 2))
            dve.wait_ge(y_added[1], 2 * (KC // 2))
            norm_values(0, True)

            for s, uses in ((0, 1),):
                split_w(0, USES["proj"][0])
            with dve.Fori(0, NT // 2) as i:
                split_w(1, i + USES["proj"][1])
                split_w(0, i + (USES["proj"][0] + 1))

            for t in range(QT + 1):
                w = 128 if t < QT else NS
                dve.wait_ge(tok_in_psum, t + 1)
                b = 4 + 2 * (t % 2)
                dve.tensor_copy(kvtok[0:w, t, 0:4, :], ps[0:w, b, :].rearrange("p (j c) -> p j c", j=4))
                dve.tensor_copy(kvtok[0:w, t, 4:6, :], ps[0:w, b + 1, 0:256].rearrange("p (j c) -> p j c", j=2)
                                ).then_inc(tok_out, 1)


            dve.tensor_copy(rep8[:], ident[0:8, 0:8].rearrange("p (o b) -> p o b", o=1).broadcast_to([8, NH, 8]))
            for br in range(BR):
                dve.tensor_copy(
                    gate_sel[br // 2][:, br % 2 * R:(br % 2 + 1) * R, :].rearrange("p r (g d) -> p r g d", g=G),
                    ident[0:BR * NH, br * NH:(br + 1) * NH].rearrange("p (g r o) -> p r g o", g=G, o=1).broadcast_to(
                        [BR * NH, R, G, HD]))
            for g in range(G):
                gp = slice(g * HD, (g + 1) * HD)
                last = dve.tensor_scalar(
                    qbd[gp, :, g * 16:(g + 1) * 16].rearrange("p n (r q) -> p n r q", q=NQ),
                    zr[gp, 0:R, SEQ:T].rearrange("p r (n q) -> p n r q", q=NQ), SCALE, None, ALU.mult)
            last.then_inc(q["qbd_ready"], 1)

            dve.wait_ge(q["scmp_in_psum"], 1)
            dve.tensor_reduce(small[:, C_NCM:C_NCM + 2], ps[:, 0, 0:128].rearrange("p (n b) -> p n b", b=NBLK), AX,
                              ALU.max, negate=True).then_inc(q["ncm_ready"], 1)
            dve.wait_ge(q["snew_in_psum"], 1)
            dve.tensor_reduce(small[:, C_NNM:C_NNM + 4], ps[:, 1, 0:128].rearrange("p (n b) -> p n b", b=NS), AX,
                              ALU.max, negate=True).then_inc(q["nnm_ready"], 1)
            dve.memset(one[:], 1.0)
            dve.wait_ge(q["ecmp_ready"], 1)
            steps(dve.reciprocal(small[:, C_CSUM:C_CSUM + 2], small[:, C_CSUM:C_CSUM + 2]))
            steps.settle()
            for nh in range(2):
                last = dve.tensor_scalar(pcs[:, nh, :], pcs[:, nh, :], small[:, C_CSUM + nh:C_CSUM + nh + 1], None,
                                         ALU.mult)
            last.then_inc(q["pcs_ready"], 1)
            dve.wait_ge(q["gates_in_psum"], 1)
            dve.tensor_copy(gate_s[:].rearrange("p k n -> p (k n)"), ps[:, 2, 0:BR * R * NS])
            dve.tensor_copy(sext[:, :, :, 0:2], ps[:, 3, 128:192].rearrange("p (t n i) -> p t n i", t=4, i=2))
            steps(dve.tensor_copy(gate_p[:], ps[:, 3, 0:128].rearrange("p (t k) -> p t k", t=QT)[:, :, 0:BR * NH]))
            steps.settle()
            dve.engine_nop().then_inc(q["gates_ready"], 1)

            dve.wait_ge(q["imp_in_psum"], 1)
            dve.tensor_copy(pct[:].rearrange("p n r -> p (n r)"), ps[0:NBLK, 5, 0:256]).then_inc(q["pct_ready"], 1)
            steps(dve.tensor_copy(imp[:].rearrange("p n (a h) -> p n h a", h=2),
                                  ps[:, 4, 0:128].rearrange("p (n h a) -> p n h a", n=2, h=2)))
            steps.settle()
            mid_blocks = slice(1, NBLK - 1)
            picks = N_SEL - 3
            for nh in range(2):
                cand = imp[:, nh, mid_blocks]
                m1, m2 = small[:, C_M1 + 8 * nh:C_M1 + 8 * nh + 8], small[:, C_M2 + 8 * nh:C_M2 + 8 * nh + 8]
                cnt = small[:, C_CNT + nh:C_CNT + nh + 1]
                steps(dve.max(m1, cand)); steps.settle()
                steps(dve.match_replace(rest[:, nh, mid_blocks], m1, cand, -1.0)); steps.settle()
                steps(dve.max(m2, rest[:, nh, mid_blocks])); steps.settle()
                last_in = small[:, C_M2 + 8 * nh + picks - 9:C_M2 + 8 * nh + picks - 8]
                steps(dve.tensor_scalar(gt[:, nh, mid_blocks], cand, last_in, None, ALU.is_gt, ALU.add, accum_out=cnt))
                steps(dve.tensor_scalar(eq[:, nh, mid_blocks], cand, last_in, None, ALU.is_equal)); steps.settle()
                steps(dve.tensor_scalar(cnt, cnt, -1.0, float(picks), ALU.mult, ALU.add))
                steps(dve.tensor_tensor_scan(pre[:, nh, mid_blocks], one[:, mid_blocks], eq[:, nh, mid_blocks], 0.0,
                                             ALU.mult, ALU.add)); steps.settle()
                steps(dve.scalar_tensor_tensor(rest[:, nh, mid_blocks], pre[:, nh, mid_blocks], cnt,
                                               eq[:, nh, mid_blocks], ALU.is_le, ALU.mult)); steps.settle()
                steps(dve.tensor_tensor(gt[:, nh, mid_blocks], gt[:, nh, mid_blocks], rest[:, nh, mid_blocks],
                                        ALU.add)); steps.settle()
                dve.tensor_scalar(selneg[:, nh, mid_blocks], gt[:, nh, mid_blocks], -1.0, -NEG, ALU.add, ALU.mult)
                last = dve.memset(selneg[:, nh, 0:NBLK:NBLK - 1], 0.0)
            last.then_inc(q["sel_ready"], 1)

            dve.wait_ge(q["kcp_in_psum"], 1)
            dve.tensor_scalar(kcp[:], ps[:, 6, 0:8], SCALE, None, ALU.mult)
            dve.tensor_copy(vcp[:], ps[0:8, 7, 0:128]).then_inc(q["kcp_ready"], 1)
            dve.wait_ge(q["ocs_in_psum"], 1)
            dve.tensor_copy(ocs[:].rearrange("p n d -> p (n d)"), ps[:, 0, 0:256]).then_inc(q["ocs_ready"], 1)
            dve.wait_ge(q["pnewt_in_psum"], 1)
            dve.tensor_copy(pnt[:].rearrange("p k r -> p (k r)"), ps[0:NS, 1, :]).then_inc(q["pnewt_ready"], 1)
            dve.wait_ge(q["selt_in_psum"], 1)
            dve.tensor_copy(selt[:].rearrange("p n b -> p (n b)"), ps[:, 5, 0:128]).then_inc(q["selt_ready"], 1)
            dve.wait_ge(q["rep_in_psum"], 1)
            dve.tensor_tensor(vbd[:], ps[0:64, 7, 0:128].rearrange("p (o g d) -> p o g d", o=1, g=G).broadcast_to(
                [64, R, G, HD]), diag[:].rearrange("p r (g o) -> p r g o", o=1).broadcast_to([64, R, G, HD]), ALU.mult
                ).then_inc(q["vbd_ready"], 1)

            dve.wait_ge(q["sp_in_psum"], 1)
            w_p = pp[0][:, 0:256]
            by_row = w_p.rearrange("p (x b) -> p x b", b=8)
            for g in range(G):
                steps(dve.tensor_tensor(
                    w_p.rearrange("p (t g r b) -> p t g r b", t=QT, g=G, r=R)[:, :, g, :, :],
                    ps[:, 2 + g, 0:128].rearrange("p (t r b) -> p t r b", t=QT, r=R),
                    blk_neg[:].rearrange("p t (o b) -> p t o b", o=1).broadcast_to([128, QT, R, 8]), ALU.add))
            steps.settle()
            mx = small[:, C_MX:C_MX + 32]
            wide = mx.rearrange("p (x o) -> p x o", o=1).broadcast_to([128, 32, 8])
            steps(dve.tensor_reduce(mx, by_row, AX, ALU.max)); steps.settle()
            dve.tensor_tensor(by_row, by_row, wide, ALU.subtract).then_inc(q["sp_shifted"], 1)
            dve.wait_ge(q["ep_ready"], 1)
            steps(dve.tensor_tensor(w_p.rearrange("p (t x b) -> p t x b", t=QT, b=8),
                                    w_p.rearrange("p (t x b) -> p t x b", t=QT, b=8),
                                    blk_ok[:].rearrange("p t (o b) -> p t o b", o=1).broadcast_to([128, QT, NH, 8]),
                                    ALU.mult)); steps.settle()
            steps(dve.tensor_reduce(mx, by_row, AX, ALU.add)); steps.settle()
            steps(dve.tensor_scalar(mx, mx, 0.5, None, ALU.max)); steps.settle()
            steps(dve.reciprocal(mx, mx)); steps.settle()
            steps(dve.tensor_tensor(mx.rearrange("p (t x) -> p t x", t=QT), mx.rearrange("p (t x) -> p t x", t=QT),
                                    gate_p[:, :, 0:NH], ALU.mult)); steps.settle()
            dve.tensor_tensor(by_row, by_row, wide, ALU.mult).then_inc(q["pp_ready"], 1)
            dve.wait_ge(q["onew_in_psum"], 1)
            dve.tensor_copy(onew, ps[:, 4, :]).then_inc(q["onew_ready"], 1)
            dve.wait_ge(q["ptp_in_psum"], 1)
            dve.tensor_copy(ptp[:].rearrange("p t c -> p (t c)"), ps[0:64, 6, :]).then_inc(q["ptp_ready"], 1)

            steps(dve.tensor_tensor(zc[:, 4:8, :], zc[:, 4:8, :], zc[:, 8:12, :], ALU.mult)); steps.settle()
            dve.tensor_copy(sext[:, :, :, 2:2 + NQ], zc[:, 4:8, SEQ:T].rearrange("p t (n i) -> p t n i", i=NQ)
                            ).then_inc(q["u_ready"], 1)
            dve.wait_ge(q["u_ready"], 1)
            for k in range(3):
                lag = 2 - k if k < 2 else 0
            for tap in (2, 1, 0):
                lag = 2 - tap
                for t in range(4):
                    wt = par[:, R_WC + 4 * tap + t:R_WC + 4 * tap + t + 1]
                    z, u, e = zc[:, 8 + t, :], zc[:, 4 + t, :], sext[:, t, :, tap:tap + NQ]
                    zs = z[:, SEQ:T].rearrange("p (n i) -> p n i", i=NQ)
                    if tap == 2:
                        dve.tensor_scalar(z[:, 0:SEQ], u[:, 0:SEQ], wt, None, ALU.mult)
                        steps(dve.tensor_scalar(zs, e, wt, None, ALU.mult))
                    else:
                        dve.scalar_tensor_tensor(z[:, lag:SEQ], u[:, 0:SEQ - lag], wt, z[:, lag:SEQ], ALU.mult, ALU.add)
                        steps(dve.scalar_tensor_tensor(zs, e, wt, zs, ALU.mult, ALU.add))
                steps.settle()
            dve.tensor_tensor(yconv[:], zc[:, 0:4, :], zc[:, 8:12, :], ALU.mult).then_inc(q["conv_ready"], 1)
            dve.wait_ge(q["ctok_in_psum"], 1)
            dve.tensor_copy(ctok[:, 0, :], ps[0:NS, 5, :])
            dve.tensor_copy(ctok[:, 1, :], ps[0:NS, 7, :]).then_inc(q["ctok_ready"], 1)

            units = [(br, t, g) for br in range(2) for t in range(QT) for g in range(G)]
            U = len(units)
            dve.wait_ge(q["op_ready"], 1)
            def prompt_head(r):
                dve.wait_ge(q["scores"], r * U)
                dve.tensor_scalar(qs[:].rearrange("p (o t) -> p o t", o=1), zr[:, DS(r, 1), 0:SEQ], SCALE, None, ALU.mult
                                  ).then_inc(q["qs_ready"], 1)
                for j in range(U + 3):
                    if j < U:
                        br, t, g = units[j]
                        dve.wait_ge(q["scores"], r * U + (j + 1))
                        dve.tensor_reduce(small[:, C_PNM + j:C_PNM + j + 1], ps[:, j % 3, 0:(t + 1) * 128], AX, ALU.max,
                                          negate=True).then_inc(q["negmax"], 1)
                    if j >= 3:
                        k = j - 3
                        br, t, g = units[k]
                        rec, gs = small[:, C_REC:C_REC + 1], small[:, C_GS:C_GS + 1]
                        dve.wait_ge(q["pv"], r * U + (k + 1))
                        dve.wait_ge(q["o_added"], r * U + k)
                        steps(dve.reciprocal(rec, small[:, C_PSUM + k:C_PSUM + k + 1])); steps.settle()
                        steps(dve.tensor_tensor(gs, rec, gate_p[:, t, DS(r + ((1 + br) * NH + g * R), 1)], ALU.mult))
                        steps.settle()
                        o = po[:, t, DS(r, 1), g * HD:(g + 1) * HD].rearrange("p o d -> p (o d)")
                        dve.scalar_tensor_tensor(o, ps[:, 5 + k % 2, 0:HD], gs, o, ALU.mult, ALU.add
                                                 ).then_inc(q["o_added"], 1)

            def queries(b, n, scored):
                dve.wait_ge(q["s_scores"], scored)
                dve.tensor_copy(qn[b][:].rearrange("p (o r) -> p o r", o=1), qbd[:, DS(n, 1), :]
                                ).then_inc(q["qn_ready"], 1)

            def keys_s(n):
                for m in range(1, 9, 2):
                    dve.wait_ge(q["kt_in_psum"], n * 9 + (m + 1))
                    if m == 1:
                        dve.wait_ge(q["s_scores"], n)
                    dve.tensor_copy(kt[:, 4 * m:4 * m + 4, :].rearrange("p k t -> p (k t)"), ps[:, 1, :]
                                    ).then_inc(q["kt_by_dve"], 1)

            def negmax_s(n):
                dve.wait_ge(q["s_scores"], n + 1)
                dve.tensor_reduce(cb[:, DS(n, 1), 0, OB - 1], ps[:, 2:4, :].rearrange("p b t -> p (b t)"), AX, ALU.max,
                                  negate=True)
                dve.tensor_reduce(cb[:, DS(n, 1), 1, OB - 1], ps[:, 4, 0:128], AX, ALU.max, negate=True
                                  ).then_inc(q["s_negmax"], 1)

            def probs_t_s(n):
                dve.wait_ge(q["s_probs_t"], n + 1)
                dve.tensor_copy(pwt[:, 0:4, :].rearrange("p k t -> p (k t)"), ps[:, 5, :]).then_inc(q["s_pt_dve"], 1)

            def out_s(b, i, n):
                dve.wait_ge(q[f"s_pv{b}"], i + 1)
                dve.tensor_copy(cb[:, DS(n, 1), :, 0:128].rearrange("p o b d -> p (o b) d"),
                                ps[:, 7, 0:256].rearrange("p (b d) -> p b d", b=2)).then_inc(q["s_o"], 1)

            dve.wait_ge(q["state_stored"], 16 * (NB + 1))
            with dve.Fori(0, R) as r:
                steps.enter(r, 0, 2 * U)
                prompt_head(r)
                queries(0, r * 2, r * 2)
                queries(1, r * 2 + 1, r * 2)
                keys_s(r * 2)
                negmax_s(r * 2)
                dve.wait_ge(q["pv"], (r + 1) * U)
                keys_s(r * 2 + 1)
                probs_t_s(r * 2)
                out_s(0, r, r * 2)
                negmax_s(r * 2 + 1)
                probs_t_s(r * 2 + 1)
                out_s(1, r, r * 2 + 1)
            steps.leave(R)

            dve.wait_ge(q["m_in_psum"], 1)
            steps(dve.tensor_reduce(neg_row[:], ps[0:16, 0, 0:128].rearrange("p (c r) -> p r c", c=CH), AX, ALU.min))
            steps.settle()
            dve.tensor_copy(neg_rep[:], neg_row[:].rearrange("p (o r) -> p o r", o=1).broadcast_to([16, CH, NS])
                            ).then_inc(q["m_ready"], 1)
            dve.wait_ge(q["mb_in_psum"], 1)
            steps(dve.tensor_copy(neg_all[:], ps[:, 1, 0:16])); steps.settle()
            cbf = cb[:].rearrange("p n b o -> p (n b) o")
            dve.tensor_tensor(chunk_w[:], neg_all[:], cbf[:, :, OB - 1], ALU.subtract).then_inc(q["mdiff_ready"], 1)
            dve.wait_ge(q["mw_ready"], 1)
            dve.tensor_tensor(cbf[:, :, 0:OB - 1], cbf[:, :, 0:OB - 1],
                              chunk_w[:].rearrange("p (x o) -> p x o", o=1).broadcast_to([128, 16, OB - 1]), ALU.mult)
            dve.tensor_scalar(cbf[:, :, OB - 1], neg_all[:], 1.0 / CH, None, ALU.mult).then_inc(q["cb_scaled"], 1)
            dve.wait_ge(q["comb_in_psum"], 1)
            steps(dve.tensor_copy(comb[:].rearrange("p n b o -> p n (b o)"), ps[:, 2:4, 0:2 * OB]))
            steps.settle()
            F = C_F
            four = lambda c: small[:, c:c + 4].rearrange("p (b n) -> p b n", b=2)
            wide4 = lambda c: small[:, c:c + 4].rearrange("p (x o) -> p x o", o=1).broadcast_to([128, 4, 128])
            neg_c = comb[:, :, :, OB - 1].rearrange("p n b -> p b n")
            sum_c = comb[:, :, :, OB - 2].rearrange("p n b -> p b n")
            steps(dve.tensor_tensor(four(F + 8), neg_c, four(C_NNM), ALU.min)); steps.settle()
            dve.tensor_tensor(four(F), four(F + 8), neg_c, ALU.subtract)
            dve.tensor_tensor(four(F + 4), four(F + 8), four(C_NNM), ALU.subtract).then_inc(q["diff_ready"], 1)
            dve.wait_ge(q["wts_ready"], 1)
            steps(dve.tensor_tensor(four(F + 12), four(F), sum_c, ALU.mult))
            steps(dve.tensor_tensor(four(F + 16), four(F + 4), four(C_NSUM), ALU.mult)); steps.settle()
            steps(dve.tensor_tensor(four(F + 20), four(F + 12), four(F + 16), ALU.add)); steps.settle()
            steps(dve.reciprocal(four(F + 24), four(F + 20))); steps.settle()
            steps(dve.tensor_tensor(four(F + 28), four(F), four(F + 24), ALU.mult))
            steps(dve.tensor_tensor(four(F + 32), four(F + 4), four(F + 24), ALU.mult)); steps.settle()
            onew4 = onew.rearrange("p (x d) -> p x d", d=128)
            for k in range(4):
                br, nh = k // 2, k % 2
                steps(dve.tensor_scalar(onew4[:, k, :], onew4[:, k, :], small[:, F + 32 + k:F + 33 + k], None, ALU.mult))
            steps.settle()
            for k in range(4):
                br, nh = k // 2, k % 2
                last = dve.scalar_tensor_tensor(ofin[:, nh, br, :], comb[:, nh, br, 0:128], small[:, F + 28 + k:F + 29 + k],
                                                onew4[:, k, :], ALU.mult, ALU.add)
            last.then_inc(q["ofin_ready"], 1)
            dve.wait_ge(q["ofin_in_psum"], 1)
            for g in range(G):
                gp = slice(g * HD, (g + 1) * HD)
                for br in range(BR):
                    for nh in range(2):
                        steps(dve.tensor_tensor(
                            os_all[gp, br, nh, :, :, :],
                            ps[gp, 4 + br, nh * 128:(nh + 1) * 128].rearrange(
                                "p (n g r q) -> p n g r q", n=4, g=G, r=R)[:, :, g, :, :],
                            gate_s[gp, br * R:(br + 1) * R, nh * 16:(nh + 1) * 16].rearrange(
                                "p r (n q) -> p n r q", q=NQ), ALU.mult))
            steps.settle()
            sum_o = os_all[:].rearrange("p b h n r q -> p b (h n) r q")
            out_o = os_sum[:].rearrange("p r n q -> p n r q")
            steps(dve.tensor_tensor(out_o, sum_o[:, 0], sum_o[:, 1], ALU.add)); steps.settle()
            dve.tensor_tensor(out_o, out_o, sum_o[:, 2], ALU.add).then_inc(q["os_ready"], 1)
            dve.wait_ge(q["os_ready"], 1)
            for r in range(R):
                dve.wait_ge(q["at_hi"], r + 1)
                dve.tensor_tensor(xl[:, r, 0:SEQ], ps[:, r % 2, :], xh[:, r, 0:SEQ].bitcast(F32), ALU.subtract)
                dve.tensor_tensor(xl[:, r, SEQ:T], os_sum[:, r, :, :].rearrange("p n q -> p (n q)"),
                                  xh[:, r, SEQ:T].bitcast(F32), ALU.subtract).then_inc(q["at_lo"], 1)
            dve.wait_ge(q["at_hi"], R + 1)
            dve.tensor_tensor(xl[:, R:KC, :], yconv[:], xh[:, R:KC, :].bitcast(F32), ALU.subtract
                              ).then_inc(q["at_lo"], 1)

            def add_out(t):
                s = t % 2
                dve.wait_ge(w_used[s], USES["out"][s] + t // 2 + 1)
                xt = x[:, t, :].rearrange("p (h t) -> p h t", h=2)
                dve.tensor_tensor(xt, ps[:, 2 * s:2 * s + 2, 0:HALF], xt, ALU.add).then_inc(q["out_added"], 1)

            split_w(0, USES["out"][0])
            for t in range(1, KC):
                split_w(t % 2, USES["out"][t % 2] + t // 2)
                add_out(t - 1)
            add_out(KC - 1)
            dve.wait_ge(q["out_added"], KC)
            norm_values(1, True)
            ffn_values(1)
            dve.wait_ge(y_added[0], 4 * (KC // 2))
            dve.wait_ge(y_added[1], 4 * (KC // 2))
            norm_values(2, False)
            for t in range(QT + 1):
                w = 128 if t < QT else NS
                dve.wait_ge(q["y_in_psum"], t + 1)
                dve.tensor_copy(yout[0:w, t, 512:1024], ps[0:w, 5 + 2 * (t % 2), :]).then_inc(q["y_by_dve"], 1)


_INS = ["x_prompt", "x_sample", "cache_cmp_kv", "cache_sel_kv", "state_win_kv", "state_conv", "page_table",
        "ffa_gate", "ffa_up", "ffa_down", "ln1_g", "ln1_b", "w_in", "b_in", "w_conv", "cmp_w1", "cmp_w2", "cmp_pe",
        "w_out", "ln2_g", "ln2_b", "ffb_gate", "ffb_up", "ffb_down", "ln3_g", "ln3_b"]
_OUTS = [(1, SEQ, D), (NB, NQ, D), (1, 1, SEQ, 2, G, HD), (1, 1, SEQ, 2, G, HD), (1, 1, WIN, 2, G, HD),
         (1, 1, 2, DC), (1, NB, NQ, 2, G, HD), (1, NB, NQ, 2, G, HD), (1, NB, WIN, 2, G, HD), (1, NB, 2, DC)]


def kernel(**inputs):
    import numpy as _np
    import concourse.bacc as _bacc
    from concourse import mybir as _mybir
    from concourse.bass_utils import run_bass_kernel_spmd as _run

    nc = _bacc.Bacc("TRN2", target_bir_lowering=False, num_devices=1)
    arrays, args = {}, []
    for name in _INS:
        a = _np.ascontiguousarray(inputs[name])
        arrays[f"in_{name}_dram"] = a
        args.append(nc.dram_tensor(f"in_{name}_dram", a.shape, _mybir.dt.from_np(a.dtype), kind="ExternalInput").ap())
    for i, shape in enumerate(_OUTS):
        args.append(nc.dram_tensor(f"out_{i}_dram", shape, _mybir.dt.float32, kind="ExternalOutput").ap())
    trunk(nc, *args)
    r = _run(nc, [arrays], core_ids=[0])
    return tuple(r.results[0][f"out_{i}_dram"] for i in range(len(_OUTS)))
```

```python
from contextlib import ExitStack

import concourse.bass as bass
from concourse import mybir

F32 = mybir.dt.float32
F32R = mybir.dt.float32r
BF16 = mybir.dt.bfloat16
I32 = mybir.dt.int32
ALU = mybir.AluOpType
ACT = mybir.ActivationFunctionType
AX = mybir.AxisListType.X
DS = bass.ds

D = 1024
SEQ = 512
NB = 8
NQ = 4
NS = NB * NQ
T = SEQ + NS
HALF = T // 2
KC = D // 128
FF = 2816
FT = FF // 128
FH = FT // 2
DC = 512
HD = 64
G = 2
R = 4
NH = G * R
BR = 3
BLK = 64
PAGE = 128
NPG = 32
NPHYS = 320
NBLK = NPG * 2
KVW = 256
QT = SEQ // 128
CH = 4
PC = NPG // CH
WIN = 512
N_SEL = 16
ALPHA = 2.0 ** 0.25
SCALE = HD ** -0.5
EPS = 1e-5
NEG = -1e30
ZC = 3 * DC // 128
ZR = 11
Q0, KV0, G0 = 0, 4, 10
OFF_Q = 3 * DC
OFF_KV = OFF_Q + NH * HD
OFF_G = OFF_KV + 3 * KVW
OB = 130

R_LN = 0
R_BC, R_BQ, R_BKV, R_BG = 48, 60, 64, 70
R_WC = 71
R_ALL = 83


USES = {"ffa": (0, 0), "proj": (FT, FT), "out": (FT + 12, FT + 11), "ffb": (FT + 16, FT + 15)}
FILLS = {"ffa": (0, 0), "proj": (FT, FT), "out": (FT + 24, FT + 22), "ffb": (FT + 36, FT + 34)}
PER_FILL = {"ffa": 1, "proj": 2, "out": 3, "ffb": 1}
NT = ZC + ZR

UP = NPG // 2
PARTS = ((0, 1, 2), (3, 4, 5), (6, 7, 8), (9, 10, 11), (15, 12, 13, 14))
FIRST = (3, 0, 3, 0, 2)
GROUPS = len(PARTS)
PLACE = UP * KVW
PLACES0 = 2 * KC * T - 2 * PLACE
GW = 4 * 2 * UP
SPAN = PLACES0 + 6 * PLACE + 2 * HD * 128 + 2 * 2 * G * GW


C_NCM, C_CSUM, C_M1, C_M2, C_CNT, C_NNM, C_NSUM, C_PNM, C_PSUM = 0, 2, 4, 20, 36, 38, 42, 46, 62
C_REC, C_GS, C_MX, C_KEY, C_LO, C_HI, C_Q = 78, 80, 82, 114, 115, 117, 119
C_F = 120


class Steps:

    def __init__(self, eng, sem):
        self.eng, self.sem, self.n, self.i = eng, sem, 0, None

    def __call__(self, ins):
        ins.then_inc(self.sem, 1)
        self.n += 1
        return ins

    def settle(self):
        if self.i is None:
            self.eng.wait_ge(self.sem, self.n)
        else:
            i, first, per, start = self.i
            self.eng.wait_ge(self.sem, (i - first) * per + self.n)

    def enter(self, i, first, per):
        self.i = (i, first, per, self.n)

    def leave(self, times):
        _, _, per, start = self.i
        assert self.n - start == per, (self.n - start, per)
        self.i = None
        self.n = start + per * times


def trunk(nc, x_prompt, x_sample, cache_cmp, cache_sel, state_win, state_conv, page_table,
          ffa_gate, ffa_up, ffa_down, ln1_g, ln1_b, w_in, b_in, w_conv, cmp_w1, cmp_w2, cmp_pe,
          w_out, ln2_g, ln2_b, ffb_gate, ffb_up, ffb_down, ln3_g, ln3_b,
          y_prompt, y_sample, p_cmp, p_sel, p_win, p_conv, s_cmp, s_sel, s_win, s_conv):
    ctx = ExitStack()
    with ctx:
        def sb(name, shape, dt=F32, stack=ctx):
            return stack.enter_context(nc.sbuf_tensor(name, shape, dt))

        def sem(name):
            return ctx.enter_context(nc.semaphore(name))

        ident = sb("ident", [128, 128])
        identb = sb("identb", [128, 128], BF16)
        causal = sb("causal", [128, 128], BF16)
        mean_w = sb("mean_w", [128, 128])
        eps = sb("eps", [128, 1])
        par = sb("par", [128, 96])
        x = sb("x", [128, KC, T])
        pages_sb = sb("pages_sb", [1, NB * NPG], I32)
        kc_all = sb("kc_all", [128, NB, NBLK])
        vc_all = sb("vc_all", [64, NB, 128])
        w2 = sb("w2", [128, 2, HD])
        pe_sb = sb("pe_sb", [128, 2, HD])
        pe_sum = sb("pe_sum", [128, 2, HD])
        hid_bias = sb("hid_bias", [128, 3])
        same = sb("same", [128, 128])
        fold = sb("fold", [128, NS])
        win_mask = sb("win_mask", [128, 128], BF16)
        new_mask = sb("new_mask", [128, 2, NS], BF16)
        qbd = sb("qbd", [128, NB, NS])
        qn = [sb(f"qn{n}", [128, NS]) for n in range(2)]
        gate_p = sb("gate_p", [128, QT, BR * NH])
        blk_neg = sb("blk_neg", [128, QT, 8])
        blk_ok = sb("blk_ok", [128, QT, 8])
        diag = sb("diag", [64, R, G])
        selneg = sb("selneg", [128, 2, NBLK], BF16)
        selt = sb("selt", [128, NB, 16], BF16)
        small = sb("small", [128, 160])
        u1 = ExitStack()
        xh = sb("xh", [128, KC, T], F32R, u1)
        xl = sb("xl", [128, KC, T], F32R, u1)
        u1.close()
        up = ExitStack()
        w1p = sb("w1p", [128, 2, HD, HD], F32, up)
        up.close()
        first = ExitStack()
        span = sb("span", [128, SPAN], F32, first)
        first.close()
        place = [span[:, PLACES0 + k * PLACE:PLACES0 + (k + 1) * PLACE] for k in range(6)]
        cpages = [span[:, PLACES0 + at * PLACE:PLACES0 + (at + len(parts)) * PLACE].rearrange("p (a c) -> p a c", c=KVW)
                  for at, parts in zip(FIRST, PARTS)]
        xin = place[0].rearrange("p (t d) -> p t d", d=D)
        w1 = span[:, PLACES0 + PLACE:PLACES0 + 3 * PLACE].rearrange("p (c d h) -> p c d h", c=2, d=HD)
        prow = place[5][:, 0:128]
        xin_s = place[5][0:NS, 128:128 + D]
        at = PLACES0 + 6 * PLACE
        wbd = span[:, at:at + 2 * HD * 2 * HD].rearrange("p (c d a h) -> p c d a h", c=2, d=HD, a=2)
        at += 2 * HD * 2 * HD
        hid = [span[:, at + k * 2 * G * GW:at + (k + 1) * 2 * G * GW].rearrange(
            "p (c g u b) -> p c g u b", c=2, g=G, u=4) for k in range(2)]
        page0 = sb("page0", [128, 2 * KC * T])
        ffn = ExitStack()
        hh = sb("hh", [128, FH, T], F32R, ffn)
        hl = sb("hl", [128, FH, T], F32R, ffn)
        draw = [sb(f"draw{n}", [128, FH, 128], F32, ffn) for n in range(2)]
        dhi = [sb(f"dhi{n}", [128, FH, 128], F32R, ffn) for n in range(2)]
        dlo = [sb(f"dlo{n}", [128, FH, 128], F32R, ffn) for n in range(2)]
        sg = sb("sg", [128, T], F32, ffn)
        ht = sb("ht", [128, T], F32, ffn)
        csum = sb("csum", [128, T], F32, ffn)
        rstd = sb("rstd", [128, T], F32, ffn)
        sq = sb("sq", [128, KC, T], F32, ffn)
        ffn.close()
        norm = ExitStack()
        yout = sb("yout", [128, QT + 1, D], F32, norm)
        norm.close()
        zr = sb("zr", [128, ZR, T])
        kvtok = sb("kvtok", [128, QT + 1, 6, 128])
        yconv = sb("yconv", [128, 4, T])
        conv = ExitStack()
        zc = sb("zc", [128, ZC, T], F32, conv)
        conv.close()
        page1 = sb("page1", [128, NPG, KVW])
        pr = ExitStack()
        crow = sb("crow", [NB * 2, DC], F32, pr)
        ctok = sb("ctok", [NS, 2, DC], F32, pr)
        sext = sb("sext", [128, 4, NB, NQ + 2], F32, pr)
        kcp = sb("kcp", [128, 8], F32, pr)
        vcp = sb("vcp", [8, 128], F32, pr)
        hidp = sb("hidp", [128, 2, QT, G], F32, pr)
        vbd = sb("vbd", [64, R, G, HD], F32, pr)
        ptp = sb("ptp", [64, QT, 128], F32, pr)
        pnt = sb("pnt", [NS, 4, 128], F32, pr)
        rep8 = sb("rep8", [8, NH, 8], F32, pr)
        pr.close()
        fin = ExitStack()
        neg_row = sb("neg_row", [16, NS], F32, fin)
        neg_rep = sb("neg_rep", [16, CH, NS], F32, fin)
        neg_all = sb("neg_all", [128, 16], F32, fin)
        chunk_w = sb("chunk_w", [128, 16], F32, fin)
        comb = sb("comb", [128, 2, 2, OB], F32, fin)
        ofin = sb("ofin", [128, 2, 2, 128], F32, fin)
        os_all = sb("os_all", [128, BR, 2, 4, R, NQ], F32, fin)
        os_sum = sb("os_sum", [128, R, NB, NQ], F32, fin)
        fin.close()
        kt = sb("kt", [128, NPG + CH, 128])
        win = [sb(f"win{n}", [128, CH, KVW]) for n in range(2)]
        qs = sb("qs", [128, SEQ])
        two = ExitStack()
        pp = [sb(f"pp{n}", [128, SEQ], F32, two) for n in range(2)]
        two.close()
        pw = sb("pw", [128, PC + 1, 128])
        two = ExitStack()
        ppt = [sb(f"ppt{n}", [128, SEQ], F32, two) for n in range(2)]
        two.close()
        pwt = sb("pwt", [128, PC + 1, 128])
        ring = ExitStack()
        ghi = [sb(f"ghi{n}", [128, KC, 128], F32R, ring) for n in range(2)]
        glo = [sb(f"glo{n}", [128, KC, 128], F32R, ring) for n in range(2)]
        graw = [sb(f"graw{n}", [128, KC, 128], F32, ring) for n in range(2)]
        ring.close()
        mid = ExitStack()
        cb = sb("cb", [128, NB, 2, OB], F32, mid)
        po = sb("po", [128, QT, R, 128], F32, mid)
        pcs = sb("pcs", [128, 2, NBLK], F32, mid)
        pct = sb("pct", [64, 2, 128], F32, mid)
        ocs = sb("ocs", [128, 2, 128], F32, mid)
        imp = sb("imp", [128, 2, NBLK], F32, mid)
        rest = sb("rest", [128, 2, NBLK], F32, mid)
        gt = sb("gt", [128, 2, NBLK], F32, mid)
        eq = sb("eq", [128, 2, NBLK], F32, mid)
        pre = sb("pre", [128, 2, NBLK], F32, mid)
        one = sb("one", [128, NBLK], F32, mid)
        gate_s = sb("gate_s", [128, BR * R, NS], F32, mid)
        pnew = sb("pnew", [128, 4, NS], F32, mid)
        mid.close()
        onew = page0[:, NPG * KVW:NPG * KVW + 512]
        gate_sel = [win[0][0:BR * NH].rearrange("p a (b m) -> p (a b) m", m=128),
                    win[1][0:BR * NH].rearrange("p a (b m) -> p (a b) m", m=128)]
        pages = (page0[:, 0:NPG * KVW].rearrange("p (a c) -> p a c", c=KVW), page1[:])

        ps = ctx.enter_context(nc.psum_tensor("ps", [128, 8, 512], F32))

        dma_x, dma_par = sem("dma_x"), sem("dma_par")
        prow_clear, const_ready = sem("prow_clear"), sem("const_ready")
        dve_step, act_step, pool_step = sem("dve_step"), sem("act_step"), sem("pool_step")
        par_in_psum, par_ready = sem("par_in_psum"), sem("par_ready")
        xt_in_psum = sem("xt_in_psum")
        dma_w = [sem("dma_w0"), sem("dma_w1")]
        w_hi, w_lo = [sem("w_hi0"), sem("w_hi1")], [sem("w_lo0"), sem("w_lo1")]
        w_used = [sem("w_used0"), sem("w_used1")]
        sg_ready, ht_ready, hh_ready, hl_ready = sem("sg_ready"), sem("ht_ready"), sem("hh_ready"), sem("hl_ready")
        dma_d = [sem("dma_d0"), sem("dma_d1")]
        d_hi, d_lo = [sem("d_hi0"), sem("d_hi1")], [sem("d_lo0"), sem("d_lo1")]
        d_used, y_added = [sem("d_used0"), sem("d_used1")], [sem("y_added0"), sem("y_added1")]
        csum_step, mean_ready, centered = sem("csum_step"), sem("mean_ready"), sem("centered")
        sq_ready, var_ready, std_ready = sem("sq_ready"), sem("var_ready"), sem("std_ready")
        scaled, normed, norm_hi, norm_lo = sem("scaled"), sem("normed"), sem("norm_hi"), sem("norm_lo")
        z_out = [sem("z_out0"), sem("z_out1")]
        tok_in_psum, tok_out = sem("tok_in_psum"), sem("tok_out")
        stored = sem("stored")
        names = ("dma_first", "dma_cmp_w", "dma_cpage0", "dma_cpage1", "hid_in_psum", "hid_ready", "kc_in_psum", "kc_ready",
                 "wbd_by_act", "wbd_by_dve", "zeros_ready", "x_by_act", "x_by_dve", "x_hi", "x_lo", "bias_in_psum", "pe_summed", "bias_ready", "qbd_ready", "scmp_in_psum", "ncm_ready", "ecmp_ready", "pcs_ready",
                 "imp_in_psum", "pct_ready", "ocs_in_psum", "ocs_ready", "sel_ready", "selt_in_psum", "selt_ready",
                 "snew_in_psum", "nnm_ready", "pnew_ready", "pnewt_in_psum", "pnewt_ready", "onew_in_psum",
                 "onew_ready", "gates_in_psum", "gates_ready", "dma_conv", "u_ready",
                 "conv_ready", "ctok_in_psum", "ctok_ready", "dma_w1p", "hidp_in_psum", "hidp_ready",
                 "kcp_in_psum", "kcp_ready", "rep_in_psum", "vbd_ready", "sp_in_psum", "sp_shifted", "ep_ready",
                 "pp_ready", "ptp_in_psum", "ptp_ready", "op_in_psum", "op_ready", "qs_ready", "scores", "negmax",
                 "probs", "probs_t", "pt_copied", "pv", "o_added", "dma_page0", "dma_page1", "dma_win0", "dma_win1",
                 "qn_ready", "kt_in_psum", "kt_by_act", "kt_by_dve", "s_scores", "s_negmax", "s_probs",
                 "s_probs_t", "s_pt_act", "s_pt_dve", "s_pv0", "s_pv1", "s_o", "masks_ready", "state_stored", "m_in_psum", "m_ready", "mb_in_psum",
                 "mdiff_ready", "mw_ready", "cb_scaled", "comb_in_psum", "diff_ready", "wts_ready", "ofin_ready",
                 "ofin_in_psum", "os_ready", "pt_in_psum", "at_hi", "at_lo", "out_added", "y_in_psum", "y_by_act",
                 "y_by_dve", "residual")
        q = {name: sem(name) for name in names}

        block = ctx.enter_context(nc.Block())


        @block.sync
        def _(sp):
            sp.dma_start(xin, x_prompt[0].rearrange("(t p) d -> p t d", p=128)).then_inc(dma_x, 16)
            sp.dma_start(xin_s, x_sample.rearrange("n q d -> (n q) d")).then_inc(dma_x, 16)
            sp.wait_ge(prow_clear, 1)
            rows = [(R_LN + 8 * n, a[0].rearrange("(a b) -> a b", b=128))
                    for n, a in enumerate((ln1_g, ln1_b, ln2_g, ln2_b, ln3_g, ln3_b))]
            rows.append((R_BC, b_in[0, 0:OFF_Q].rearrange("(a b) -> a b", b=128)))
            rows.append((R_BKV, b_in[0, OFF_KV:OFF_G].rearrange("(a b) -> a b", b=128)))
            rows.append((R_WC, w_conv[0].rearrange("i (a b) -> (i a) b", b=128)))
            for row, src in rows:
                sp.dma_start(prow[row:row + src.shape[0], :], src).then_inc(dma_par, 16)
            for g in range(G):
                sp.dma_start(prow[R_BQ:R_BQ + R, g * HD:g * HD + HD],
                             b_in[0, OFF_Q + g * R * HD:OFF_Q + (g + 1) * R * HD].rearrange("(r d) -> r d", d=HD)
                             ).then_inc(dma_par, 16)
            sp.dma_start(prow[R_BG:R_BG + 1, 0:BR * NH],
                         b_in[0, OFF_G:OFF_G + BR * NH].rearrange("(a b) -> a b", a=1)).then_inc(dma_par, 16)

            sp.dma_start(pages_sb[:], page_table.rearrange("(a n) g -> a (n g)", a=1)).then_inc(q["dma_first"], 16)
            for h in range(2):
                rows = slice(h * BLK, (h + 1) * BLK)
                for c in range(2):
                    sp.dma_start(w1[rows, c, :, :], cmp_w1[0, c]).then_inc(q["dma_cmp_w"], 16)
                sp.dma_start(w2[rows, :, :], cmp_w2[0].rearrange("c h d -> h c d")).then_inc(q["dma_first"], 16)
                sp.dma_start(pe_sb[rows, :, :], cmp_pe[0]).then_inc(q["dma_first"], 16)

            def page_loads(dst, at, first, pool, landed):
                for j in range(0, UP, 8):
                    _, numbers = nc.values_load_multi_w_load_instructions(
                        pages_sb[0:1, DS(first + j, 8)], engines=[sp.engine], min_val=0, max_val=NPHYS - 1,
                        skip_runtime_bounds_check_because="the DMA itself checks its bounds")
                    for k, page in enumerate(numbers):
                        sp.dma_start(dst[:, DS(at + (j + k), 1), :], pool[0, DS(page, 1)].rearrange("o p c g d -> p o (c g d)")
                                     ).then_inc(landed, 16)

            sp.wait_ge(q["dma_first"], 16 * 5)
            def group_loads(g, k0, k1):
                with sp.Fori(k0, k1) as k:
                    page_loads(cpages[g], k * UP, (k + (PARTS[g][k0] - k0)) * UP, cache_cmp, q[f"dma_cpage{g % 2}"])

            group_loads(0, 0, 2)
            sp.wait_ge(q["x_by_act"], KC // 2)
            sp.wait_ge(q["x_by_dve"], KC // 2)
            group_loads(0, 2, 3)
            sp.wait_ge(q["pe_summed"], 1)
            group_loads(1, 0, 3)
            for g in range(2, GROUPS):
                sp.wait_ge(q["hid_in_psum"], g - 1)
                group_loads(g, len(PARTS[g]) - 3, len(PARTS[g]))
            sp.wait_ge(q["hid_in_psum"], GROUPS - 1)
            group_loads(GROUPS - 1, 0, 1)

            def ffn_loads(n, gate, up, down_w):
                phase = ("ffa", "ffb")[n]
                for half in range(2):
                    with sp.Fori(0, FH) as i:
                        for s, w in enumerate((gate, up)):
                            col = sp.snap((i + half * FH) * 128)
                            free = sp.snap(i + (USES[phase][s] + half * FH))
                            sp.wait_ge(w_lo[s], free)
                            sp.dma_start(graw[s][:], w[0].rearrange("(k p) f -> p k f", p=128)[:, :, DS(col, 128)]
                                         ).then_inc(dma_w[s], 16)
                    if n == 0 and half == 0:
                        sp.wait_ge(q["kc_in_psum"], GROUPS)
                    with sp.Fori(0, KC // 2) as i:
                        for s in range(2):
                            col = sp.snap((2 * i + s) * 128)
                            free = sp.snap(i + (2 * n + half) * (KC // 2))
                            sp.wait_ge(d_lo[s], free)
                            sp.dma_start(draw[s][:], down_w[0, half * FH * 128:(half + 1) * FH * 128, :].rearrange(
                                "(k p) f -> p k f", p=128)[:, :, DS(col, 128)]).then_inc(dma_d[s], 16)

            ffn_loads(0, ffa_gate, ffa_up, ffa_down)

            w_in_k = w_in[0].rearrange("(k p) f -> p k f", p=128)
            for t in range(NT):
                s = t % 2
                sp.wait_ge(w_lo[s], USES["proj"][s] + t // 2)
                for part in range(2):
                    if ZC <= t < ZC + R:
                        c0 = OFF_Q + (part * R + t - ZC) * HD
                        dst, src = graw[s][:, :, part * HD:(part + 1) * HD], w_in_k[:, :, c0:c0 + HD]
                    else:
                        wide = BR * NH if t == NT - 1 else 128
                        k = slice(part * KC // 2, (part + 1) * KC // 2)
                        dst, src = graw[s][:, k, 0:wide], w_in_k[:, k, t * 128:t * 128 + wide]
                    sp.dma_start(dst, src).then_inc(dma_w[s], 16)

            sp.dma_start(crow[:], state_conv[0].rearrange("n i d -> (n i) d")).then_inc(q["dma_conv"], 16)
            sp.wait_ge(w_used[0], USES["proj"][0] + NT // 2 + 1)
            for c in range(2):
                for h in range(2):
                    sp.dma_start(w1p[h * BLK:(h + 1) * BLK, c, :, :], cmp_w1[0, c]).then_inc(q["dma_w1p"], 16)
            n_stored = 0
            for n in range(NB):
                sp.dma_start(s_win[0, n, 0:WIN - NQ].rearrange("p c g d -> p (c g d)"),
                             state_win[0, n, NQ:WIN].rearrange("p c g d -> p (c g d)")).then_inc(stored, 16)
                n_stored += 1
            sp.wait_ge(tok_out, QT + 1)
            for j, (prompt, sample) in enumerate(((p_cmp, s_cmp), (p_sel, s_sel), (p_win, s_win))):
                for t in range(QT):
                    sp.dma_start(prompt[0, 0, t * 128:(t + 1) * 128].rearrange("p c g d -> p (c g d)"),
                                 kvtok[:, t, 2 * j:2 * j + 2, :]).then_inc(stored, 16)
                    n_stored += 1
                if j < 2:
                    sp.dma_start(sample[0].rearrange("n q c g d -> (n q) (c g d)"),
                                 kvtok[0:NS, QT, 2 * j:2 * j + 2, :]).then_inc(stored, 16)
                    n_stored += 1
                else:
                    for n in range(NB):
                        sp.dma_start(sample[0, n, WIN - NQ:WIN].rearrange("q c g d -> q (c g d)"),
                                     kvtok[n * NQ:(n + 1) * NQ, QT, 2 * j:2 * j + 2, :]).then_inc(stored, 16)
                        n_stored += 1

            def sample_loads(b, i):
                with sp.Fori(0, 2) as k:
                    page_loads(pages[b], k * UP, k * UP + (i * 2 + b) * NPG, cache_sel, q[f"dma_page{b}"])
                sp.dma_start(win[b][:], state_win[0, DS(i * 2 + b, 1)].rearrange("o (c p) k g d -> p (o c) (k g d)", p=128)
                             ).then_inc(q[f"dma_win{b}"], 16)

            sp.wait_ge(q["hidp_in_psum"], 1)
            sample_loads(0, 0)
            sp.wait_ge(q["ctok_ready"], 1)
            sp.dma_start(p_conv[0, 0], ctok[NS - 2:NS, 0, :]).then_inc(q["state_stored"], 16)
            for n in range(NB):
                sp.dma_start(s_conv[0, n], ctok[n * NQ + 2:n * NQ + 4, 1, :]).then_inc(q["state_stored"], 16)
            sp.wait_ge(q["conv_ready"], 1)
            sample_loads(1, 0)
            sp.wait_ge(stored, 16 * n_stored)
            with sp.Fori(1, NB // 2) as i:
                for b in range(2):
                    free = sp.snap(i)
                    sp.wait_ge(q["dma_first"], 16 * 5)
                    sp.wait_ge(q[f"s_pv{b}"], free)
                    sample_loads(b, i)

            w_o = w_out[0]
            sp.wait_ge(q["at_hi"], R)
            sp.wait_ge(q["pt_in_psum"], R)
            for t in range(KC):
                s = t % 2
                sp.wait_ge(w_lo[s], USES["out"][s] + t // 2)
                cols = slice(t * 128, (t + 1) * 128)
                for g in range(G):
                    sp.dma_start(graw[s][g * HD:(g + 1) * HD, 0:R, :],
                                 w_o[g * R * HD:(g + 1) * R * HD, cols].rearrange("(r d) n -> d r n", d=HD)
                                 ).then_inc(dma_w[s], 16)
                sp.dma_start(graw[s][:, R:KC, :], w_o[DC:D, cols].rearrange("(k p) n -> p k n", p=128)
                             ).then_inc(dma_w[s], 16)

            ffn_loads(1, ffb_gate, ffb_up, ffb_down)

            for t in range(QT + 1):
                sp.wait_ge(q["y_by_act"], t + 1)
                sp.wait_ge(q["y_by_dve"], t + 1)
                if t < QT:
                    sp.dma_start(y_prompt[0, t * 128:(t + 1) * 128, :], yout[:, t, :]).then_inc(stored, 16)
                else:
                    sp.dma_start(y_sample.rearrange("n q d -> (n q) d"), yout[0:NS, t, :]).then_inc(stored, 16)
                n_stored += 1
            sp.wait_ge(q["state_stored"], 16 * (NB + 1))
            sp.wait_ge(stored, 16 * n_stored)

        @block.gpsimd
        def _(pool):
            steps = Steps(pool, pool_step)
            pool.memset(prow, 0.0).then_inc(prow_clear, 1)
            steps(pool.memset(ident[:], 0.0))
            steps(pool.memset(causal[:], 0.0))
            pool.memset(mean_w[:], 1.0 / D).then_inc(const_ready, 1)
            pool.memset(eps[:], EPS).then_inc(const_ready, 1)
            pool.memset(wbd[:, 1], 0.0).then_inc(q["zeros_ready"], 1)
            for tile in hid:
                pool.memset(tile, 0.0).then_inc(q["zeros_ready"], 1)
            for tile in (qbd, win_mask):
                pool.memset(tile[:], 0.0)
            pool.memset(new_mask[:], NEG)
            steps(pool.memset(blk_neg[:], 0.0))
            steps(pool.memset(blk_ok[:], 1.0))
            steps(pool.memset(diag[:], 1.0))
            steps.settle()
            pool.affine_select(out=ident[:], in_=ident[:], compare_op=ALU.not_equal, fill=1.0, base=0,
                               pattern=[[-1, 128]], channel_multiplier=1).then_inc(const_ready, 1)
            pool.affine_select(out=causal[:], in_=causal[:], compare_op=ALU.is_ge, fill=NEG, base=0,
                               pattern=[[-1, 128]], channel_multiplier=1).then_inc(const_ready, 1)
            pool.wait_ge(const_ready, 4)
            pool.tensor_copy(identb[:], ident[:]).then_inc(const_ready, 1)
            for tile, fill in ((blk_neg, NEG), (blk_ok, 0.0)):
                pool.affine_select(out=tile[:], in_=tile[:], compare_op=ALU.is_ge, fill=fill, base=1 - BLK,
                                   pattern=[[128, QT], [-BLK, 2], [-PAGE, QT]], channel_multiplier=1)
            steps(pool.affine_select(out=diag[:], in_=diag[:], compare_op=ALU.is_ge, fill=0.0, base=0,
                                     pattern=[[-8, R], [-8 * R, G]], channel_multiplier=1))
            steps.settle()
            pool.affine_select(out=diag[:], in_=diag[:], compare_op=ALU.is_ge, fill=0.0, base=7,
                               pattern=[[8, R], [8 * R, G]], channel_multiplier=-1).then_inc(const_ready, 1)
            for n in range(2):
                for k in range(KC):
                    pool.wait_ge(norm_lo, n * KC + k + 1)
                    pool.tensor_scalar(x[:, k, :], x[:, k, :], ALPHA, None, ALU.mult).then_inc(q["residual"], 1)

        @block.tensor
        def _(pe):
            def product(out, hi, lo, xhi, xlo, chunks, parts=None):
                last = None
                for k in range(chunks):
                    if parts is not None:
                        pe.wait_ge(norm_lo, parts + k + 1)
                    for a, b in ((hi, xhi), (hi, xlo), (lo, xhi)):
                        for h in range(2):
                            last = nc.tensor.matmul(
                                out[:, h, 0:HALF], a[:, k, :], b[:, k, h * HALF:(h + 1) * HALF],
                                start=(k == 0 and a is hi and b is xhi),
                                stop=(k == chunks - 1 and a is lo))
                return last

            pe.wait_ge(const_ready, 5)
            pe.wait_ge(dma_par, 16 * 12)
            nc.tensor.transpose(ps[:, 7, 0:128], prow, ident[:]).then_inc(par_in_psum, 1)
            pe.wait_ge(dma_x, 32)
            for k in range(KC):
                if k == 3:
                    pe.wait_ge(par_ready, 1)
                if k >= 4:
                    pe.wait_ge((q["x_by_act"], q["x_by_dve"])[k % 2], (k - 4) // 2 + 1)
                b = 2 * (k % 4)
                for t in range(QT):
                    nc.tensor.transpose(ps[:, b, t * 128:(t + 1) * 128], xin[:, t, k * 128:(k + 1) * 128], ident[:])
                nc.tensor.transpose(ps[:, b + 1, 0:NS], xin_s[:, k * 128:(k + 1) * 128],
                                    ident[0:NS, 0:NS]).then_inc(xt_in_psum, 1)

            def hidden(src, w, out_bank, wide):
                for d in range(HD):
                    for c in range(2):
                        for h in range(2):
                            last = nc.tensor.matmul(ps[c * HD:(c + 1) * HD, out_bank + h, 0:wide],
                                                    w[h * BLK:(h + 1) * BLK, c, d, :], src(h, c, d),
                                                    start=(d == 0), stop=(d == HD - 1))
                return last

            def hidden_cached(g):
                if g >= 2:
                    pe.wait_ge(q["hid_ready"], g - 1)
                pe.wait_ge(q[f"dma_cpage{g % 2}"], sum(len(PARTS[k]) for k in range(g % 2, g + 1, 2)) * UP * 16)
                for d in range(HD):
                    for c in range(2):
                        col = c * 128 + d
                        last = nc.tensor.matmul(
                            ps[:, 2 * (g % 2) + c, 0:len(PARTS[g]) * UP * G], wbd[:, c, d, :, :].rearrange("p a h -> p (a h)"),
                            cpages[g][:, :, col:col + HD + 1:HD], start=(d == 0), stop=(d == HD - 1))
                last.then_inc(q["hid_in_psum"], 1)

            def compressed(p):
                pe.wait_ge(q["hid_ready"], p + 1)
                if p >= 2:
                    pe.wait_ge(q["kc_ready"], p - 1)
                for g in range(G):
                    nc.tensor.matmul(ps[g * HD:(g + 1) * HD, 4 + p % 2, 0:32 * len(PARTS[p])], w2[:, 0, :],
                                     hid[p % 2][:, 0, g, 0:len(PARTS[p]), :].rearrange("p u b -> p (u b)"), start=True, stop=True)
                for k, part in enumerate(PARTS[p]):
                    rows = slice(part % 2 * 32, part % 2 * 32 + 32)
                    for g in range(G):
                        last = nc.tensor.matmul(ps[rows, 6 + p % 2, k * 128 + g * HD:k * 128 + (g + 1) * HD],
                                                hid[p % 2][:, 1, g, k, :], w2[:, 1, :], start=True, stop=True)
                last.then_inc(q["kc_in_psum"], 1)

            def ffn_products(n):
                uses = USES[("ffa", "ffb")[n]]
                for half in range(2):
                    before = n * FT + half * FH

                    def tile(i, parts=None):
                        for s, (done, bank) in enumerate(((sg_ready, 0), (ht_ready, 2))):
                            pe.wait_ge(w_lo[s], i + (uses[s] + half * FH + 1))
                            if parts is None:
                                pe.wait_ge(done, i + before)
                            product(ps[:, bank:bank + 2, :], ghi[s], glo[s], xh, xl, KC, parts if s == 0 else None
                                    ).then_inc(w_used[s], 1)

                    first = n == 1 and half == 0
                    if first:
                        pe.wait_ge(std_ready, 4)
                        tile(0, KC)
                    with pe.Fori(int(first), FH) as i:
                        tile(i)
                    pe.wait_ge(hl_ready, before + FH)
                    with pe.Fori(0, KC // 2) as i:
                        for s in range(2):
                            use = (2 * n + half) * (KC // 2)
                            pe.wait_ge(d_lo[s], i + (use + 1))
                            pe.wait_ge(y_added[s], i + use)
                            product(ps[:, 4 + 2 * s:6 + 2 * s, :], dhi[s], dlo[s], hh, hl, FH
                                    ).then_inc(d_used[s], 1)

            def norm_products(n):
                pe.wait_ge(csum_step, (KC + 1) * (n + 1))
                for h in range(2):
                    nc.tensor.matmul(ps[:, h, 0:HALF], mean_w[:], csum[:, h * HALF:(h + 1) * HALF],
                                     start=True, stop=True).then_inc(mean_ready, 1)
                for h in range(2):
                    for k in range(KC):
                        if k % 4 == 0:
                            pe.wait_ge(sq_ready, 4 * n + 2 * h + k // 4 + 1)
                        last = nc.tensor.matmul(ps[:, 2 + h, 0:HALF], mean_w[:], sq[:, k, h * HALF:(h + 1) * HALF],
                                                start=(k == 0), stop=(k == KC - 1))
                    last.then_inc(var_ready, 1)

            pe.wait_ge(q["dma_first"], 16 * 5)
            pe.wait_ge(q["x_by_act"], KC // 2)
            pe.wait_ge(q["x_by_dve"], KC // 2)
            pe.wait_ge(q["pe_summed"], 1)
            for c in range(2):
                for h in range(2):
                    rows = slice(h * HD, (h + 1) * HD)
                    last = nc.tensor.matmul(ps[rows, 7, c:c + 1], pe_sum[rows, c, :], mean_w[rows, 0:1],
                                            start=True, stop=True)
            last.then_inc(q["bias_in_psum"], 1)
            pe.wait_ge(q["wbd_by_act"], 1)
            pe.wait_ge(q["wbd_by_dve"], 1)
            hidden_cached(0)
            pe.wait_ge(q["bias_ready"], 1)
            for g in range(1, GROUPS):
                hidden_cached(g)
                compressed(g - 1)
            compressed(GROUPS - 1)
            pe.wait_ge(q["x_lo"], KC // 2)
            pe.wait_ge(q["kc_ready"], GROUPS)
            ffn_products(0)
            norm_products(0)

            pe.wait_ge(std_ready, 2)
            for s in range(2):
                pe.wait_ge(w_lo[s], USES["proj"][s] + 1)
                product(ps[:, 2 * s:2 * s + 2, :], ghi[s], glo[s], xh, xl, KC, 0 if s == 0 else None
                        ).then_inc(w_used[s], 1)
            with pe.Fori(1, NT // 2) as i:
                for s in range(2):
                    pe.wait_ge(w_lo[s], i + (USES["proj"][s] + 1))
                    pe.wait_ge(z_out[s], i)
                    product(ps[:, 2 * s:2 * s + 2, :], ghi[s], glo[s], xh, xl, KC).then_inc(w_used[s], 1)
            pe.wait_ge(w_lo[0], USES["proj"][0] + NT // 2 + 1)
            pe.wait_ge(z_out[0], NT // 2)
            product(ps[:, 0:2, :], ghi[0], glo[0], xh, xl, KC).then_inc(w_used[0], 1)

            pe.wait_ge(z_out[0], NT // 2 + 1)
            pe.wait_ge(z_out[1], NT // 2)
            for t in range(QT + 1):
                if t >= 2:
                    pe.wait_ge(tok_out, t - 1)
                w = 128 if t < QT else NS
                for j in range(6):
                    last = nc.tensor.transpose(ps[0:w, 4 + 2 * (t % 2) + j // 4, (j % 4) * 128:(j % 4 + 1) * 128],
                                               zr[:, KV0 + j, t * 128:t * 128 + w], ident[:])
                last.then_inc(tok_in_psum, 1)

            pe.wait_ge(q["qbd_ready"], 1)
            pe.wait_ge(q["masks_ready"], 1)
            for n in range(NB):
                last = nc.tensor.matmul(ps[32 * (n % 4):32 * (n % 4) + 32, 0, n // 4 * NBLK:(n // 4 + 1) * NBLK],
                                        qbd[:, n, :], kc_all[:, n, :], start=True, stop=True)
            last.then_inc(q["scmp_in_psum"], 1)
            for br in range(2):
                for nh in range(2):
                    out = ps[:, 1, (2 * br + nh) * NS:(2 * br + nh + 1) * NS]
                    nc.tensor.matmul(out, qbd[:, 4 * nh:4 * nh + 4, :].rearrange("p n r -> p (n r)"),
                                     zr[:, KV0 + 2 + 2 * br, SEQ:T], start=True, stop=False)
                    last = nc.tensor.matmul(out, identb[:], new_mask[:, nh, :], start=False, stop=True)
            last.then_inc(q["snew_in_psum"], 1)
            for k in range(BR * R):
                br, r = k // R, k % R
                nc.tensor.matmul(ps[:, 2, k * NS:(k + 1) * NS], gate_sel[k // 8][:, k % 8, :],
                                 zr[0:BR * NH, G0, SEQ:T], start=True, stop=True)
            for t in range(QT):
                nc.tensor.transpose(ps[:, 3, t * 32:t * 32 + BR * NH], zr[0:BR * NH, G0, t * 128:(t + 1) * 128],
                                    ident[0:BR * NH, 0:BR * NH])
            pe.wait_ge(q["dma_conv"], 16)
            for t in range(4):
                last = nc.tensor.transpose(ps[:, 3, 128 + t * 16:144 + t * 16], crow[:, t * 128:(t + 1) * 128],
                                           ident[0:16, 0:16])
            last.then_inc(q["gates_in_psum"], 1)

            pe.wait_ge(q["dma_w1p"], 16 * 4)
            pe.wait_ge(tok_out, QT + 1)
            hidden(lambda h, c, d: kvtok[h * BLK:(h + 1) * BLK, 0:QT, c, :].rearrange(
                "p a (g d) -> p a g d", g=G)[:, :, :, d], w1p, 6, QT * G).then_inc(q["hidp_in_psum"], 1)

            pe.wait_ge(q["pcs_ready"], 1)
            nc.tensor.matmul(ps[:, 4, 0:128], same[:], pcs[:].rearrange("p n b -> p (n b)"), start=True, stop=True)
            for nh in range(2):
                last = nc.tensor.transpose(ps[0:NBLK, 5, nh * 128:(nh + 1) * 128], pcs[:, nh, :], ident[:])
            last.then_inc(q["imp_in_psum"], 1)

            pe.wait_ge(q["hidp_ready"], 1)
            for g in range(G):
                nc.tensor.matmul(ps[g * HD:(g + 1) * HD, 6, 0:8], w2[0:HD, 0, :], hidp[0:HD, :, :, g],
                                 start=True, stop=True)
            for g in range(G):
                last = nc.tensor.matmul(ps[0:8, 7, g * HD:(g + 1) * HD],
                                        hidp[HD:128, :, :, g].rearrange("p h a -> p (h a)"), w2[HD:128, 1, :],
                                        start=True, stop=True)
            last.then_inc(q["kcp_in_psum"], 1)

            pe.wait_ge(q["pct_ready"], 1)
            for n in range(NB):
                last = nc.tensor.matmul(ps[32 * (n % 4):32 * (n % 4) + 32, 0, n // 4 * 128:(n // 4 + 1) * 128],
                                        pct[:, n // 4, 32 * (n % 4):32 * (n % 4) + 32], vc_all[:, n, :],
                                        start=True, stop=True)
            last.then_inc(q["ocs_in_psum"], 1)

            pe.wait_ge(q["pnew_ready"], 1)
            for k in range(4):
                last = nc.tensor.transpose(ps[0:NS, 1, k * 128:(k + 1) * 128], pnew[:, k, :], ident[:])
            last.then_inc(q["pnewt_in_psum"], 1)

            pe.wait_ge(q["sel_ready"], 1)
            for n in range(NB):
                for c in range(CH):
                    last = nc.tensor.matmul(ps[32 * c:32 * c + 32, 5, n * 16:(n + 1) * 16],
                                            identb[:, 32 * (n % 4):32 * (n % 4) + 32],
                                            selneg[:, n // 4, c * 16:(c + 1) * 16], start=True, stop=True)
            last.then_inc(q["selt_in_psum"], 1)

            pe.wait_ge(q["kcp_ready"], 1)
            nc.tensor.matmul(ps[0:64, 7, 0:128], rep8[:].rearrange("p x b -> p (x b)"), vcp[:],
                             start=True, stop=True).then_inc(q["rep_in_psum"], 1)
            pe.wait_ge(q["gates_ready"], 1)
            for g in range(G):
                for t in range(QT):
                    for r in range(R):
                        last = nc.tensor.matmul(ps[:, 2 + g, (t * R + r) * 8:(t * R + r + 1) * 8],
                                                zr[g * HD:(g + 1) * HD, r, t * 128:(t + 1) * 128],
                                                kcp[g * HD:(g + 1) * HD, :], start=True, stop=True)
            last.then_inc(q["sp_in_psum"], 1)

            pe.wait_ge(q["pnewt_ready"], 1)
            for k in range(4):
                last = nc.tensor.matmul(ps[:, 4, k * 128:(k + 1) * 128], pnt[:, k, :],
                                        kvtok[0:NS, QT, 3 + 2 * (k // 2), :], start=True, stop=True)
            last.then_inc(q["onew_in_psum"], 1)

            pe.wait_ge(q["pp_ready"], 1)
            for t in range(QT):
                last = nc.tensor.transpose(ps[0:64, 6, t * 128:(t + 1) * 128], pp[0][:, t * 64:(t + 1) * 64], ident[:])
            last.then_inc(q["ptp_in_psum"], 1)
            pe.wait_ge(q["ptp_ready"], 1)
            pe.wait_ge(q["vbd_ready"], 1)
            pe.wait_ge(q["ocs_ready"], 1)
            for t in range(QT):
                last = nc.tensor.matmul(ps[:, t, :], ptp[:, t, :], vbd[:].rearrange("p r g d -> p (r g d)"),
                                        start=True, stop=True)
            last.then_inc(q["op_in_psum"], 1)
            pe.wait_ge(q["u_ready"], 1)
            pe.wait_ge(q["selt_ready"], 1)
            for k, c0 in enumerate((SEQ - NS, SEQ)):
                for t in range(4):
                    last = nc.tensor.transpose(ps[0:NS, 5 + 2 * k, t * 128:(t + 1) * 128],
                                               zc[:, 4 + t, c0:c0 + NS], ident[:])
            last.then_inc(q["ctok_in_psum"], 1)

            units = [(br, t, g) for br in range(2) for t in range(QT) for g in range(G)]
            U = len(units)
            for name in ("op_ready", "ctok_ready", "onew_ready", "conv_ready"):
                pe.wait_ge(q[name], 1)
            def prompt_head(r):
                pe.wait_ge(q["qs_ready"], r + 1)
                for j in range(U + 3):
                    if j < U:
                        br, t, g = units[j]
                        gp = slice(g * HD, (g + 1) * HD)
                        if j >= 3:
                            pe.wait_ge(q["probs"], r * U + (j - 2))
                        nc.tensor.matmul(ps[:, j % 3, 0:(t + 1) * 128], qs[gp, t * 128:(t + 1) * 128],
                                         zr[gp, KV0 + 2 + 2 * br, 0:(t + 1) * 128], start=True, stop=True)
                        nc.tensor.matmul(ps[:, j % 3, t * 128:(t + 1) * 128], identb[:], causal[:],
                                         start=False, stop=True, skip_group_check=True).then_inc(q["scores"], 1)
                    if 2 <= j < U + 2:
                        k = j - 2
                        br, t, g = units[k]
                        pe.wait_ge(q["probs"], r * U + (k + 1))
                        if k >= 2:
                            pe.wait_ge(q["pt_copied"], r * U + (k - 1))
                        for m in range(t + 1):
                            last = nc.tensor.transpose(ps[:, 3 + k % 2, m * 128:(m + 1) * 128],
                                                       pp[k % 2][:, m * 128:(m + 1) * 128], ident[:])
                        last.then_inc(q["probs_t"], 1)
                    if j >= 3:
                        k = j - 3
                        br, t, g = units[k]
                        pe.wait_ge(q["pt_copied"], r * U + (k + 1))
                        if k >= 2:
                            pe.wait_ge(q["o_added"], r * U + (k - 1))
                        for m in range(t + 1):
                            last = nc.tensor.matmul(ps[:, 5 + k % 2, 0:HD], ppt[k % 2][:, m * 128:(m + 1) * 128],
                                                    kvtok[:, m, 3 + 2 * br, g * HD:(g + 1) * HD],
                                                    start=(m == 0), stop=(m == t))
                        last.then_inc(q["pv"], 1)

            def keys_t(b, i, n):
                pe.wait_ge(q[f"dma_page{b}"], (i + 1) * (NPG * 16))
                pe.wait_ge(q[f"dma_win{b}"], (i + 1) * 16)
                for m in range(9):
                    if m % 2 == 0:
                        pe.wait_ge(q["kt_by_act"], n * 5 + m // 2)
                    else:
                        pe.wait_ge(q["kt_by_dve"], n * 4 + m // 2)
                    for k in range(4):
                        src = pages[b][:, 4 * m + k, 0:128] if m < 8 else win[b][:, k, 0:128]
                        last = nc.tensor.transpose(ps[:, m % 2, k * 128:(k + 1) * 128], src, ident[:])
                    last.then_inc(q["kt_in_psum"], 1)

            def scores_s(b, n):
                pe.wait_ge(q["kt_by_act"], n * 5 + 5)
                pe.wait_ge(q["kt_by_dve"], n * 4 + 4)
                pe.wait_ge(q["qn_ready"], n + 1)
                pe.wait_ge(q["s_probs"], n)
                for h in range(2):
                    nc.tensor.matmul(ps[:, 2 + h, :], identb[:],
                                     selt[:, DS(n, 1), h * 8:(h + 1) * 8].rearrange("p o (k u) -> p (o k) u", u=1)
                                     .broadcast_to([128, 8, BLK]), start=True, stop=True, skip_group_check=True)
                nc.tensor.matmul(ps[:, 4, 0:128], identb[:], win_mask[:], start=True, stop=True,
                                 skip_group_check=True)
                for h in range(2):
                    for c in range(CH):
                        nc.tensor.matmul(ps[32 * c:32 * c + 32, 2 + h, :], qn[b][:],
                                         kt[:, c * 8 + h * 4:c * 8 + h * 4 + 4, :].rearrange("p k t -> p (k t)"),
                                         start=False, stop=True, skip_group_check=True)
                for c in range(CH):
                    last = nc.tensor.matmul(ps[32 * c:32 * c + 32, 4, 0:128], qn[b][:], kt[:, NPG + c, :],
                                            start=False, stop=True, skip_group_check=True)
                last.then_inc(q["s_scores"], 1)

            def values_s(b, n):
                pe.wait_ge(q["s_probs"], n + 1)
                pe.wait_ge(q["s_o"], n)
                pe.wait_ge(q["s_pt_act"], n)
                pe.wait_ge(q["s_pt_dve"], n)
                for k in range(PC + 1):
                    last = nc.tensor.transpose(ps[:, 5 + k // 4, k % 4 * 128 if k < 8 else 256:(k % 4 * 128 if k < 8 else 256) + 128],
                                               pw[:, k, :], ident[:])
                last.then_inc(q["s_probs_t"], 1)
                pe.wait_ge(q["s_pt_act"], n + 1)
                pe.wait_ge(q["s_pt_dve"], n + 1)
                for k in range(PC):
                    for c in range(CH):
                        nc.tensor.matmul(ps[32 * c:32 * c + 32, 7, 0:128], pwt[:, k, 32 * c:32 * c + 32],
                                         pages[b][:, c * PC + k, 128:256], start=(k == 0), stop=(k == PC - 1))
                for c in range(CH):
                    last = nc.tensor.matmul(ps[32 * c:32 * c + 32, 7, 128:256], pwt[:, PC, 32 * c:32 * c + 32],
                                            win[b][:, c, 128:256], start=True, stop=True)
                last.then_inc(q[f"s_pv{b}"], 1)

            with pe.Fori(0, R) as r:
                prompt_head(r)
                keys_t(0, r, r * 2)
                scores_s(0, r * 2)
                pe.wait_ge(q["o_added"], (r + 1) * U)
                keys_t(1, r, r * 2 + 1)
                values_s(0, r * 2)
                scores_s(1, r * 2 + 1)
                values_s(1, r * 2 + 1)

            pe.wait_ge(q["s_o"], NB)
            nc.tensor.transpose(ps[0:16, 0, 0:128], cb[:, :, :, OB - 1].rearrange("p n b -> p (n b)"), ident[:]
                                ).then_inc(q["m_in_psum"], 1)
            pe.wait_ge(q["m_ready"], 1)
            nc.tensor.transpose(ps[:, 1, 0:16], neg_rep[:].rearrange("p c r -> p (c r)"), ident[0:16, 0:16]
                                ).then_inc(q["mb_in_psum"], 1)
            pe.wait_ge(q["cb_scaled"], 1)
            for n in range(NB):
                last = nc.tensor.matmul(ps[32 * (n % 4):32 * (n % 4) + 32, 2 + n // 4, 0:2 * OB], fold[:],
                                        cb[:, n, :, :].rearrange("p b o -> p (b o)"), start=True, stop=True)
            last.then_inc(q["comb_in_psum"], 1)
            pe.wait_ge(q["ofin_ready"], 1)
            for nh in range(2):
                nc.tensor.transpose(ps[:, 4, nh * 128:(nh + 1) * 128], ocs[:, nh, :], ident[:])
                for br in range(2):
                    last = nc.tensor.transpose(ps[:, 5 + br, nh * 128:(nh + 1) * 128], ofin[:, nh, br, :], ident[:])
            last.then_inc(q["ofin_in_psum"], 1)
            pe.wait_ge(q["mb_in_psum"], 1)
            for r in range(R):
                if r >= 2:
                    pe.wait_ge(q["at_lo"], r - 1)
                for t in range(QT):
                    last = nc.tensor.transpose(ps[:, r % 2, t * 128:(t + 1) * 128], po[:, t, r, :], ident[:])
                last.then_inc(q["pt_in_psum"], 1)

            pe.wait_ge(q["at_lo"], R + 1)
            for t in range(KC):
                s = t % 2
                pe.wait_ge(w_lo[s], USES["out"][s] + t // 2 + 1)
                if t >= 2:
                    pe.wait_ge(q["out_added"], t - 1)
                product(ps[:, 2 * s:2 * s + 2, :], ghi[s], glo[s], xh, xl, KC).then_inc(w_used[s], 1)
            norm_products(1)
            ffn_products(1)
            norm_products(2)
            for t in range(QT + 1):
                if t in (0, HALF // 128):
                    pe.wait_ge(normed, (3 + (t > 0)) * KC)
                if t >= 2:
                    pe.wait_ge(q["y_by_act"], t - 1)
                    pe.wait_ge(q["y_by_dve"], t - 1)
                w = 128 if t < QT else NS
                for k in range(KC):
                    last = nc.tensor.transpose(ps[0:w, 4 + 2 * (t % 2) + k // 4, k % 4 * 128:(k % 4 + 1) * 128],
                                               x[:, k, t * 128:t * 128 + w], ident[:])
                last.then_inc(q["y_in_psum"], 1)

        @block.scalar
        def _(act):
            def split_w(s, use, fills):
                act.wait_ge(dma_w[s], fills)
                act.wait_ge(w_used[s], use)
                act.activation(ghi[s][:], graw[s][:], ACT.Copy).then_inc(w_hi[s], 1)

            def split_d(s, use):
                act.wait_ge(dma_d[s], use * 16 + 16)
                act.wait_ge(d_used[s], use)
                act.activation(dhi[s][:], draw[s][:], ACT.Copy).then_inc(d_hi[s], 1)

            for k in range(0, KC, 2):
                act.wait_ge(xt_in_psum, k + 1)
                b = 2 * (k % 4)
                act.activation(x[:, k, 0:SEQ], ps[:, b, :], ACT.Copy)
                act.activation(x[:, k, SEQ:T], ps[:, b + 1, 0:NS], ACT.Copy).then_inc(q["x_by_act"], 1)
            act.wait_ge(q["dma_cmp_w"], 16 * 4)
            act.wait_ge(q["zeros_ready"], 4)
            act.activation(wbd[BLK:128, :, :, 1, :], w1[BLK:128], ACT.Copy).then_inc(q["wbd_by_act"], 1)

            def ffn_gates(n):
                phase = ("ffa", "ffb")[n]
                uses, fills = USES[phase], FILLS[phase]
                for half in range(2):
                    before = n * FT + half * FH

                    def copy_h(j):
                        act.wait_ge(ht_ready, j + (before + 1))
                        act.activation(hh[:, DS(j, 1), :], ht[:], ACT.Copy).then_inc(hh_ready, 1)

                    def tile(i, first):
                        if not (first and n == 1 and half == 0):
                            split_w(0, i + (uses[0] + half * FH), (i + (fills[0] + half * FH + 1)) * 16)
                            if not first:
                                copy_h(i - 1)
                            split_w(1, i + (uses[1] + half * FH), (i + (fills[1] + half * FH + 1)) * 16)
                        act.wait_ge(w_used[0], i + (uses[0] + half * FH + 1))
                        act.wait_ge(ht_ready, i + before)
                        act.activation(sg[:].rearrange("p (h t) -> p h t", h=2), ps[:, 0:2, 0:HALF], ACT.Silu
                                       ).then_inc(sg_ready, 1)

                    tile(0, True)
                    with act.Fori(1, FH) as i:
                        tile(i, False)
                    use = (2 * n + half) * (KC // 2)
                    split_d(0, use)
                    copy_h(FH - 1)
                    with act.Fori(0, KC // 2 - 1) as i:
                        split_d(1, i + use)
                        split_d(0, i + (use + 1))
                    split_d(1, use + KC // 2 - 1)

            def norm_scale(n):
                for h in range(2):
                    hs = slice(h * HALF, (h + 1) * HALF)
                    for k in range(0, KC, 4):
                        act.wait_ge(centered, 4 * n + 2 * h + k // 4 + 1)
                        act.activation(sq[:, k:k + 4, hs], x[:, k:k + 4, hs], ACT.Square).then_inc(sq_ready, 1)
                for s in ((0,), (0, 1), ())[n]:
                    phase = ("proj", "ffb")[n]
                    split_w(s, USES[phase][s], (FILLS[phase][s] + PER_FILL[phase]) * 16)
                for h in range(2):
                    hs = slice(h * HALF, (h + 1) * HALF)
                    act.wait_ge(var_ready, 2 * n + h + 1)
                    act.activation(rstd[:, hs], ps[:, 2 + h, 0:HALF], ACT.Sqrt, bias=eps[:]).then_inc(std_ready, 1)
                g, b = R_LN + 16 * n, R_LN + 16 * n + 8
                affine = lambda out, part, k: act.activation(out, part, ACT.Identity, scale=par[:, g + k:g + k + 1],
                                                             bias=par[:, b + k:b + k + 1])
                if n < 2:
                    for k in range(KC):
                        act.wait_ge(scaled, KC * n + k + 1)
                        affine(xh[:, k, :], x[:, k, :], k).then_inc(norm_hi, 1)
                        affine(x[:, k, :], x[:, k, :], k).then_inc(normed, 1)
                else:
                    for h in range(2):
                        for k in range(KC):
                            if k % 4 == 0:
                                act.wait_ge(scaled, KC * n + 2 * h + k // 4 + 1)
                            part = x[:, k, h * HALF:(h + 1) * HALF]
                            affine(part, part, k).then_inc(normed, 1)

            steps = Steps(act, act_step)
            act.wait_ge(par_ready, 1)
            act.wait_ge(q["bias_ready"], 1)
            for p in range(GROUPS):
                act.wait_ge(q["hid_in_psum"], p + 1)
                if p >= 2:
                    act.wait_ge(q["kc_in_psum"], p - 1)
                for c in range(2):
                    for h in range(2):
                        rows = slice(h * HD, (h + 1) * HD)
                        for g in range(G):
                            last = act.activation(
                                hid[p % 2][rows, c, g, 0:len(PARTS[p]), h * UP:(h + 1) * UP],
                                ps[rows, 2 * (p % 2) + c, 0:32 * len(PARTS[p])].rearrange("p (u a g) -> p g u a", a=UP, g=G)[:, g],
                                ACT.Silu, bias=hid_bias[rows, c:c + 1])
                last.then_inc(q["hid_ready"], 1)
                if p == GROUPS - 2:
                    act.wait_ge(q["x_by_dve"], KC // 2)
                    for k in range(0, KC, 2):
                        act.activation(xh[:, k:k + 2, :], x[:, k:k + 2, :], ACT.Copy).then_inc(q["x_hi"], 1)
            act.wait_ge(q["kc_in_psum"], GROUPS)
            ffn_gates(0)
            norm_scale(0)

            def z_tile(t, s, i):
                split_w(s, i + USES["proj"][s], (i * 2 + (FILLS["proj"][s] + 2)) * 16)

            def z_split(s, i):
                split_w(s, i + USES["proj"][s], (i * 2 + (FILLS["proj"][s] + 2)) * 16)

            def z_result(dst, col, s, i, func=ACT.Identity):
                act.wait_ge(w_used[s], i + (USES["proj"][s] + 1))
                act.activation(dst.rearrange("p o (h t) -> p (o h) t", h=2), ps[:, 2 * s:2 * s + 2, 0:HALF], func,
                               bias=par[:, DS(col, 1)]).then_inc(z_out[s], 1)

            with act.Fori(0, ZC // 2) as i:
                z_split(1, i)
                z_result(zc[:, DS(i * 2, 1), :], i * 2 + R_BC, 0, i)
                z_split(0, i + 1)
                z_result(zc[:, DS(i * 2 + 1, 1), :], i * 2 + (R_BC + 1), 1, i)
            with act.Fori(ZC // 2, NT // 2) as i:
                z_split(1, i)
                z_result(zr[:, DS(i * 2 - ZC, 1), :], i * 2 + R_BC, 0, i)
                z_split(0, i + 1)
                z_result(zr[:, DS(i * 2 - (ZC - 1), 1), :], i * 2 + (R_BC + 1), 1, i)
            z_result(zr[:, G0:G0 + 1, :], R_BG, 0, NT // 2, ACT.Sigmoid)

            act.wait_ge(q["ncm_ready"], 1)
            for nh in range(2):
                last = act.activation(pcs[:, nh, :], ps[:, 0, nh * NBLK:(nh + 1) * NBLK], ACT.Exp,
                                      bias=small[:, C_NCM + nh:C_NCM + nh + 1],
                                      accum_out=small[:, C_CSUM + nh:C_CSUM + nh + 1])
            last.then_inc(q["ecmp_ready"], 1)
            act.wait_ge(q["nnm_ready"], 1)
            for k in range(4):
                last = act.activation(pnew[:, k, :], ps[:, 1, k * NS:(k + 1) * NS], ACT.Exp,
                                      bias=small[:, C_NNM + k:C_NNM + k + 1],
                                      accum_out=small[:, C_NSUM + k:C_NSUM + k + 1])
            last.then_inc(q["pnew_ready"], 1)
            act.wait_ge(q["hidp_in_psum"], 1)
            act.activation(hidp[:].rearrange("p h a g -> p h (a g)"), ps[:, 6:8, 0:QT * G], ACT.Silu,
                           bias=hid_bias[:, 2:3]).then_inc(q["hidp_ready"], 1)
            act.wait_ge(q["sp_shifted"], 1)
            act.activation(pp[0][:, 0:256], pp[0][:, 0:256], ACT.Exp).then_inc(q["ep_ready"], 1)
            act.wait_ge(q["op_in_psum"], 1)
            act.activation(po[:].rearrange("p t r d -> p t (r d)"), ps[:, 0:4, :], ACT.Copy).then_inc(q["op_ready"], 1)

            units = [(br, t, g) for br in range(2) for t in range(QT) for g in range(G)]
            U = len(units)
            def prompt_head(r):
                act.wait_ge(q["o_added"], r * U)
                act.wait_ge(q["s_pv0"], r)
                act.wait_ge(q["s_pv1"], r)
                for j in range(U + 2):
                    if j < U:
                        br, t, g = units[j]
                        act.wait_ge(q["negmax"], r * U + (j + 1))
                        act.wait_ge(q["probs_t"], r * U + max(j - 1, 0))
                        act.activation(pp[j % 2][:, 0:(t + 1) * 128], ps[:, j % 3, 0:(t + 1) * 128], ACT.Exp,
                                       bias=small[:, C_PNM + j:C_PNM + j + 1],
                                       accum_out=small[:, C_PSUM + j:C_PSUM + j + 1]).then_inc(q["probs"], 1)
                    if j >= 2:
                        k = j - 2
                        br, t, g = units[k]
                        act.wait_ge(q["probs_t"], r * U + (k + 1))
                        act.wait_ge(q["pv"], r * U + max(k - 1, 0))
                        act.activation(ppt[k % 2][:, 0:(t + 1) * 128], ps[:, 3 + k % 2, 0:(t + 1) * 128], ACT.Copy
                                       ).then_inc(q["pt_copied"], 1)

            def keys_s(n):
                for m in range(0, 9, 2):
                    act.wait_ge(q["kt_in_psum"], n * 9 + (m + 1))
                    if m == 0:
                        act.wait_ge(q["s_scores"], n)
                    act.activation(kt[:, 4 * m:4 * m + 4, :].rearrange("p k t -> p (k t)"), ps[:, 0, :], ACT.Copy
                                   ).then_inc(q["kt_by_act"], 1)

            def probs_s(b, n):
                act.wait_ge(q["s_negmax"], n + 1)
                act.wait_ge(q["s_probs_t"], n)
                act.activation(pw[:, 0:PC, :].rearrange("p k t -> p (k t)"), ps[:, 2:4, :].rearrange("p b t -> p (b t)"),
                               ACT.Exp, bias=cb[:, DS(n, 1), 0, OB - 1], accum_out=cb[:, DS(n, 1), 0, OB - 2])
                act.activation(pw[:, PC, :], ps[:, 4, 0:128], ACT.Exp, bias=cb[:, DS(n, 1), 1, OB - 1],
                               accum_out=cb[:, DS(n, 1), 1, OB - 2]).then_inc(q["s_probs"], 1)

            def probs_t_s(b, i, n):
                act.wait_ge(q["s_probs_t"], n + 1)
                act.activation(pwt[:, 4:8, :].rearrange("p k t -> p (k t)"), ps[:, 6, :], ACT.Copy)
                act.activation(pwt[:, 8, :], ps[:, 7, 256:384], ACT.Copy).then_inc(q["s_pt_act"], 1)

            act.wait_ge(q["state_stored"], 16 * (NB + 1))
            with act.Fori(0, R) as r:
                prompt_head(r)
                act.wait_ge(q["pv"], (r + 1) * U)
                keys_s(r * 2)
                probs_s(0, r * 2)
                keys_s(r * 2 + 1)
                probs_t_s(0, r, r * 2)
                probs_s(1, r * 2 + 1)
                probs_t_s(1, r, r * 2 + 1)

            act.wait_ge(q["mdiff_ready"], 1)
            act.activation(chunk_w[:], chunk_w[:], ACT.Exp).then_inc(q["mw_ready"], 1)
            act.wait_ge(q["diff_ready"], 1)
            act.activation(small[:, C_F:C_F + 8], small[:, C_F:C_F + 8], ACT.Exp).then_inc(q["wts_ready"], 1)

            act.wait_ge(q["os_ready"], 1)
            for r in range(R):
                act.wait_ge(q["pt_in_psum"], r + 1)
                act.activation(xh[:, r, 0:SEQ], ps[:, r % 2, :], ACT.Copy)
                act.activation(xh[:, r, SEQ:T], os_sum[:, r, :, :].rearrange("p n q -> p (n q)"), ACT.Copy
                               ).then_inc(q["at_hi"], 1)
            act.activation(xh[:, R:KC, :], yconv[:], ACT.Copy).then_inc(q["at_hi"], 1)

            for t in range(KC):
                s = t % 2
                split_w(s, USES["out"][s] + t // 2, (FILLS["out"][s] + 3 * (t // 2 + 1)) * 16)
            norm_scale(1)
            ffn_gates(1)
            norm_scale(2)
            for t in range(QT + 1):
                w = 128 if t < QT else NS
                act.wait_ge(q["y_in_psum"], t + 1)
                act.activation(yout[0:w, t, 0:512], ps[0:w, 4 + 2 * (t % 2), :], ACT.Copy).then_inc(q["y_by_act"], 1)

        @block.vector
        def _(dve):
            steps = Steps(dve, dve_step)
            def split_w(s, use):
                dve.wait_ge(w_hi[s], use + 1)
                dve.tensor_tensor(glo[s][:], graw[s][:], ghi[s][:].bitcast(F32), ALU.subtract).then_inc(w_lo[s], 1)

            def split_d(s, use):
                dve.wait_ge(d_hi[s], use + 1)
                dve.tensor_tensor(dlo[s][:], draw[s][:], dhi[s][:].bitcast(F32), ALU.subtract).then_inc(d_lo[s], 1)

            dve.memset(wbd[:, 0], 0.0).then_inc(q["zeros_ready"], 1)
            dve.wait_ge(const_ready, 6)
            F = C_F
            by_head = ident[:].rearrange("p (x r q) -> p x q r", r=R, q=NQ)
            steps(dve.tensor_reduce(small[:, F:F + 32].rearrange("p (x q) -> p x q", q=NQ), by_head, AX, ALU.add))
            dve.tensor_reduce(fold[:], ident[:].rearrange("p (c r) -> p r c", c=CH), AX, ALU.add)
            steps.settle()
            dve.tensor_copy(same[:].rearrange("p (x r q) -> p x r q", r=R, q=NQ),
                            small[:, F:F + 32].rearrange("p (x o q) -> p x o q", o=1, q=NQ).broadcast_to([128, 8, R, NQ]))
            steps(dve.tensor_reduce(small[:, 0:NQ], ident[:, 0:NS].rearrange("p (x q) -> p q x", q=NQ), AX, ALU.add))
            steps(dve.tensor_reduce(small[:, 16:32].rearrange("p (n q) -> p n q", q=NQ),
                                    ident[:].rearrange("p (n x q) -> p n q x", n=4, q=NQ), AX, ALU.add))
            steps.settle()
            for k in range(NQ):
                steps(dve.tensor_reduce(small[:, 4 + k:5 + k], small[:, k:NQ], AX, ALU.add))
                steps(dve.tensor_reduce(small[:, 32:48].rearrange("p (n k) -> p n k", k=NQ)[:, :, k],
                                        small[:, 16:32].rearrange("p (n q) -> p n q", q=NQ)[:, :, k:NQ], AX, ALU.add))
            steps.settle()
            dve.tensor_scalar(win_mask[:, 0:NQ], small[:, 4:8], NEG, None, ALU.mult)
            for nh in range(2):
                last = dve.tensor_scalar(new_mask[:, nh, 16 * nh:16 * nh + 16], small[:, 32:48], -1.0, -NEG,
                                         ALU.add, ALU.mult)
            last.then_inc(q["masks_ready"], 1)

            dve.wait_ge(par_in_psum, 1)
            dve.tensor_copy(par[:], ps[:, 7, 0:96]).then_inc(par_ready, 1)
            for k in range(1, KC, 2):
                dve.wait_ge(xt_in_psum, k + 1)
                b = 2 * (k % 4)
                dve.tensor_copy(x[:, k, 0:SEQ], ps[:, b, :])
                dve.tensor_copy(x[:, k, SEQ:T], ps[:, b + 1, 0:NS]).then_inc(q["x_by_dve"], 1)
            dve.wait_ge(q["dma_cmp_w"], 16 * 4)
            dve.wait_ge(q["zeros_ready"], 4)
            dve.tensor_copy(wbd[0:BLK, :, :, 0, :], w1[0:BLK]).then_inc(q["wbd_by_dve"], 1)
            dve.wait_ge(q["dma_first"], 16 * 5)
            dve.wait_ge(q["wbd_by_dve"], 1)
            dve.wait_ge(q["wbd_by_act"], 1)
            steps(dve.tensor_tensor(w1, w1, pe_sb[:].rearrange("p c (d o) -> p c d o", o=1).broadcast_to(
                [128, 2, HD, HD]), ALU.mult)); steps.settle()
            for c in range(2):
                last = dve.tensor_reduce(pe_sum[:, c, :], w1[:, c].rearrange("p d h -> p h d"), AX, ALU.add)
            last.then_inc(q["pe_summed"], 1)
            dve.wait_ge(q["bias_in_psum"], 1)
            dve.tensor_scalar(hid_bias[:, 0:2], ps[:, 7, 0:2], float(D), None, ALU.mult)
            dve.tensor_scalar(hid_bias[0:HD, 2:3], ps[0:HD, 7, 0:1], float(D), None, ALU.mult)
            dve.tensor_scalar(hid_bias[HD:128, 2:3], ps[HD:128, 7, 1:2], float(D), None, ALU.mult
                              ).then_inc(q["bias_ready"], 1)
            for p in range(GROUPS):
                dve.wait_ge(q["kc_in_psum"], p + 1)
                for k, n in enumerate(PARTS[p]):
                    n, part = divmod(n, 2)
                    rows = slice(part * 32, part * 32 + 32)
                    dve.tensor_copy(kc_all[:, n, rows], ps[:, 4 + p % 2, k * 32:(k + 1) * 32])
                    last = dve.tensor_copy(vc_all[rows, n, :], ps[rows, 6 + p % 2, k * 128:(k + 1) * 128])
                last.then_inc(q["kc_ready"], 1)
                if p == GROUPS - 3:
                    dve.wait_ge(q["x_by_act"], KC // 2)
                    dve.wait_ge(q["x_by_dve"], KC // 2)
                    for j in range(KC // 2):
                        part = slice(2 * j, 2 * j + 2)
                        dve.wait_ge(q["x_hi"], j + 1)
                        dve.tensor_tensor(xl[:, part, :], x[:, part, :], xh[:, part, :].bitcast(F32), ALU.subtract
                                          ).then_inc(q["x_lo"], 1)
                        dve.wait_ge(q["x_lo"], j + 1)
                        steps(dve.tensor_scalar(x[:, part, :], x[:, part, :], ALPHA, None, ALU.mult))
                    steps.settle()

            def ffn_values(n):
                uses = USES[("ffa", "ffb")[n]]
                for half in range(2):
                    before = n * FT + half * FH

                    def gated(j):
                        dve.wait_ge(w_used[1], j + (uses[1] + half * FH + 1))
                        dve.wait_ge(sg_ready, j + (before + 1))
                        dve.wait_ge(hh_ready, j + before)
                        dve.wait_ge(hl_ready, j + before)
                        dve.tensor_tensor(ht[:].rearrange("p (h t) -> p h t", h=2), ps[:, 2:4, 0:HALF],
                                          sg[:].rearrange("p (h t) -> p h t", h=2), ALU.mult).then_inc(ht_ready, 1)
                        dve.wait_ge(ht_ready, j + (before + 1))
                        dve.wait_ge(hh_ready, j + (before + 1))
                        dve.tensor_tensor(hl[:, DS(j, 1), :], ht[:], hh[:, DS(j, 1), :].bitcast(F32),
                                          ALU.subtract).then_inc(hl_ready, 1)

                    if n == 0 or half == 1:
                        split_w(0, uses[0] + half * FH)
                        split_w(1, uses[1] + half * FH)
                    with dve.Fori(1, FH) as i:
                        split_w(0, i + (uses[0] + half * FH))
                        gated(i - 1)
                        split_w(1, i + (uses[1] + half * FH))
                    use = (2 * n + half) * (KC // 2)
                    split_d(0, use)
                    gated(FH - 1)

                    if half == 1:
                        dve.memset(csum[:], 0.0).then_inc(csum_step, 1)

                    def add_y(s, i):
                        dve.wait_ge(d_used[s], i + (use + 1))
                        xt = x[:, DS(i * 2 + s, 1), :].rearrange("p o (h t) -> p (o h) t", h=2)
                        dve.scalar_tensor_tensor(xt, ps[:, 4 + 2 * s:6 + 2 * s, 0:HALF], 0.5, xt, ALU.mult, ALU.add
                                                 ).then_inc(y_added[s], 1)
                        if half == 1:
                            dve.wait_ge(y_added[s], i + (use + 1))
                            dve.wait_ge(csum_step, i * 2 + ((2 * n) * (KC + 1) + s + 1))
                            dve.tensor_tensor(csum[:].rearrange("p (o t) -> p o t", o=1), x[:, DS(i * 2 + s, 1), :],
                                              csum[:].rearrange("p (o t) -> p o t", o=1), ALU.add
                                              ).then_inc(csum_step, 1)

                    if n == 1 and half == 0:
                        dve.wait_ge(q["residual"], 2 * KC)
                    with dve.Fori(0, KC // 2 - 1) as i:
                        split_d(1, i + use)
                        add_y(0, i)
                        split_d(0, i + (use + 1))
                        add_y(1, i)
                    split_d(1, use + KC // 2 - 1)
                    add_y(0, KC // 2 - 1)
                    add_y(1, KC // 2 - 1)

            def norm_values(n):
                for h in range(2):
                    hs = slice(h * HALF, (h + 1) * HALF)
                    dve.wait_ge(mean_ready, 2 * n + h + 1)
                    for k in range(0, KC, 4):
                        dve.tensor_tensor(x[:, k:k + 4, hs], x[:, k:k + 4, hs],
                                          ps[:, h:h + 1, 0:HALF].broadcast_to([128, 4, HALF]), ALU.subtract
                                          ).then_inc(centered, 1)
                for s in ((0,), (0, 1), ())[n]:
                    split_w(s, USES[("proj", "ffb")[n]][s])
                dve.wait_ge(centered, 4 * n + 4)
                for h in range(2):
                    hs = slice(h * HALF, (h + 1) * HALF)
                    dve.wait_ge(std_ready, 2 * n + h + 1)
                    steps(dve.reciprocal(rstd[:, hs], rstd[:, hs]))
                    if n == 2:
                        steps.settle()
                        wide = rstd[:, hs].rearrange("p (o t) -> p o t", o=1).broadcast_to([128, 4, HALF])
                        for k in range(0, KC, 4):
                            dve.tensor_tensor(x[:, k:k + 4, hs], x[:, k:k + 4, hs], wide, ALU.mult).then_inc(scaled, 1)
                if n < 2:
                    steps.settle()

                    def low(k):
                        dve.wait_ge(norm_hi, KC * n + k + 1)
                        dve.wait_ge(normed, KC * n + k + 1)
                        dve.tensor_tensor(xl[:, k, :], x[:, k, :], xh[:, k, :].bitcast(F32), ALU.subtract
                                          ).then_inc(norm_lo, 1)

                    for k in range(KC):
                        dve.tensor_tensor(x[:, k, :], x[:, k, :], rstd[:], ALU.mult).then_inc(scaled, 1)
                        if k >= 2:
                            low(k - 2)
                    low(KC - 2)
                    low(KC - 1)

            ffn_values(0)
            norm_values(0)
            with dve.Fori(0, NT // 2) as i:
                split_w(1, i + USES["proj"][1])
                split_w(0, i + (USES["proj"][0] + 1))

            for t in range(QT + 1):
                w = 128 if t < QT else NS
                dve.wait_ge(tok_in_psum, t + 1)
                b = 4 + 2 * (t % 2)
                dve.tensor_copy(kvtok[0:w, t, 0:4, :], ps[0:w, b, :].rearrange("p (j c) -> p j c", j=4))
                dve.tensor_copy(kvtok[0:w, t, 4:6, :], ps[0:w, b + 1, 0:256].rearrange("p (j c) -> p j c", j=2)
                                ).then_inc(tok_out, 1)


            dve.tensor_copy(rep8[:], ident[0:8, 0:8].rearrange("p (o b) -> p o b", o=1).broadcast_to([8, NH, 8]))
            for br in range(BR):
                dve.tensor_copy(
                    gate_sel[br // 2][:, br % 2 * R:(br % 2 + 1) * R, :].rearrange("p r (g d) -> p r g d", g=G),
                    ident[0:BR * NH, br * NH:(br + 1) * NH].rearrange("p (g r o) -> p r g o", g=G, o=1).broadcast_to(
                        [BR * NH, R, G, HD]))
            for g in range(G):
                gp = slice(g * HD, (g + 1) * HD)
                last = dve.tensor_scalar(
                    qbd[gp, :, g * 16:(g + 1) * 16].rearrange("p n (r q) -> p n r q", q=NQ),
                    zr[gp, 0:R, SEQ:T].rearrange("p r (n q) -> p n r q", q=NQ), SCALE, None, ALU.mult)
            last.then_inc(q["qbd_ready"], 1)

            dve.wait_ge(q["scmp_in_psum"], 1)
            dve.tensor_reduce(small[:, C_NCM:C_NCM + 2], ps[:, 0, 0:128].rearrange("p (n b) -> p n b", b=NBLK), AX,
                              ALU.max, negate=True).then_inc(q["ncm_ready"], 1)
            dve.wait_ge(q["snew_in_psum"], 1)
            dve.tensor_reduce(small[:, C_NNM:C_NNM + 4], ps[:, 1, 0:128].rearrange("p (n b) -> p n b", b=NS), AX,
                              ALU.max, negate=True).then_inc(q["nnm_ready"], 1)
            dve.memset(one[:], 1.0)
            dve.wait_ge(q["ecmp_ready"], 1)
            steps(dve.reciprocal(small[:, C_CSUM:C_CSUM + 2], small[:, C_CSUM:C_CSUM + 2]))
            steps.settle()
            for nh in range(2):
                last = dve.tensor_scalar(pcs[:, nh, :], pcs[:, nh, :], small[:, C_CSUM + nh:C_CSUM + nh + 1], None,
                                         ALU.mult)
            last.then_inc(q["pcs_ready"], 1)
            dve.wait_ge(q["gates_in_psum"], 1)
            dve.tensor_copy(gate_s[:].rearrange("p k n -> p (k n)"), ps[:, 2, 0:BR * R * NS])
            dve.tensor_copy(sext[:, :, :, 0:2], ps[:, 3, 128:192].rearrange("p (t n i) -> p t n i", t=4, i=2))
            steps(dve.tensor_copy(gate_p[:], ps[:, 3, 0:128].rearrange("p (t k) -> p t k", t=QT)[:, :, 0:BR * NH]))
            steps.settle()
            dve.engine_nop().then_inc(q["gates_ready"], 1)

            dve.wait_ge(q["imp_in_psum"], 1)
            dve.tensor_copy(pct[:].rearrange("p n r -> p (n r)"), ps[0:NBLK, 5, 0:256]).then_inc(q["pct_ready"], 1)
            for nh in range(2):
                steps(dve.tensor_copy(imp[:, nh, :].rearrange("p (j a h) -> p j h a", j=2, h=2),
                                      ps[:, 4, nh * NBLK:(nh + 1) * NBLK].rearrange("p (j h a) -> p j h a", j=2, h=2)))
            steps.settle()
            mid_blocks = slice(1, NBLK - 1)
            picks = N_SEL - 3
            for nh in range(2):
                cand = imp[:, nh, mid_blocks]
                m1, m2 = small[:, C_M1 + 8 * nh:C_M1 + 8 * nh + 8], small[:, C_M2 + 8 * nh:C_M2 + 8 * nh + 8]
                cnt = small[:, C_CNT + nh:C_CNT + nh + 1]
                steps(dve.max(m1, cand)); steps.settle()
                steps(dve.match_replace(rest[:, nh, mid_blocks], m1, cand, -1.0)); steps.settle()
                steps(dve.max(m2, rest[:, nh, mid_blocks])); steps.settle()
                last_in = small[:, C_M2 + 8 * nh + picks - 9:C_M2 + 8 * nh + picks - 8]
                steps(dve.tensor_scalar(gt[:, nh, mid_blocks], cand, last_in, None, ALU.is_gt, ALU.add, accum_out=cnt))
                steps(dve.tensor_scalar(eq[:, nh, mid_blocks], cand, last_in, None, ALU.is_equal)); steps.settle()
                steps(dve.tensor_scalar(cnt, cnt, -1.0, float(picks), ALU.mult, ALU.add))
                steps(dve.tensor_tensor_scan(pre[:, nh, mid_blocks], one[:, mid_blocks], eq[:, nh, mid_blocks], 0.0,
                                             ALU.mult, ALU.add)); steps.settle()
                steps(dve.scalar_tensor_tensor(rest[:, nh, mid_blocks], pre[:, nh, mid_blocks], cnt,
                                               eq[:, nh, mid_blocks], ALU.is_le, ALU.mult)); steps.settle()
                steps(dve.tensor_tensor(gt[:, nh, mid_blocks], gt[:, nh, mid_blocks], rest[:, nh, mid_blocks],
                                        ALU.add)); steps.settle()
                dve.tensor_scalar(selneg[:, nh, mid_blocks], gt[:, nh, mid_blocks], -1.0, -NEG, ALU.add, ALU.mult)
                last = dve.memset(selneg[:, nh, 0:NBLK:NBLK - 1], 0.0)
            last.then_inc(q["sel_ready"], 1)

            dve.wait_ge(q["kcp_in_psum"], 1)
            dve.tensor_scalar(kcp[:], ps[:, 6, 0:8], SCALE, None, ALU.mult)
            dve.tensor_copy(vcp[:], ps[0:8, 7, 0:128]).then_inc(q["kcp_ready"], 1)
            dve.wait_ge(q["ocs_in_psum"], 1)
            dve.tensor_copy(ocs[:].rearrange("p n d -> p (n d)"), ps[:, 0, 0:256]).then_inc(q["ocs_ready"], 1)
            dve.wait_ge(q["pnewt_in_psum"], 1)
            dve.tensor_copy(pnt[:].rearrange("p k r -> p (k r)"), ps[0:NS, 1, :]).then_inc(q["pnewt_ready"], 1)
            dve.wait_ge(q["selt_in_psum"], 1)
            dve.tensor_copy(selt[:].rearrange("p n b -> p (n b)"), ps[:, 5, 0:128]).then_inc(q["selt_ready"], 1)
            dve.wait_ge(q["rep_in_psum"], 1)
            dve.tensor_tensor(vbd[:], ps[0:64, 7, 0:128].rearrange("p (o g d) -> p o g d", o=1, g=G).broadcast_to(
                [64, R, G, HD]), diag[:].rearrange("p r (g o) -> p r g o", o=1).broadcast_to([64, R, G, HD]), ALU.mult
                ).then_inc(q["vbd_ready"], 1)

            dve.wait_ge(q["sp_in_psum"], 1)
            w_p = pp[0][:, 0:256]
            by_row = w_p.rearrange("p (x b) -> p x b", b=8)
            for g in range(G):
                steps(dve.tensor_tensor(
                    w_p.rearrange("p (t g r b) -> p t g r b", t=QT, g=G, r=R)[:, :, g, :, :],
                    ps[:, 2 + g, 0:128].rearrange("p (t r b) -> p t r b", t=QT, r=R),
                    blk_neg[:].rearrange("p t (o b) -> p t o b", o=1).broadcast_to([128, QT, R, 8]), ALU.add))
            steps.settle()
            mx = small[:, C_MX:C_MX + 32]
            wide = mx.rearrange("p (x o) -> p x o", o=1).broadcast_to([128, 32, 8])
            steps(dve.tensor_reduce(mx, by_row, AX, ALU.max)); steps.settle()
            dve.tensor_tensor(by_row, by_row, wide, ALU.subtract).then_inc(q["sp_shifted"], 1)
            dve.wait_ge(q["ep_ready"], 1)
            steps(dve.tensor_tensor(w_p.rearrange("p (t x b) -> p t x b", t=QT, b=8),
                                    w_p.rearrange("p (t x b) -> p t x b", t=QT, b=8),
                                    blk_ok[:].rearrange("p t (o b) -> p t o b", o=1).broadcast_to([128, QT, NH, 8]),
                                    ALU.mult)); steps.settle()
            steps(dve.tensor_reduce(mx, by_row, AX, ALU.add)); steps.settle()
            steps(dve.tensor_scalar(mx, mx, 0.5, None, ALU.max)); steps.settle()
            steps(dve.reciprocal(mx, mx)); steps.settle()
            steps(dve.tensor_tensor(mx.rearrange("p (t x) -> p t x", t=QT), mx.rearrange("p (t x) -> p t x", t=QT),
                                    gate_p[:, :, 0:NH], ALU.mult)); steps.settle()
            dve.tensor_tensor(by_row, by_row, wide, ALU.mult).then_inc(q["pp_ready"], 1)
            dve.wait_ge(q["onew_in_psum"], 1)
            dve.tensor_copy(onew, ps[:, 4, :]).then_inc(q["onew_ready"], 1)
            dve.wait_ge(q["ptp_in_psum"], 1)
            dve.tensor_copy(ptp[:].rearrange("p t c -> p (t c)"), ps[0:64, 6, :]).then_inc(q["ptp_ready"], 1)

            steps(dve.tensor_tensor(zc[:, 4:8, :], zc[:, 4:8, :], zc[:, 8:12, :], ALU.mult)); steps.settle()
            dve.tensor_copy(sext[:, :, :, 2:2 + NQ], zc[:, 4:8, SEQ:T].rearrange("p t (n i) -> p t n i", i=NQ)
                            ).then_inc(q["u_ready"], 1)
            dve.wait_ge(q["u_ready"], 1)
            for k in range(3):
                lag = 2 - k if k < 2 else 0
            for tap in (2, 1, 0):
                lag = 2 - tap
                for t in range(4):
                    wt = par[:, R_WC + 4 * tap + t:R_WC + 4 * tap + t + 1]
                    z, u, e = zc[:, 8 + t, :], zc[:, 4 + t, :], sext[:, t, :, tap:tap + NQ]
                    zs = z[:, SEQ:T].rearrange("p (n i) -> p n i", i=NQ)
                    if tap == 2:
                        dve.tensor_scalar(z[:, 0:SEQ], u[:, 0:SEQ], wt, None, ALU.mult)
                        steps(dve.tensor_scalar(zs, e, wt, None, ALU.mult))
                    else:
                        dve.scalar_tensor_tensor(z[:, lag:SEQ], u[:, 0:SEQ - lag], wt, z[:, lag:SEQ], ALU.mult, ALU.add)
                        steps(dve.scalar_tensor_tensor(zs, e, wt, zs, ALU.mult, ALU.add))
                steps.settle()
            dve.tensor_tensor(yconv[:], zc[:, 0:4, :], zc[:, 8:12, :], ALU.mult).then_inc(q["conv_ready"], 1)
            dve.wait_ge(q["ctok_in_psum"], 1)
            dve.tensor_copy(ctok[:, 0, :], ps[0:NS, 5, :])
            dve.tensor_copy(ctok[:, 1, :], ps[0:NS, 7, :]).then_inc(q["ctok_ready"], 1)

            units = [(br, t, g) for br in range(2) for t in range(QT) for g in range(G)]
            U = len(units)
            dve.wait_ge(q["op_ready"], 1)
            def prompt_head(r):
                dve.wait_ge(q["scores"], r * U)
                dve.tensor_scalar(qs[:].rearrange("p (o t) -> p o t", o=1), zr[:, DS(r, 1), 0:SEQ], SCALE, None, ALU.mult
                                  ).then_inc(q["qs_ready"], 1)
                for j in range(U + 3):
                    if j < U:
                        br, t, g = units[j]
                        dve.wait_ge(q["scores"], r * U + (j + 1))
                        dve.tensor_reduce(small[:, C_PNM + j:C_PNM + j + 1], ps[:, j % 3, 0:(t + 1) * 128], AX, ALU.max,
                                          negate=True).then_inc(q["negmax"], 1)
                    if j >= 3:
                        k = j - 3
                        br, t, g = units[k]
                        rec, gs = small[:, C_REC:C_REC + 1], small[:, C_GS:C_GS + 1]
                        dve.wait_ge(q["pv"], r * U + (k + 1))
                        dve.wait_ge(q["o_added"], r * U + k)
                        steps(dve.reciprocal(rec, small[:, C_PSUM + k:C_PSUM + k + 1])); steps.settle()
                        steps(dve.tensor_tensor(gs, rec, gate_p[:, t, DS(r + ((1 + br) * NH + g * R), 1)], ALU.mult))
                        steps.settle()
                        o = po[:, t, DS(r, 1), g * HD:(g + 1) * HD].rearrange("p o d -> p (o d)")
                        dve.scalar_tensor_tensor(o, ps[:, 5 + k % 2, 0:HD], gs, o, ALU.mult, ALU.add
                                                 ).then_inc(q["o_added"], 1)

            def queries(b, n, scored):
                dve.wait_ge(q["s_scores"], scored)
                dve.tensor_copy(qn[b][:].rearrange("p (o r) -> p o r", o=1), qbd[:, DS(n, 1), :]
                                ).then_inc(q["qn_ready"], 1)

            def keys_s(n):
                for m in range(1, 9, 2):
                    dve.wait_ge(q["kt_in_psum"], n * 9 + (m + 1))
                    if m == 1:
                        dve.wait_ge(q["s_scores"], n)
                    dve.tensor_copy(kt[:, 4 * m:4 * m + 4, :].rearrange("p k t -> p (k t)"), ps[:, 1, :]
                                    ).then_inc(q["kt_by_dve"], 1)

            def negmax_s(n):
                dve.wait_ge(q["s_scores"], n + 1)
                dve.tensor_reduce(cb[:, DS(n, 1), 0, OB - 1], ps[:, 2:4, :].rearrange("p b t -> p (b t)"), AX, ALU.max,
                                  negate=True)
                dve.tensor_reduce(cb[:, DS(n, 1), 1, OB - 1], ps[:, 4, 0:128], AX, ALU.max, negate=True
                                  ).then_inc(q["s_negmax"], 1)

            def probs_t_s(n):
                dve.wait_ge(q["s_probs_t"], n + 1)
                dve.tensor_copy(pwt[:, 0:4, :].rearrange("p k t -> p (k t)"), ps[:, 5, :]).then_inc(q["s_pt_dve"], 1)

            def out_s(b, i, n):
                dve.wait_ge(q[f"s_pv{b}"], i + 1)
                dve.tensor_copy(cb[:, DS(n, 1), :, 0:128].rearrange("p o b d -> p (o b) d"),
                                ps[:, 7, 0:256].rearrange("p (b d) -> p b d", b=2)).then_inc(q["s_o"], 1)

            dve.wait_ge(q["state_stored"], 16 * (NB + 1))
            with dve.Fori(0, R) as r:
                steps.enter(r, 0, 2 * U)
                prompt_head(r)
                queries(0, r * 2, r * 2)
                queries(1, r * 2 + 1, r * 2)
                keys_s(r * 2)
                negmax_s(r * 2)
                dve.wait_ge(q["pv"], (r + 1) * U)
                keys_s(r * 2 + 1)
                probs_t_s(r * 2)
                out_s(0, r, r * 2)
                negmax_s(r * 2 + 1)
                probs_t_s(r * 2 + 1)
                out_s(1, r, r * 2 + 1)
            steps.leave(R)

            dve.wait_ge(q["m_in_psum"], 1)
            steps(dve.tensor_reduce(neg_row[:], ps[0:16, 0, 0:128].rearrange("p (c r) -> p r c", c=CH), AX, ALU.min))
            steps.settle()
            dve.tensor_copy(neg_rep[:], neg_row[:].rearrange("p (o r) -> p o r", o=1).broadcast_to([16, CH, NS])
                            ).then_inc(q["m_ready"], 1)
            dve.wait_ge(q["mb_in_psum"], 1)
            steps(dve.tensor_copy(neg_all[:], ps[:, 1, 0:16])); steps.settle()
            cbf = cb[:].rearrange("p n b o -> p (n b) o")
            dve.tensor_tensor(chunk_w[:], neg_all[:], cbf[:, :, OB - 1], ALU.subtract).then_inc(q["mdiff_ready"], 1)
            dve.wait_ge(q["mw_ready"], 1)
            dve.tensor_tensor(cbf[:, :, 0:OB - 1], cbf[:, :, 0:OB - 1],
                              chunk_w[:].rearrange("p (x o) -> p x o", o=1).broadcast_to([128, 16, OB - 1]), ALU.mult)
            dve.tensor_scalar(cbf[:, :, OB - 1], neg_all[:], 1.0 / CH, None, ALU.mult).then_inc(q["cb_scaled"], 1)
            dve.wait_ge(q["comb_in_psum"], 1)
            steps(dve.tensor_copy(comb[:].rearrange("p n b o -> p n (b o)"), ps[:, 2:4, 0:2 * OB]))
            steps.settle()
            F = C_F
            four = lambda c: small[:, c:c + 4].rearrange("p (b n) -> p b n", b=2)
            wide4 = lambda c: small[:, c:c + 4].rearrange("p (x o) -> p x o", o=1).broadcast_to([128, 4, 128])
            neg_c = comb[:, :, :, OB - 1].rearrange("p n b -> p b n")
            sum_c = comb[:, :, :, OB - 2].rearrange("p n b -> p b n")
            steps(dve.tensor_tensor(four(F + 8), neg_c, four(C_NNM), ALU.min)); steps.settle()
            dve.tensor_tensor(four(F), four(F + 8), neg_c, ALU.subtract)
            dve.tensor_tensor(four(F + 4), four(F + 8), four(C_NNM), ALU.subtract).then_inc(q["diff_ready"], 1)
            dve.wait_ge(q["wts_ready"], 1)
            steps(dve.tensor_tensor(four(F + 12), four(F), sum_c, ALU.mult))
            steps(dve.tensor_tensor(four(F + 16), four(F + 4), four(C_NSUM), ALU.mult)); steps.settle()
            steps(dve.tensor_tensor(four(F + 20), four(F + 12), four(F + 16), ALU.add)); steps.settle()
            steps(dve.reciprocal(four(F + 24), four(F + 20))); steps.settle()
            steps(dve.tensor_tensor(four(F + 28), four(F), four(F + 24), ALU.mult))
            steps(dve.tensor_tensor(four(F + 32), four(F + 4), four(F + 24), ALU.mult)); steps.settle()
            onew4 = onew.rearrange("p (x d) -> p x d", d=128)
            for k in range(4):
                br, nh = k // 2, k % 2
                steps(dve.tensor_scalar(onew4[:, k, :], onew4[:, k, :], small[:, F + 32 + k:F + 33 + k], None, ALU.mult))
            steps.settle()
            for k in range(4):
                br, nh = k // 2, k % 2
                last = dve.scalar_tensor_tensor(ofin[:, nh, br, :], comb[:, nh, br, 0:128], small[:, F + 28 + k:F + 29 + k],
                                                onew4[:, k, :], ALU.mult, ALU.add)
            last.then_inc(q["ofin_ready"], 1)
            dve.wait_ge(q["ofin_in_psum"], 1)
            for g in range(G):
                gp = slice(g * HD, (g + 1) * HD)
                for br in range(BR):
                    for nh in range(2):
                        steps(dve.tensor_tensor(
                            os_all[gp, br, nh, :, :, :],
                            ps[gp, 4 + br, nh * 128:(nh + 1) * 128].rearrange(
                                "p (n g r q) -> p n g r q", n=4, g=G, r=R)[:, :, g, :, :],
                            gate_s[gp, br * R:(br + 1) * R, nh * 16:(nh + 1) * 16].rearrange(
                                "p r (n q) -> p n r q", q=NQ), ALU.mult))
            steps.settle()
            sum_o = os_all[:].rearrange("p b h n r q -> p b (h n) r q")
            out_o = os_sum[:].rearrange("p r n q -> p n r q")
            steps(dve.tensor_tensor(out_o, sum_o[:, 0], sum_o[:, 1], ALU.add)); steps.settle()
            dve.tensor_tensor(out_o, out_o, sum_o[:, 2], ALU.add).then_inc(q["os_ready"], 1)
            dve.wait_ge(q["os_ready"], 1)
            for r in range(R):
                dve.wait_ge(q["at_hi"], r + 1)
                dve.tensor_tensor(xl[:, r, 0:SEQ], ps[:, r % 2, :], xh[:, r, 0:SEQ].bitcast(F32), ALU.subtract)
                dve.tensor_tensor(xl[:, r, SEQ:T], os_sum[:, r, :, :].rearrange("p n q -> p (n q)"),
                                  xh[:, r, SEQ:T].bitcast(F32), ALU.subtract).then_inc(q["at_lo"], 1)
            dve.wait_ge(q["at_hi"], R + 1)
            dve.tensor_tensor(xl[:, R:KC, :], yconv[:], xh[:, R:KC, :].bitcast(F32), ALU.subtract
                              ).then_inc(q["at_lo"], 1)

            def add_out(t):
                s = t % 2
                dve.wait_ge(w_used[s], USES["out"][s] + t // 2 + 1)
                xt = x[:, t, :].rearrange("p (h t) -> p h t", h=2)
                dve.tensor_tensor(xt, ps[:, 2 * s:2 * s + 2, 0:HALF], xt, ALU.add).then_inc(q["out_added"], 1)
                dve.wait_ge(q["out_added"], t + 1)
                dve.wait_ge(csum_step, KC + 1 + t + 1)
                dve.tensor_tensor(csum[:], x[:, t, :], csum[:], ALU.add).then_inc(csum_step, 1)

            split_w(0, USES["out"][0])
            dve.wait_ge(q["residual"], KC)
            dve.wait_ge(q["at_lo"], R + 1)
            dve.memset(csum[:], 0.0).then_inc(csum_step, 1)
            for t in range(1, KC):
                split_w(t % 2, USES["out"][t % 2] + t // 2)
                add_out(t - 1)
            add_out(KC - 1)
            norm_values(1)
            ffn_values(1)
            norm_values(2)
            for t in range(QT + 1):
                w = 128 if t < QT else NS
                dve.wait_ge(q["y_in_psum"], t + 1)
                dve.tensor_copy(yout[0:w, t, 512:1024], ps[0:w, 5 + 2 * (t % 2), :]).then_inc(q["y_by_dve"], 1)


_INS = ["x_prompt", "x_sample", "cache_cmp_kv", "cache_sel_kv", "state_win_kv", "state_conv", "page_table",
        "ffa_gate", "ffa_up", "ffa_down", "ln1_g", "ln1_b", "w_in", "b_in", "w_conv", "cmp_w1", "cmp_w2", "cmp_pe",
        "w_out", "ln2_g", "ln2_b", "ffb_gate", "ffb_up", "ffb_down", "ln3_g", "ln3_b"]
_OUTS = [(1, SEQ, D), (NB, NQ, D), (1, 1, SEQ, 2, G, HD), (1, 1, SEQ, 2, G, HD), (1, 1, WIN, 2, G, HD),
         (1, 1, 2, DC), (1, NB, NQ, 2, G, HD), (1, NB, NQ, 2, G, HD), (1, NB, WIN, 2, G, HD), (1, NB, 2, DC)]


def kernel(**inputs):
    import numpy as _np
    import concourse.bacc as _bacc
    from concourse import mybir as _mybir
    from concourse.bass_utils import run_bass_kernel_spmd as _run

    nc = _bacc.Bacc("TRN2", target_bir_lowering=False, num_devices=1)
    arrays, args = {}, []
    for name in _INS:
        a = _np.ascontiguousarray(inputs[name])
        arrays[f"in_{name}_dram"] = a
        args.append(nc.dram_tensor(f"in_{name}_dram", a.shape, _mybir.dt.from_np(a.dtype), kind="ExternalInput").ap())
    for i, shape in enumerate(_OUTS):
        args.append(nc.dram_tensor(f"out_{i}_dram", shape, _mybir.dt.float32, kind="ExternalOutput").ap())
    trunk(nc, *args)
    r = _run(nc, [arrays], core_ids=[0])
    return tuple(r.results[0][f"out_{i}_dram"] for i in range(len(_OUTS)))
```

```python
from contextlib import ExitStack

import concourse.bass as bass
from concourse import mybir

F32 = mybir.dt.float32
F32R = mybir.dt.float32r
BF16 = mybir.dt.bfloat16
I32 = mybir.dt.int32
ALU = mybir.AluOpType
ACT = mybir.ActivationFunctionType
AX = mybir.AxisListType.X
DS = bass.ds

D = 1024
SEQ = 512
NB = 8
NQ = 4
NS = NB * NQ
T = SEQ + NS
HALF = T // 2
KC = D // 128
FF = 2816
FT = FF // 128
FH = FT // 2
DC = 512
HD = 64
G = 2
R = 4
NH = G * R
BR = 3
BLK = 64
PAGE = 128
NPG = 32
NPHYS = 320
NBLK = NPG * 2
KVW = 256
QT = SEQ // 128
CH = 4
PC = NPG // CH
WIN = 512
N_SEL = 16
ALPHA = 2.0 ** 0.25
SCALE = HD ** -0.5
EPS = 1e-5
NEG = -1e30
ZC = 3 * DC // 128
ZR = 11
KV0, G0 = 4, 10
OFF_Q = 3 * DC
OFF_KV = OFF_Q + NH * HD
OFF_G = OFF_KV + 3 * KVW
OB = 130

R_LN = 0
R_BC, R_BQ, R_BKV, R_BG = 48, 60, 64, 70
R_WC = 71


USES = {"ffa": (0, 0), "proj": (FT, FT), "out": (FT + 12, FT + 11), "ffb": (FT + 16, FT + 15)}
FILLS = {"ffa": (0, 0), "proj": (FT, FT), "out": (FT + 24, FT + 22), "ffb": (FT + 36, FT + 34)}
PER_FILL = {"ffa": 1, "proj": 2, "out": 3, "ffb": 1}
NT = ZC + ZR

UP = NPG // 2
PARTS = ((0, 1, 2), (3, 4, 5), (6, 7, 8), (9, 10, 11), (15, 12, 13, 14))
FIRST = (3, 0, 3, 0, 2)
GROUPS = len(PARTS)
PLACE = UP * KVW
PLACES0 = 2 * KC * T - 2 * PLACE
GW = 4 * 2 * UP
SPAN = PLACES0 + 6 * PLACE + 2 * HD * 128 + 2 * 2 * G * GW


ONE = 1

C_NCM, C_CSUM, C_M1, C_M2, C_CNT, C_NNM, C_NSUM, C_PNM, C_PSUM = 0, 2, 4, 20, 36, 38, 42, 46, 62
C_MX = 82
C_REC = C_M1
C_F = 120


class Steps:

    def __init__(self, eng, sem):
        self.eng, self.sem, self.n, self.i = eng, sem, 0, None

    def __call__(self, ins):
        ins.then_inc(self.sem, 1)
        self.n += 1
        return ins

    def settle(self):
        if self.i is None:
            self.eng.wait_ge(self.sem, self.n)
        else:
            i, first, per, start = self.i
            self.eng.wait_ge(self.sem, (i - first) * per + self.n)

    def enter(self, i, first, per):
        self.i = (i, first, per, self.n)

    def leave(self, times):
        _, _, per, start = self.i
        assert self.n - start == per, (self.n - start, per)
        self.i = None
        self.n = start + per * times


def trunk(nc, x_prompt, x_sample, cache_cmp, cache_sel, state_win, state_conv, page_table,
          ffa_gate, ffa_up, ffa_down, ln1_g, ln1_b, w_in, b_in, w_conv, cmp_w1, cmp_w2, cmp_pe,
          w_out, ln2_g, ln2_b, ffb_gate, ffb_up, ffb_down, ln3_g, ln3_b,
          y_prompt, y_sample, p_cmp, p_sel, p_win, p_conv, s_cmp, s_sel, s_win, s_conv):
    ctx = ExitStack()
    with ctx:
        def sb(name, shape, dt=F32, stack=ctx):
            return stack.enter_context(nc.sbuf_tensor(name, shape, dt))

        def sem(name):
            return ctx.enter_context(nc.semaphore(name))

        ident = sb("ident", [128, 128])
        identb = sb("identb", [128, 128], BF16)
        causal = sb("causal", [128, 128], BF16)
        mean_w = sb("mean_w", [128, 128])
        eps = sb("eps", [128, 1])
        par = sb("par", [128, 96])
        x = sb("x", [128, KC, T])
        pages_sb = sb("pages_sb", [1, NB * NPG], I32)
        kc_all = sb("kc_all", [128, NB, NBLK])
        vc_all = sb("vc_all", [64, NB, 128])
        w2 = sb("w2", [128, 2, HD])
        hid_bias = sb("hid_bias", [128, 3])
        same = sb("same", [128, 128])
        fold = sb("fold", [128, NS])
        win_mask = sb("win_mask", [128, 128], BF16)
        new_mask = sb("new_mask", [128, 2, NS], BF16)
        qbd = sb("qbd", [128, NB, NS])
        qn = [sb(f"qn{n}", [128, NS]) for n in range(2)]
        gate_p = sb("gate_p", [128, QT, BR * NH])
        gate_r = sb("gate_r", [128, QT, 4])
        blk_neg = sb("blk_neg", [128, QT, 8])
        blk_ok = sb("blk_ok", [128, QT, 8])
        diag = sb("diag", [64, R, G])
        selneg = sb("selneg", [128, 2, NBLK], BF16)
        selt = sb("selt", [128, NB, 16], BF16)
        small = sb("small", [128, 160])
        u1 = ExitStack()
        xh = sb("xh", [128, KC, T], F32R, u1)
        xl = sb("xl", [128, KC, T], F32R, u1)
        u1.close()
        up = ExitStack()
        w1p = sb("w1p", [128, 2, HD, HD], F32, up)
        up.close()
        first = ExitStack()
        span = sb("span", [128, SPAN], F32, first)
        first.close()
        place = [span[:, PLACES0 + k * PLACE:PLACES0 + (k + 1) * PLACE] for k in range(6)]
        cpages = [span[:, PLACES0 + at * PLACE:PLACES0 + (at + len(parts)) * PLACE].rearrange("p (a c) -> p a c", c=KVW)
                  for at, parts in zip(FIRST, PARTS)]
        xin = place[0].rearrange("p (t d) -> p t d", d=D)
        w1 = span[:, PLACES0 + PLACE:PLACES0 + 3 * PLACE].rearrange("p (c d h) -> p c d h", c=2, d=HD)
        prow = place[5][:, 0:128]
        xin_s = place[5][0:NS, 128:128 + D]
        at = PLACES0 + 6 * PLACE
        wbd = span[:, at:at + 2 * HD * 2 * HD].rearrange("p (c d a h) -> p c d a h", c=2, d=HD, a=2)
        at += 2 * HD * 2 * HD
        hid = [span[:, at + k * 2 * G * GW:at + (k + 1) * 2 * G * GW].rearrange(
            "p (c g u b) -> p c g u b", c=2, g=G, u=4) for k in range(2)]
        page0 = sb("page0", [128, 2 * KC * T])
        ffn = ExitStack()
        hh = sb("hh", [128, FH, T], F32R, ffn)
        hl = sb("hl", [128, FH, T], F32R, ffn)
        draw = [sb(f"draw{n}", [128, FH, 128], F32, ffn) for n in range(2)]
        dhi = [sb(f"dhi{n}", [128, FH, 128], F32R, ffn) for n in range(2)]
        dlo = [sb(f"dlo{n}", [128, FH, 128], F32R, ffn) for n in range(2)]
        sg = sb("sg", [128, T], F32, ffn)
        ht = sb("ht", [128, T], F32, ffn)
        csum = sb("csum", [128, T], F32, ffn)
        rstd = sb("rstd", [128, T], F32, ffn)
        sq = sb("sq", [128, KC, T], F32, ffn)
        ffn.close()
        norm = ExitStack()
        yout = sb("yout", [128, QT + 1, D], F32, norm)
        norm.close()
        zr = sb("zr", [128, ZR, T])
        kvtok = sb("kvtok", [128, QT + 1, 6, 128])
        yconv = sb("yconv", [128, 4, T])
        conv = ExitStack()
        zc = sb("zc", [128, ZC, T], F32, conv)
        tap_u = [sb(f"tap_u{n}", [128, T], F32, conv) for n in range(2)]
        sext = sb("sext", [128, 4, NB, NQ + 2], F32, conv)
        conv.close()
        page1 = sb("page1", [128, NPG, KVW])
        pr = ExitStack()
        crow = sb("crow", [NB * 2, DC], F32, pr)
        ctok = sb("ctok", [NS, 2, DC], F32, pr)
        kcp = sb("kcp", [128, G, 32], F32, pr)
        vcp = sb("vcp", [8, 128], F32, pr)
        hidp = sb("hidp", [128, 2, QT, G], F32, pr)
        vbd = sb("vbd", [128, R, G, HD], F32, pr)
        ptp = sb("ptp", [128, QT, 128], F32, pr)
        pnt = sb("pnt", [NS, 4, 128], F32, pr)
        rep8 = sb("rep8", [8, NH, 8], F32, pr)
        pr.close()
        fin = ExitStack()
        neg_row = sb("neg_row", [16, NS], F32, fin)
        neg_rep = sb("neg_rep", [16, CH, NS], F32, fin)
        neg_all = sb("neg_all", [128, 16], F32, fin)
        chunk_w = sb("chunk_w", [128, 16], F32, fin)
        comb = sb("comb", [128, 2, 2, OB], F32, fin)
        ofin = sb("ofin", [128, 2, 2, 128], F32, fin)
        os_all = sb("os_all", [128, BR, 2, 4, R, NQ], F32, fin)
        os_sum = sb("os_sum", [128, R, NB, NQ], F32, fin)
        fin.close()
        units_mem = ExitStack()
        pp = [sb(f"pp{n}", [128, G, SEQ], F32, units_mem) for n in range(2)]
        ppt = [sb(f"ppt{n}", [128, G, SEQ], F32, units_mem) for n in range(2)]
        norm_diag = [sb(f"norm_diag{n}", [128, G, 128], F32, units_mem) for n in range(2)]
        units_mem.close()
        kt = sb("kt", [128, NPG + CH, 128])
        win = [sb(f"win{n}", [128, CH, KVW]) for n in range(2)]
        qs = sb("qs", [128, G, SEQ])
        u1 = ExitStack()
        kd = sb("kd", [128, 2, 2, HD, 2 * QT], F32, u1)
        u1.close()
        pw = sb("pw", [128, PC + 1, 128])
        pwt = sb("pwt", [128, PC + 1, 128])
        ring = ExitStack()
        ghi = [sb(f"ghi{n}", [128, KC, 128], F32R, ring) for n in range(2)]
        glo = [sb(f"glo{n}", [128, KC, 128], F32R, ring) for n in range(2)]
        graw = [sb(f"graw{n}", [128, KC, 128], F32, ring) for n in range(2)]
        pe_sb = sb("pe_sb", [128, 2, HD], F32, ring)
        pe_sum = sb("pe_sum", [128, 2, HD], F32, ring)
        ring.close()
        mid = ExitStack()
        po = sb("po", [128, R, SEQ], F32, mid)
        cb = sb("cb", [128, NB, 2, OB], F32, mid)
        pcs = sb("pcs", [128, 2, NBLK], F32, mid)
        pct = sb("pct", [64, 2, 128], F32, mid)
        imp = sb("imp", [128, 2, NBLK], F32, mid)
        rest = sb("rest", [128, 2, NBLK], F32, mid)
        gt = sb("gt", [128, 2, NBLK], F32, mid)
        eq = sb("eq", [128, 2, NBLK], F32, mid)
        pre = sb("pre", [128, 2, NBLK], F32, mid)
        one = sb("one", [128, NBLK], F32, mid)
        pnew = sb("pnew", [128, 4, NS], F32, mid)
        ocs = sb("ocs", [128, 2, 128], F32, mid)
        gate_s = sb("gate_s", [128, BR * R, NS], F32, mid)
        onew = sb("onew", [128, 4, 128], F32, mid)
        mid.close()
        w_cmp = pw[:, 0:2, :].rearrange("p a b -> p (a b)")
        hidx = qs[:, 0, 0:4 * HD]
        spt = pwt[:, 0:8, :].rearrange("p a b -> p (a b)").rearrange("p (g t) -> p g t", g=G)
        gate_sel = [win[0][0:BR * NH].rearrange("p a (b m) -> p (a b) m", m=128),
                    win[1][0:BR * NH].rearrange("p a (b m) -> p (a b) m", m=128)]
        pages = (page0[:, 0:NPG * KVW].rearrange("p (a c) -> p a c", c=KVW), page1[:])

        ps = ctx.enter_context(nc.psum_tensor("ps", [128, 8, 512], F32))


        dma_x, dma_par = sem("dma_x"), sem("dma_par")
        prow_clear, const_ready = sem("prow_clear"), sem("const_ready")
        dve_step, pool_step = sem("dve_step"), sem("pool_step")
        small_in_psum, par_ready = sem("small_in_psum"), sem("par_ready")
        xt_in_psum = sem("xt_in_psum")
        dma_w = [sem("dma_w0"), sem("dma_w1")]
        w_hi, w_lo = [sem("w_hi0"), sem("w_hi1")], [sem("w_lo0"), sem("w_lo1")]
        w_used = [sem("w_used0"), sem("w_used1")]
        sg_ready, ht_ready, hh_ready, hl_ready = sem("sg_ready"), sem("ht_ready"), sem("hh_ready"), sem("hl_ready")
        dma_d = [sem("dma_d0"), sem("dma_d1")]
        d_hi, d_lo = [sem("d_hi0"), sem("d_hi1")], [sem("d_lo0"), sem("d_lo1")]
        d_used, y_added = [sem("d_used0"), sem("d_used1")], [sem("y_added0"), sem("y_added1")]
        csum_step, mean_ready, centered = sem("csum_step"), sem("mean_ready"), sem("centered")
        sq_ready, var_ready, std_ready = sem("sq_ready"), sem("var_ready"), sem("std_ready")
        scaled, normed, norm_hi, norm_lo = sem("scaled"), sem("normed"), sem("norm_hi"), sem("norm_lo")
        z_out = [sem("z_out0"), sem("z_out1")]
        tok_in_psum, tok_out = sem("tok_in_psum"), sem("tok_out")
        stored = sem("stored")
        names = ("dma_first", "dma_cmp_w", "dma_cpage0", "dma_cpage1", "hid_in_psum", "hid_ready", "kc_in_psum",
                 "kc_ready", "wbd_by_act", "wbd_by_dve", "zeros_ready", "x_by_act", "x_by_dve", "x_hi", "x_lo",
                 "pe_summed", "bias_ready", "qbd_ready", "ecmp_ready", "pcs_ready", "imp_in_psum", "pct_ready",
                 "ocs_in_psum", "ocs_ready", "sel_ready", "selt_in_psum", "selt_ready", "s_small_in_psum",
                 "maxima_ready", "pnew_ready", "pnewt_in_psum", "pnewt_ready", "onew_in_psum", "onew_ready",
                 "gates_in_psum", "gates_ready", "dma_conv", "u_ready", "conv_ready", "ctok_in_psum", "ctok_ready",
                 "dma_page1_pool", "hidx_in_psum", "pads_ready", "hid_operand_ready", "hidp_in_psum", "hidp_ready",
                 "kcp_in_psum", "kcp_ready", "rep_in_psum", "vbd_ready", "spt_in_psum", "spt_by_act", "spt_by_dve",
                 "sp_in_psum", "sp_shifted", "ep_ready", "pp_ready", "ptp_in_psum", "ptp_ready", "op_in_psum",
                 "diag_ready", "op_ready", "qs_ready", "scores", "negmax", "probs", "probs_t", "pt_copied", "pv",
                 "o_added", "dma_page0", "dma_page1", "dma_win0", "dma_win1", "qn_ready", "kt_in_psum", "kt_by_act",
                 "kt_by_dve", "s_scores", "s_negmax", "s_probs", "s_probs_t", "s_pt_act", "s_pt_dve", "s_pv0",
                 "s_pv1", "s_o", "masks_ready", "state_stored", "m_ready", "maxima_in_psum", "cb_scaled",
                 "comb_in_psum", "exponents_ready", "powers_ready", "ofin_ready", "ofin_in_psum", "os_ready",
                 "at_hi", "at_lo", "out_added", "y_in_psum", "y_by_act", "y_by_dve", "residual")
        q = {name: sem(name) for name in names}

        block = ctx.enter_context(nc.Block())

        def count_from_one(eng, sems):
            for s in sems:
                eng.sem_inc(s, ONE)

        def page_loads(eng, dst, at, first, pool, landed):
            for j in range(0, UP, 8):
                _, numbers = nc.values_load_multi_w_load_instructions(
                    pages_sb[0:1, DS(first + j, 8)], engines=[eng.engine], min_val=0, max_val=NPHYS - 1,
                    skip_runtime_bounds_check_because="the DMA itself checks its bounds")
                for k, page in enumerate(numbers):
                    eng.dma_start(dst[:, DS(at + (j + k), 1), :], pool[0, DS(page, 1)].rearrange("o p c g d -> p o (c g d)")
                                  ).then_inc(landed, 16)

        def group_loads(eng, g, k0, k1):
            with eng.Fori(k0, k1) as k:
                page_loads(eng, cpages[g], k * UP, (k + (PARTS[g][k0] - k0)) * UP, cache_cmp, q[f"dma_cpage{g % 2}"])

        @block.sync
        def _(sp):
            sp.dma_start(xin, x_prompt[0].rearrange("(t p) d -> p t d", p=128)).then_inc(dma_x, 16)
            sp.dma_start(xin_s, x_sample.rearrange("n q d -> (n q) d")).then_inc(dma_x, 16)
            sp.wait_ge(prow_clear, 1)
            rows = [(R_LN + 8 * n, a[0].rearrange("(a b) -> a b", b=128))
                    for n, a in enumerate((ln1_g, ln1_b, ln2_g, ln2_b, ln3_g, ln3_b))]
            rows.append((R_BC, b_in[0, 0:OFF_Q].rearrange("(a b) -> a b", b=128)))
            rows.append((R_BKV, b_in[0, OFF_KV:OFF_G].rearrange("(a b) -> a b", b=128)))
            rows.append((R_WC, w_conv[0].rearrange("i (a b) -> (i a) b", b=128)))
            for row, src in rows:
                sp.dma_start(prow[row:row + src.shape[0], :], src).then_inc(dma_par, 16)
            for g in range(G):
                sp.dma_start(prow[R_BQ:R_BQ + R, g * HD:g * HD + HD],
                             b_in[0, OFF_Q + g * R * HD:OFF_Q + (g + 1) * R * HD].rearrange("(r d) -> r d", d=HD)
                             ).then_inc(dma_par, 16)
            sp.dma_start(prow[R_BG:R_BG + 1, 0:BR * NH],
                         b_in[0, OFF_G:OFF_G + BR * NH].rearrange("(a b) -> a b", a=1)).then_inc(dma_par, 16)

            sp.dma_start(pages_sb[:], page_table.rearrange("(a n) g -> a (n g)", a=1)).then_inc(q["dma_first"], 16)
            for h in range(2):
                rows = slice(h * BLK, (h + 1) * BLK)
                for c in range(2):
                    sp.dma_start(w1[rows, c, :, :], cmp_w1[0, c]).then_inc(q["dma_cmp_w"], 16)
                sp.dma_start(w2[rows, :, :], cmp_w2[0].rearrange("c h d -> h c d")).then_inc(q["dma_first"], 16)
                sp.dma_start(pe_sb[rows, :, :], cmp_pe[0]).then_inc(q["dma_first"], 16)

            sp.wait_ge(q["dma_first"], 16 * 5)
            group_loads(sp, 0, 0, 2)
            sp.wait_ge(q["pe_summed"], 1)
            sp.wait_ge(q["x_by_act"], KC // 2)
            sp.wait_ge(q["x_by_dve"], KC // 2)
            group_loads(sp, 1, 0, 2)
            for g in range(2, GROUPS):
                sp.wait_ge(q["hid_in_psum"], g - 1)
                group_loads(sp, g, len(PARTS[g]) - 3, len(PARTS[g]) - 1)
            sp.wait_ge(q["hid_in_psum"], GROUPS - 1)
            group_loads(sp, GROUPS - 1, 0, 1)

            def ffn_loads(n, gate, up, down_w):
                phase = ("ffa", "ffb")[n]
                for half in range(2):
                    with sp.Fori(0, FH) as i:
                        for s, w in enumerate((gate, up)):
                            col = sp.snap((i + half * FH) * 128)
                            free = sp.snap(i + (USES[phase][s] + half * FH + ONE))
                            sp.wait_ge(w_lo[s], free)
                            sp.dma_start(graw[s][:], w[0].rearrange("(k p) f -> p k f", p=128)[:, :, DS(col, 128)]
                                         ).then_inc(dma_w[s], 16)
                    if n == 0 and half == 0:
                        sp.wait_ge(q["kc_in_psum"], GROUPS)
                    with sp.Fori(0, KC // 2) as i:
                        for s in range(2):
                            col = sp.snap((2 * i + s) * 128)
                            free = sp.snap(i + ((2 * n + half) * (KC // 2) + ONE))
                            sp.wait_ge(d_lo[s], free)
                            sp.dma_start(draw[s][:], down_w[0, half * FH * 128:(half + 1) * FH * 128, :].rearrange(
                                "(k p) f -> p k f", p=128)[:, :, DS(col, 128)]).then_inc(dma_d[s], 16)

            ffn_loads(0, ffa_gate, ffa_up, ffa_down)

            w_in_k = w_in[0].rearrange("(k p) f -> p k f", p=128)
            for t in range(NT):
                s = t % 2
                sp.wait_ge(w_lo[s], USES["proj"][s] + t // 2 + ONE)
                for part in range(2):
                    if ZC <= t < ZC + R:
                        c0 = OFF_Q + (part * R + t - ZC) * HD
                        dst, src = graw[s][:, :, part * HD:(part + 1) * HD], w_in_k[:, :, c0:c0 + HD]
                    else:
                        wide = BR * NH if t == NT - 1 else 128
                        k = slice(part * KC // 2, (part + 1) * KC // 2)
                        dst, src = graw[s][:, k, 0:wide], w_in_k[:, k, t * 128:t * 128 + wide]
                    sp.dma_start(dst, src).then_inc(dma_w[s], 16)

            sp.dma_start(crow[:], state_conv[0].rearrange("n i d -> (n i) d")).then_inc(q["dma_conv"], 16)
            sp.wait_ge(w_used[0], USES["proj"][0] + NT // 2 + 1)
            for c in range(2):
                for h in range(2):
                    sp.dma_start(w1p[h * BLK:(h + 1) * BLK, c, :, :], cmp_w1[0, c]).then_inc(q["dma_cmp_w"], 16)
            n_stored = 0
            for n in range(NB):
                sp.dma_start(s_win[0, n, 0:WIN - NQ].rearrange("p c g d -> p (c g d)"),
                             state_win[0, n, NQ:WIN].rearrange("p c g d -> p (c g d)")).then_inc(stored, 16)
                n_stored += 1
            sp.wait_ge(q["ctok_ready"], 1)
            sp.dma_start(p_conv[0, 0], ctok[NS - 2:NS, 0, :]).then_inc(q["state_stored"], 16)
            for n in range(NB):
                sp.dma_start(s_conv[0, n], ctok[n * NQ + 2:n * NQ + 4, 1, :]).then_inc(q["state_stored"], 16)
            sp.wait_ge(tok_out, QT + 1)
            for j, (prompt, sample) in enumerate(((p_cmp, s_cmp), (p_sel, s_sel), (p_win, s_win))):
                for t in range(QT):
                    sp.dma_start(prompt[0, 0, t * 128:(t + 1) * 128].rearrange("p c g d -> p (c g d)"),
                                 kvtok[:, t, 2 * j:2 * j + 2, :]).then_inc(stored, 16)
                    n_stored += 1
                if j < 2:
                    sp.dma_start(sample[0].rearrange("n q c g d -> (n q) (c g d)"),
                                 kvtok[0:NS, QT, 2 * j:2 * j + 2, :]).then_inc(stored, 16)
                    n_stored += 1
                else:
                    for n in range(NB):
                        sp.dma_start(sample[0, n, WIN - NQ:WIN].rearrange("q c g d -> q (c g d)"),
                                     kvtok[n * NQ:(n + 1) * NQ, QT, 2 * j:2 * j + 2, :]).then_inc(stored, 16)
                        n_stored += 1

            def sample_loads(b, i):
                sp.dma_start(win[b][:], state_win[0, DS(i * 2 + b, 1)].rearrange("o (c p) k g d -> p (o c) (k g d)", p=128)
                             ).then_inc(q[f"dma_win{b}"], 16)
                with sp.Fori(0, 2 - b) as k:
                    page_loads(sp, pages[b], k * UP, k * UP + (i * 2 + b) * NPG, cache_sel, q[f"dma_page{b}"])

            sp.wait_ge(q["hidp_in_psum"], 1)
            sample_loads(0, 0)
            sp.wait_ge(q["conv_ready"], 1)
            sample_loads(1, 0)
            sp.wait_ge(stored, 16 * n_stored)
            with sp.Fori(1, NB // 2) as i:
                for b in range(2):
                    free = sp.snap(i + ONE)
                    sp.wait_ge(q["dma_first"], 16 * 5)
                    sp.wait_ge(q[f"s_pv{b}"], free)
                    sample_loads(b, i)

            w_o = w_out[0]
            for t in range(KC):
                s = t % 2
                if t < 2:
                    sp.wait_ge(q[("comb_in_psum", "os_ready")[t]], 1)
                sp.wait_ge(w_lo[s], USES["out"][s] + t // 2 + ONE)
                cols = slice(t * 128, (t + 1) * 128)
                for g in range(G):
                    sp.dma_start(graw[s][g * HD:(g + 1) * HD, 0:R, :],
                                 w_o[g * R * HD:(g + 1) * R * HD, cols].rearrange("(r d) n -> d r n", d=HD)
                                 ).then_inc(dma_w[s], 16)
                sp.dma_start(graw[s][:, R:KC, :], w_o[DC:D, cols].rearrange("(k p) n -> p k n", p=128)
                             ).then_inc(dma_w[s], 16)

            ffn_loads(1, ffb_gate, ffb_up, ffb_down)

            for t in range(QT + 1):
                sp.wait_ge(q["y_by_act"], t + 1)
                sp.wait_ge(q["y_by_dve"], t + 1)
                if t < QT:
                    sp.dma_start(y_prompt[0, t * 128:(t + 1) * 128, :], yout[:, t, :]).then_inc(stored, 16)
                else:
                    sp.dma_start(y_sample.rearrange("n q d -> (n q) d"), yout[0:NS, t, :]).then_inc(stored, 16)
                n_stored += 1
            sp.wait_ge(q["state_stored"], 16 * (NB + 1))
            sp.wait_ge(stored, 16 * n_stored)

        @block.gpsimd
        def _(pool):
            steps = Steps(pool, pool_step)
            pool.memset(prow, 0.0).then_inc(prow_clear, 1)
            steps(pool.memset(ident[:], 0.0))
            steps(pool.memset(causal[:], 0.0))
            pool.memset(mean_w[:], 1.0 / D).then_inc(const_ready, 1)
            pool.memset(eps[:], EPS).then_inc(const_ready, 1)
            pool.memset(wbd[:, 1], 0.0).then_inc(q["zeros_ready"], 1)
            for tile in hid:
                pool.memset(tile, 0.0).then_inc(q["zeros_ready"], 1)
            for tile in (qbd, win_mask):
                pool.memset(tile[:], 0.0)
            pool.memset(new_mask[:], NEG)
            steps(pool.memset(blk_neg[:], 0.0))
            steps(pool.memset(blk_ok[:], 1.0))
            steps(pool.memset(diag[:], 1.0))
            steps.settle()
            pool.affine_select(out=ident[:], in_=ident[:], compare_op=ALU.not_equal, fill=1.0, base=0,
                               pattern=[[-1, 128]], channel_multiplier=1).then_inc(const_ready, 1)
            pool.affine_select(out=causal[:], in_=causal[:], compare_op=ALU.is_ge, fill=NEG, base=0,
                               pattern=[[-1, 128]], channel_multiplier=1).then_inc(const_ready, 1)
            pool.wait_ge(const_ready, 4)
            pool.tensor_copy(identb[:], ident[:]).then_inc(const_ready, 1)
            for tile, fill in ((blk_neg, NEG), (blk_ok, 0.0)):
                pool.affine_select(out=tile[:], in_=tile[:], compare_op=ALU.is_ge, fill=fill, base=1 - BLK,
                                   pattern=[[128, QT], [-BLK, 2], [-PAGE, QT]], channel_multiplier=1)
            steps(pool.affine_select(out=diag[:], in_=diag[:], compare_op=ALU.is_ge, fill=0.0, base=0,
                                     pattern=[[-8, R], [-8 * R, G]], channel_multiplier=1))
            steps.settle()
            pool.affine_select(out=diag[:], in_=diag[:], compare_op=ALU.is_ge, fill=0.0, base=7,
                               pattern=[[8, R], [8 * R, G]], channel_multiplier=-1).then_inc(const_ready, 1)
            def residual(n):
                for k in range(KC):
                    pool.wait_ge(norm_lo, n * KC + k + 1)
                    pool.tensor_scalar(x[:, k, :], x[:, k, :], ALPHA, None, ALU.mult).then_inc(q["residual"], 1)

            residual(0)
            pool.wait_ge(z_out[0], ZC // 2)
            pool.wait_ge(z_out[1], ZC // 2)
            for tile in (kcp, vbd, ptp):
                pool.memset(tile[:], 0.0)
            pool.memset(kd[:], 0.0).then_inc(q["pads_ready"], 1)
            steps(pool.tensor_tensor(zc[:, 4:8, :], zc[:, 4:8, :], zc[:, 8:12, :], ALU.mult)); steps.settle()
            pool.tensor_copy(sext[:, :, :, 2:2 + NQ], zc[:, 4:8, SEQ:T].rearrange("p t (n i) -> p t n i", i=NQ)
                             ).then_inc(q["u_ready"], 1)
            pool.wait_ge(q["u_ready"], 1)

            def taps(cols, source):
                for tap in (2, 1, 0):
                    for t in range(4):
                        u, first = source(t, tap)
                        out = (zc[:, 8 + t, :] if tap == 2 else tap_u[t % 2][:])[:, cols][:, first:]
                        if len(u.shape) == 3:
                            out = out.rearrange("p (n i) -> p n i", i=NQ)
                        wt = par[:, R_WC + 4 * tap + t:R_WC + 4 * tap + t + 1]
                        steps(pool.tensor_scalar(out, u, wt, None, ALU.mult))
                        if tap < 2 and t % 2:
                            steps.settle()
                            for k in range(2):
                                z = zc[:, 8 + t - 1 + k, cols][:, first:]
                                steps(pool.tensor_tensor(z, z, tap_u[k][:, cols][:, first:], ALU.add))
                            steps.settle()
                    steps.settle()

            taps(slice(0, SEQ), lambda t, tap: (zc[:, 4 + t, 0:SEQ - (2 - tap)], 2 - tap))
            pool.wait_ge(q["gates_ready"], 1)
            taps(slice(SEQ, T), lambda t, tap: (sext[:, t, :, tap:tap + NQ], 0))
            pool.tensor_tensor(yconv[:], zc[:, 0:4, :], zc[:, 8:12, :], ALU.mult).then_inc(q["conv_ready"], 1)
            pool.wait_ge(q["hidp_in_psum"], 1)
            pool.memset(qs[:], 0.0).then_inc(q["pads_ready"], 1)

            pool.wait_ge(q["dma_first"], 16 * 5)
            pool.wait_ge(q["conv_ready"], 1)
            page_loads(pool, pages[1], UP, NPG + UP, cache_sel, q["dma_page1_pool"])
            with pool.Fori(1, NB // 2) as i:
                free = pool.snap(i + ONE)
                pool.wait_ge(q["dma_first"], 16 * 5)
                pool.wait_ge(q["s_pv1"], free)
                page_loads(pool, pages[1], UP, i * (2 * NPG) + (NPG + UP), cache_sel, q["dma_page1_pool"])
            residual(1)

        @block.tensor
        def _(pe):
            count_from_one(pe, (*d_used, q["s_pv0"], q["s_pv1"], q["pv"], q["s_scores"], q["s_probs_t"]))

            def product(out, hi, lo, xhi, xlo, chunks, parts=None, last_h=None):
                last = None
                for k in range(chunks):
                    if parts is not None:
                        pe.wait_ge(norm_lo, parts + k + 1)
                    if last_h is not None and k == chunks - 1:
                        pe.wait_ge(hl_ready, last_h)
                    for a, b in ((hi, xhi), (hi, xlo), (lo, xhi)):
                        for h in range(2):
                            last = nc.tensor.matmul(
                                out[:, h, 0:HALF], a[:, k, :], b[:, k, h * HALF:(h + 1) * HALF],
                                start=(k == 0 and a is hi and b is xhi),
                                stop=(k == chunks - 1 and a is lo))
                return last

            pe.wait_ge(const_ready, 5)
            pe.wait_ge(dma_par, 16 * 12)
            nc.tensor.transpose(ps[:, 7, 0:128], prow, ident[:]).then_inc(small_in_psum, 1)
            pe.wait_ge(dma_x, 32)
            for k in range(KC):
                if k == 3:
                    pe.wait_ge(par_ready, 1)
                if k >= 4:
                    pe.wait_ge((q["x_by_act"], q["x_by_dve"])[k % 2], (k - 4) // 2 + 1)
                b = 2 * (k % 4)
                for t in range(QT):
                    nc.tensor.transpose(ps[:, b, t * 128:(t + 1) * 128], xin[:, t, k * 128:(k + 1) * 128], ident[:])
                nc.tensor.transpose(ps[:, b + 1, 0:NS], xin_s[:, k * 128:(k + 1) * 128],
                                    ident[0:NS, 0:NS]).then_inc(xt_in_psum, 1)

            def hidden_cached(g):
                if g >= 2:
                    pe.wait_ge(q["hid_ready"], g - 1)
                pe.wait_ge(q[f"dma_cpage{g % 2}"], sum(len(PARTS[k]) for k in range(g % 2, g + 1, 2)) * UP * 16)
                for d in range(HD):
                    for c in range(2):
                        col = c * 128 + d
                        last = nc.tensor.matmul(
                            ps[:, 2 * (g % 2) + c, 0:len(PARTS[g]) * UP * G], wbd[:, c, d, :, :].rearrange("p a h -> p (a h)"),
                            cpages[g][:, :, col:col + HD + 1:HD], start=(d == 0), stop=(d == HD - 1))
                last.then_inc(q["hid_in_psum"], 1)

            def compressed(p):
                pe.wait_ge(q["hid_ready"], p + 1)
                if p >= 2:
                    pe.wait_ge(q["kc_ready"], p - 1)
                for g in range(G):
                    nc.tensor.matmul(ps[g * HD:(g + 1) * HD, 4 + p % 2, 0:32 * len(PARTS[p])], w2[:, 0, :],
                                     hid[p % 2][:, 0, g, 0:len(PARTS[p]), :].rearrange("p u b -> p (u b)"), start=True, stop=True)
                for k, part in enumerate(PARTS[p]):
                    rows = slice(part % 2 * 32, part % 2 * 32 + 32)
                    for g in range(G):
                        last = nc.tensor.matmul(ps[rows, 6 + p % 2, k * 128 + g * HD:k * 128 + (g + 1) * HD],
                                                hid[p % 2][:, 1, g, k, :], w2[:, 1, :], start=True, stop=True)
                last.then_inc(q["kc_in_psum"], 1)

            def ffn_products(n):
                uses = USES[("ffa", "ffb")[n]]
                for half in range(2):
                    before = n * FT + half * FH

                    def tile(i, parts=None):
                        for s, (done, bank) in enumerate(((sg_ready, 0), (ht_ready, 2))):
                            pe.wait_ge(w_lo[s], i + (uses[s] + half * FH + 1) + ONE)
                            if parts is None:
                                pe.wait_ge(done, i + before + ONE)
                            product(ps[:, bank:bank + 2, :], ghi[s], glo[s], xh, xl, KC, parts if s == 0 else None
                                    ).then_inc(w_used[s], 1)

                    first = n == 1 and half == 0
                    if first:
                        pe.wait_ge(std_ready, 4)
                        tile(0, KC)
                    with pe.Fori(int(first), FH) as i:
                        tile(i)
                    pe.wait_ge(hl_ready, before + FH - 1 + ONE)
                    with pe.Fori(0, KC // 2) as i:
                        for s in range(2):
                            use = (2 * n + half) * (KC // 2)
                            pe.wait_ge(d_lo[s], i + (use + 1) + ONE)
                            pe.wait_ge(y_added[s], i + use + ONE)
                            product(ps[:, 4 + 2 * s:6 + 2 * s, :], dhi[s], dlo[s], hh, hl, FH,
                                    last_h=before + FH + ONE).then_inc(d_used[s], 1)

            def norm_products(n):
                pe.wait_ge(csum_step, (KC + 1) * (n + 1))
                for h in range(2):
                    nc.tensor.matmul(ps[:, h, 0:HALF], mean_w[:], csum[:, h * HALF:(h + 1) * HALF],
                                     start=True, stop=True).then_inc(mean_ready, 1)
                for h in range(2):
                    for k in range(KC):
                        if k % 4 == 0:
                            pe.wait_ge(sq_ready, 4 * n + 2 * h + k // 4 + 1)
                        last = nc.tensor.matmul(ps[:, 2 + h, 0:HALF], mean_w[:], sq[:, k, h * HALF:(h + 1) * HALF],
                                                start=(k == 0), stop=(k == KC - 1))
                    last.then_inc(var_ready, 1)

            pe.wait_ge(q["dma_first"], 16 * 5)
            pe.wait_ge(q["x_by_act"], KC // 2)
            pe.wait_ge(q["x_by_dve"], KC // 2)
            pe.wait_ge(q["pe_summed"], 1)
            for c in range(2):
                for h in range(2):
                    rows = slice(h * HD, (h + 1) * HD)
                    last = nc.tensor.matmul(ps[rows, 7, c:c + 1], pe_sum[rows, c, :], mean_w[rows, 0:1],
                                            start=True, stop=True)
            last.then_inc(small_in_psum, 1)
            pe.wait_ge(q["wbd_by_act"], 1)
            pe.wait_ge(q["wbd_by_dve"], 1)
            hidden_cached(0)
            pe.wait_ge(q["bias_ready"], 1)
            for g in range(1, GROUPS):
                hidden_cached(g)
                compressed(g - 1)
            compressed(GROUPS - 1)
            pe.wait_ge(q["x_lo"], KC // 2)
            pe.wait_ge(q["kc_ready"], GROUPS)
            ffn_products(0)
            norm_products(0)

            pe.wait_ge(std_ready, 2)
            for s in range(2):
                pe.wait_ge(w_lo[s], USES["proj"][s] + 1 + ONE)
                product(ps[:, 2 * s:2 * s + 2, :], ghi[s], glo[s], xh, xl, KC, 0 if s == 0 else None
                        ).then_inc(w_used[s], 1)
            with pe.Fori(1, NT // 2) as i:
                for s in range(2):
                    pe.wait_ge(w_lo[s], i + (USES["proj"][s] + 1) + ONE)
                    pe.wait_ge(z_out[s], i)
                    product(ps[:, 2 * s:2 * s + 2, :], ghi[s], glo[s], xh, xl, KC).then_inc(w_used[s], 1)
            pe.wait_ge(w_lo[0], USES["proj"][0] + NT // 2 + 1 + ONE)
            pe.wait_ge(z_out[0], NT // 2)
            product(ps[:, 0:2, :], ghi[0], glo[0], xh, xl, KC).then_inc(w_used[0], 1)

            pe.wait_ge(z_out[0], NT // 2 + 1)
            pe.wait_ge(z_out[1], NT // 2)
            for t in range(QT + 1):
                if t >= 2:
                    pe.wait_ge(tok_out, t - 1)
                w = 128 if t < QT else NS
                for j in range(6):
                    last = nc.tensor.transpose(ps[0:w, 4 + 2 * (t % 2) + j // 4, (j % 4) * 128:(j % 4 + 1) * 128],
                                               zr[:, KV0 + j, t * 128:t * 128 + w], ident[:])
                last.then_inc(tok_in_psum, 1)

            pe.wait_ge(q["u_ready"], 1)
            for k, c0 in enumerate((SEQ - NS, SEQ)):
                for t in range(4):
                    last = nc.tensor.transpose(ps[0:NS, 2 + k, t * 128:(t + 1) * 128],
                                               zc[:, 4 + t, c0:c0 + NS], ident[:])
            last.then_inc(q["ctok_in_psum"], 1)
            pe.wait_ge(q["qbd_ready"], 1)
            pe.wait_ge(q["masks_ready"], 1)
            for n in range(NB):
                last = nc.tensor.matmul(ps[32 * (n % 4):32 * (n % 4) + 32, 0, n // 4 * NBLK:(n // 4 + 1) * NBLK],
                                        qbd[:, n, :], kc_all[:, n, :], start=True, stop=True)
            last.then_inc(q["s_small_in_psum"], 1)
            for br in range(2):
                for nh in range(2):
                    out = ps[:, 1, (2 * br + nh) * NS:(2 * br + nh + 1) * NS]
                    nc.tensor.matmul(out, qbd[:, 4 * nh:4 * nh + 4, :].rearrange("p n r -> p (n r)"),
                                     zr[:, KV0 + 2 + 2 * br, SEQ:T], start=True, stop=False)
                    last = nc.tensor.matmul(out, identb[:], new_mask[:, nh, :], start=False, stop=True)
            last.then_inc(q["s_small_in_psum"], 1)
            pe.wait_ge(q["ctok_ready"], 1)
            for k in range(BR * R):
                nc.tensor.matmul(ps[:, 2, k * NS:(k + 1) * NS], gate_sel[k // 8][:, k % 8, :],
                                 zr[0:BR * NH, G0, SEQ:T], start=True, stop=True)
            for t in range(QT):
                nc.tensor.transpose(ps[:, 3, t * 32:t * 32 + BR * NH], zr[0:BR * NH, G0, t * 128:(t + 1) * 128],
                                    ident[0:BR * NH, 0:BR * NH])
            pe.wait_ge(q["dma_conv"], 16)
            for t in range(4):
                last = nc.tensor.transpose(ps[:, 3, 128 + t * 16:144 + t * 16], crow[:, t * 128:(t + 1) * 128],
                                           ident[0:16, 0:16])
            last.then_inc(q["gates_in_psum"], 1)

            pe.wait_ge(q["pcs_ready"], 1)
            pe.wait_ge(tok_out, QT + 1)
            nc.tensor.matmul(ps[:, 4, 0:128], same[:], pcs[:].rearrange("p n b -> p (n b)"), start=True, stop=True)
            for nh in range(2):
                last = nc.tensor.transpose(ps[0:NBLK, 5, nh * 128:(nh + 1) * 128], pcs[:, nh, :], ident[:])
            last.then_inc(q["imp_in_psum"], 1)

            pe.wait_ge(q["dma_cmp_w"], 16 * 8)
            pe.wait_ge(q["hid_operand_ready"], 1)
            for d in range(0, HD, 4):
                for c in range(2):
                    for h in range(2):
                        part = slice(c * 64 + h * 32, c * 64 + h * 32 + 32)
                        last = nc.tensor.matmul(ps[part, 6, 0:4 * HD], kd[:, h, c, d:d + 4, :].rearrange("p d x -> p (d x)"),
                                                w1p[:, c, d:d + 4, :], start=(d == 0), stop=(d == HD - 4))
            last.then_inc(q["hidx_in_psum"], 1)

            pe.wait_ge(q["sel_ready"], 1)
            pe.wait_ge(q["pct_ready"], 1)
            for n in range(NB):
                for c in range(CH):
                    last = nc.tensor.matmul(ps[32 * c:32 * c + 32, 5, n * 16:(n + 1) * 16],
                                            identb[:, 32 * (n % 4):32 * (n % 4) + 32],
                                            selneg[:, n // 4, c * 16:(c + 1) * 16], start=True, stop=True)
            last.then_inc(q["selt_in_psum"], 1)

            pe.wait_ge(q["hid_operand_ready"], 2)
            for c in range(2):
                for d in range(4):
                    kept = ident[:, c * 64:c * 64 + 64].rearrange("p (h d x) -> p d h x", h=2, d=4)[:, d]
                    last = nc.tensor.matmul(ps[c * HD:(c + 1) * HD, 7, 0:2 * QT * G], hidx[:, d * HD:(d + 1) * HD], kept,
                                            start=(d == 0), stop=(d == 3))
            last.then_inc(q["hidp_in_psum"], 1)
            pe.wait_ge(q["hidp_ready"], 1)
            for g in range(G):
                nc.tensor.matmul(ps[g * HD:(g + 1) * HD, 6, 0:8], w2[0:HD, 0, :], hidp[0:HD, :, :, g],
                                 start=True, stop=True)
            for g in range(G):
                last = nc.tensor.matmul(ps[0:8, 7, g * HD:(g + 1) * HD],
                                        hidp[HD:128, :, :, g].rearrange("p h a -> p (h a)"), w2[HD:128, 1, :],
                                        start=True, stop=True)
            last.then_inc(q["kcp_in_psum"], 1)

            pe.wait_ge(q["pct_ready"], 1)
            for n in range(NB):
                last = nc.tensor.matmul(ps[32 * (n % 4):32 * (n % 4) + 32, 0, n // 4 * 128:(n // 4 + 1) * 128],
                                        pct[:, n // 4, 32 * (n % 4):32 * (n % 4) + 32], vc_all[:, n, :],
                                        start=True, stop=True)
            last.then_inc(q["ocs_in_psum"], 1)

            pe.wait_ge(q["pnew_ready"], 1)
            for k in range(4):
                last = nc.tensor.transpose(ps[0:NS, 1, k * 128:(k + 1) * 128], pnew[:, k, :], ident[:])
            last.then_inc(q["pnewt_in_psum"], 1)

            pe.wait_ge(q["kcp_ready"], 1)
            nc.tensor.matmul(ps[0:64, 7, 0:128], rep8[:].rearrange("p x b -> p (x b)"), vcp[:],
                             start=True, stop=True).then_inc(q["rep_in_psum"], 1)
            pe.wait_ge(q["gates_ready"], 1)
            for g in range(G):
                for r in range(R):
                    last = nc.tensor.matmul(ps[32 * r:32 * r + 32, 2 + g, :], kcp[:, g, :],
                                            zr[:, r, 0:SEQ], start=True, stop=True)
            last.then_inc(q["spt_in_psum"], 1)

            pe.wait_ge(q["pnewt_ready"], 1)
            for k in range(4):
                last = nc.tensor.matmul(ps[:, 4, k * 128:(k + 1) * 128], pnt[:, k, :],
                                        kvtok[0:NS, QT, 3 + 2 * (k // 2), :], start=True, stop=True)
            last.then_inc(q["onew_in_psum"], 1)

            pe.wait_ge(q["spt_by_act"], 1)
            pe.wait_ge(q["spt_by_dve"], 1)
            for g in range(G):
                for t in range(QT):
                    last = nc.tensor.transpose(ps[:, 2 + g, t * 128:(t + 1) * 128], spt[:, g, t * 128:(t + 1) * 128],
                                               ident[:])
            last.then_inc(q["sp_in_psum"], 1)

            pe.wait_ge(q["pp_ready"], 1)
            for t in range(QT):
                last = nc.tensor.transpose(ps[0:64, 6, t * 128:(t + 1) * 128], w_cmp[:, t * 64:(t + 1) * 64], ident[:])
            last.then_inc(q["ptp_in_psum"], 1)
            pe.wait_ge(q["ptp_ready"], 1)
            pe.wait_ge(q["vbd_ready"], 1)
            pe.wait_ge(q["ocs_ready"], 1)
            pe.wait_ge(q["onew_ready"], 1)
            pe.wait_ge(q["selt_ready"], 1)
            for r in range(R):
                last = nc.tensor.matmul(ps[:, 4 + r, :], vbd[:, r, :, :].rearrange("p g d -> p (g d)"),
                                        ptp[:].rearrange("p t c -> p (t c)"), start=True, stop=True)
            last.then_inc(q["op_in_psum"], 1)

            units = [(t, br) for t in range(QT) for br in range(2)]
            U = len(units)
            def prompt_head(r):
                pe.wait_ge(q["qs_ready"], r + 1)
                for j in range(U + 3):
                    if j < U:
                        t, br = units[j]
                        if j >= 2:
                            pe.wait_ge(q["probs"], r * U + (j - 1))
                        for g in range(G):
                            bank = 2 * (j % 2) + g
                            nc.tensor.matmul(ps[:, bank, 0:(t + 1) * 128], qs[:, g, t * 128:(t + 1) * 128],
                                             zr[:, KV0 + 2 + 2 * br, 0:(t + 1) * 128], start=True, stop=True)
                            last = nc.tensor.matmul(ps[:, bank, t * 128:(t + 1) * 128], identb[:], causal[:],
                                                    start=False, stop=True, skip_group_check=True)
                        last.then_inc(q["scores"], 1)
                    if 2 <= j < U + 2:
                        k = j - 2
                        t, br = units[k]
                        if k == 0:
                            pe.wait_ge(q["op_ready"], 1)
                        pe.wait_ge(q["diag_ready"], r * U + (k + 1))
                        if k >= 1:
                            pe.wait_ge(q["pt_copied"], r * U + k)
                        for g in range(G):
                            for m in range(t + 1):
                                last = nc.tensor.matmul(ps[:, 4 + g, m * 128:(m + 1) * 128],
                                                        pp[k % 2][:, g, m * 128:(m + 1) * 128],
                                                        norm_diag[k % 2][:, g, :], start=True, stop=True)
                        last.then_inc(q["probs_t"], 1)
                    if j >= 3:
                        k = j - 3
                        t, br = units[k]
                        pe.wait_ge(q["pt_copied"], r * U + (k + 1))
                        for m in range(t + 1):
                            for g in range(G):
                                last = nc.tensor.matmul(ps[g * HD:(g + 1) * HD, 6, t * 128:(t + 1) * 128],
                                                        kvtok[:, m, 3 + 2 * br, g * HD:(g + 1) * HD],
                                                        ppt[k % 2][:, g, m * 128:(m + 1) * 128],
                                                        start=(br == 0 and m == 0), stop=(br == 1 and m == t))
                        last.then_inc(q["pv"], 1)

            def keys_t(b, i, n):
                pe.wait_ge(q[f"dma_page{b}"], (i + 1) * ((2 - b) * UP * 16))
                if b == 1:
                    pe.wait_ge(q["dma_page1_pool"], (i + 1) * (UP * 16))
                pe.wait_ge(q[f"dma_win{b}"], (i + 1) * 16)
                for m in range(9):
                    if m % 2 == 0:
                        pe.wait_ge(q["kt_by_act"], n * 5 + m // 2 + ONE)
                    else:
                        pe.wait_ge(q["kt_by_dve"], n * 4 + m // 2 + ONE)
                    for k in range(4):
                        src = pages[b][:, 4 * m + k, 0:128] if m < 8 else win[b][:, k, 0:128]
                        last = nc.tensor.transpose(ps[:, m % 2, k * 128:(k + 1) * 128], src, ident[:])
                    last.then_inc(q["kt_in_psum"], 1)

            def scores_s(b, n):
                pe.wait_ge(q["kt_by_act"], n * 5 + 5 + ONE)
                pe.wait_ge(q["kt_by_dve"], n * 4 + 4 + ONE)
                pe.wait_ge(q["qn_ready"], n + 1)
                pe.wait_ge(q["s_probs"], n + ONE)
                for h in range(2):
                    nc.tensor.matmul(ps[:, 2 + h, :], identb[:],
                                     selt[:, DS(n, 1), h * 8:(h + 1) * 8].rearrange("p o (k u) -> p (o k) u", u=1)
                                     .broadcast_to([128, 8, BLK]), start=True, stop=True, skip_group_check=True)
                nc.tensor.matmul(ps[:, 4, 0:128], identb[:], win_mask[:], start=True, stop=True,
                                 skip_group_check=True)
                for h in range(2):
                    for c in range(CH):
                        nc.tensor.matmul(ps[32 * c:32 * c + 32, 2 + h, :], qn[b][:],
                                         kt[:, c * 8 + h * 4:c * 8 + h * 4 + 4, :].rearrange("p k t -> p (k t)"),
                                         start=False, stop=True, skip_group_check=True)
                for c in range(CH):
                    last = nc.tensor.matmul(ps[32 * c:32 * c + 32, 4, 0:128], qn[b][:], kt[:, NPG + c, :],
                                            start=False, stop=True, skip_group_check=True)
                last.then_inc(q["s_scores"], 1)

            def values_s(b, n):
                pe.wait_ge(q["s_probs"], n + 1 + ONE)
                pe.wait_ge(q["s_o"], n + ONE)
                pe.wait_ge(q["s_pt_act"], n + ONE)
                pe.wait_ge(q["s_pt_dve"], n + ONE)
                for k in range(PC + 1):
                    last = nc.tensor.transpose(ps[:, 5 + k // 4, DS(k % 4 * 128 + 256 * (k // 8), 128)],
                                               pw[:, k, :], ident[:])
                last.then_inc(q["s_probs_t"], 1)
                pe.wait_ge(q["s_pt_act"], n + 1 + ONE)
                pe.wait_ge(q["s_pt_dve"], n + 1 + ONE)
                for k in range(PC):
                    for c in range(CH):
                        nc.tensor.matmul(ps[32 * c:32 * c + 32, 7, 0:128], pwt[:, k, 32 * c:32 * c + 32],
                                         pages[b][:, c * PC + k, 128:256], start=(k == 0), stop=(k == PC - 1))
                for c in range(CH):
                    last = nc.tensor.matmul(ps[32 * c:32 * c + 32, 7, 128:256], pwt[:, PC, 32 * c:32 * c + 32],
                                            win[b][:, c, 128:256], start=True, stop=True)
                last.then_inc(q[f"s_pv{b}"], 1)

            with pe.Fori(0, R) as r:
                prompt_head(r)
                keys_t(0, r, r * 2)
                scores_s(0, r * 2)
                keys_t(1, r, r * 2 + 1)
                scores_s(1, r * 2 + 1)
                pe.wait_ge(q["o_added"], r + 1)
                values_s(0, r * 2)
                values_s(1, r * 2 + 1)

            pe.wait_ge(q["s_o"], NB + ONE)
            nc.tensor.transpose(ps[0:16, 0, 0:128], cb[:, :, :, OB - 1].rearrange("p n b -> p (n b)"), ident[:]
                                ).then_inc(q["maxima_in_psum"], 1)
            pe.wait_ge(q["m_ready"], 1)
            nc.tensor.transpose(ps[:, 1, 0:16], neg_rep[:].rearrange("p c r -> p (c r)"), ident[0:16, 0:16]
                                ).then_inc(q["maxima_in_psum"], 1)
            pe.wait_ge(q["cb_scaled"], 1)
            for n in range(NB):
                last = nc.tensor.matmul(ps[32 * (n % 4):32 * (n % 4) + 32, 2 + n // 4, 0:2 * OB], fold[:],
                                        cb[:, n, :, :].rearrange("p b o -> p (b o)"), start=True, stop=True)
            last.then_inc(q["comb_in_psum"], 1)
            pe.wait_ge(q["ofin_ready"], 1)
            for nh in range(2):
                nc.tensor.transpose(ps[:, 4, nh * 128:(nh + 1) * 128], ocs[:, nh, :], ident[:])
                for br in range(2):
                    last = nc.tensor.transpose(ps[:, 5 + br, nh * 128:(nh + 1) * 128], ofin[:, nh, br, :], ident[:])
            last.then_inc(q["ofin_in_psum"], 1)
            pe.wait_ge(q["at_lo"], 3)
            for t in range(KC):
                s = t % 2
                pe.wait_ge(w_lo[s], USES["out"][s] + t // 2 + 1 + ONE)
                if t >= 2:
                    pe.wait_ge(q["out_added"], t - 1)
                product(ps[:, 2 * s:2 * s + 2, :], ghi[s], glo[s], xh, xl, KC).then_inc(w_used[s], 1)
            norm_products(1)
            ffn_products(1)
            norm_products(2)
            for t in range(QT + 1):
                if t in (0, HALF // 128):
                    pe.wait_ge(normed, (3 + (t > 0)) * KC)
                if t >= 2:
                    pe.wait_ge(q["y_by_act"], t - 1)
                    pe.wait_ge(q["y_by_dve"], t - 1)
                w = 128 if t < QT else NS
                for k in range(KC):
                    last = nc.tensor.transpose(ps[0:w, 4 + 2 * (t % 2) + k // 4, k % 4 * 128:(k % 4 + 1) * 128],
                                               x[:, k, t * 128:t * 128 + w], ident[:])
                last.then_inc(q["y_in_psum"], 1)

        @block.scalar
        def _(act):
            count_from_one(act, (sg_ready, hh_ready, q["kt_by_act"], q["s_probs"], q["s_pt_act"]))
            def split_w(s, use, fills):
                act.wait_ge(dma_w[s], fills)
                act.wait_ge(w_used[s], use)
                act.activation(ghi[s][:], graw[s][:], ACT.Copy).then_inc(w_hi[s], 1)

            def split_d(s, use):
                act.wait_ge(dma_d[s], use * 16 + 16)
                act.wait_ge(d_used[s], use + ONE)
                act.activation(dhi[s][:], draw[s][:], ACT.Copy).then_inc(d_hi[s], 1)

            for k in range(0, KC, 2):
                act.wait_ge(xt_in_psum, k + 1)
                b = 2 * (k % 4)
                act.activation(x[:, k, 0:SEQ], ps[:, b, :], ACT.Copy)
                act.activation(x[:, k, SEQ:T], ps[:, b + 1, 0:NS], ACT.Copy).then_inc(q["x_by_act"], 1)
            act.wait_ge(q["dma_cmp_w"], 16 * 4)
            act.wait_ge(q["zeros_ready"], 4)
            act.activation(wbd[BLK:128, :, :, 1, :], w1[BLK:128], ACT.Copy).then_inc(q["wbd_by_act"], 1)

            def ffn_gates(n):
                phase = ("ffa", "ffb")[n]
                uses, fills = USES[phase], FILLS[phase]
                for half in range(2):
                    before = n * FT + half * FH

                    def copy_h(j):
                        act.wait_ge(ht_ready, j + (before + 1) + ONE)
                        act.activation(hh[:, DS(j, 1), :], ht[:], ACT.Copy).then_inc(hh_ready, 1)

                    def tile(i, first):
                        if not (first and n == 1 and half == 0):
                            split_w(0, i + (uses[0] + half * FH), (i + (fills[0] + half * FH + 1)) * 16)
                            if not first:
                                copy_h(i - 1)
                            split_w(1, i + (uses[1] + half * FH), (i + (fills[1] + half * FH + 1)) * 16)
                        act.wait_ge(w_used[0], i + (uses[0] + half * FH + 1))
                        act.wait_ge(ht_ready, i + before + ONE)
                        act.activation(sg[:].rearrange("p (h t) -> p h t", h=2), ps[:, 0:2, 0:HALF], ACT.Silu
                                       ).then_inc(sg_ready, 1)

                    tile(0, True)
                    with act.Fori(1, FH) as i:
                        tile(i, False)
                    use = (2 * n + half) * (KC // 2)
                    split_d(0, use)
                    copy_h(FH - 1)
                    with act.Fori(0, KC // 2 - 1) as i:
                        split_d(1, i + use)
                        split_d(0, i + (use + 1))
                    split_d(1, use + KC // 2 - 1)

            def norm_scale(n):
                for h in range(2):
                    hs = slice(h * HALF, (h + 1) * HALF)
                    for k in range(0, KC, 4):
                        act.wait_ge(centered, 4 * n + 2 * h + k // 4 + 1)
                        act.activation(sq[:, k:k + 4, hs], x[:, k:k + 4, hs], ACT.Square).then_inc(sq_ready, 1)
                for s in ((0,), (0, 1), ())[n]:
                    phase = ("proj", "ffb")[n]
                    split_w(s, USES[phase][s], (FILLS[phase][s] + PER_FILL[phase]) * 16)
                for h in range(2):
                    hs = slice(h * HALF, (h + 1) * HALF)
                    act.wait_ge(var_ready, 2 * n + h + 1)
                    act.activation(rstd[:, hs], ps[:, 2 + h, 0:HALF], ACT.Sqrt, bias=eps[:]).then_inc(std_ready, 1)
                g, b = R_LN + 16 * n, R_LN + 16 * n + 8
                affine = lambda out, part, k: act.activation(out, part, ACT.Identity, scale=par[:, g + k:g + k + 1],
                                                             bias=par[:, b + k:b + k + 1])
                if n < 2:
                    for k in range(KC):
                        act.wait_ge(scaled, KC * n + k + 1)
                        affine(xh[:, k, :], x[:, k, :], k).then_inc(norm_hi, 1)
                        affine(x[:, k, :], x[:, k, :], k).then_inc(normed, 1)
                else:
                    for h in range(2):
                        for k in range(KC):
                            if k % 4 == 0:
                                act.wait_ge(scaled, KC * n + 2 * h + k // 4 + 1)
                            part = x[:, k, h * HALF:(h + 1) * HALF]
                            affine(part, part, k).then_inc(normed, 1)

            act.wait_ge(q["dma_first"], 16 * 5)
            act.wait_ge(q["x_by_act"], KC // 2)
            act.wait_ge(q["x_by_dve"], KC // 2)
            group_loads(act, 0, 2, 3)
            act.wait_ge(q["pe_summed"], 1)
            group_loads(act, 1, 2, 3)
            act.wait_ge(q["bias_ready"], 1)
            for p in range(GROUPS):
                act.wait_ge(q["hid_in_psum"], p + 1)
                if p >= 2:
                    act.wait_ge(q["kc_in_psum"], p - 1)
                for c in range(2):
                    for h in range(2):
                        rows = slice(h * HD, (h + 1) * HD)
                        for g in range(G):
                            last = act.activation(
                                hid[p % 2][rows, c, g, 0:len(PARTS[p]), h * UP:(h + 1) * UP],
                                ps[rows, 2 * (p % 2) + c, 0:32 * len(PARTS[p])].rearrange("p (u a g) -> p g u a", a=UP, g=G)[:, g],
                                ACT.Silu, bias=hid_bias[rows, c:c + 1])
                last.then_inc(q["hid_ready"], 1)
                if p + 2 < GROUPS:
                    group_loads(act, p + 2, len(PARTS[p + 2]) - 1, len(PARTS[p + 2]))
                if p == GROUPS - 2:
                    act.wait_ge(q["x_by_dve"], KC // 2)
                    for k in range(0, KC, 2):
                        act.activation(xh[:, k:k + 2, :], x[:, k:k + 2, :], ACT.Copy).then_inc(q["x_hi"], 1)
            act.wait_ge(q["kc_in_psum"], GROUPS)
            ffn_gates(0)
            norm_scale(0)

            def z_split(s, i):
                split_w(s, i + USES["proj"][s], (i * 2 + (FILLS["proj"][s] + 2)) * 16)

            def z_result(dst, col, s, i, func=ACT.Identity):
                act.wait_ge(w_used[s], i + (USES["proj"][s] + 1))
                act.activation(dst.rearrange("p o (h t) -> p (o h) t", h=2), ps[:, 2 * s:2 * s + 2, 0:HALF], func,
                               bias=par[:, DS(col, 1)]).then_inc(z_out[s], 1)

            with act.Fori(0, ZC // 2) as i:
                z_split(1, i)
                z_result(zc[:, DS(i * 2, 1), :], i * 2 + R_BC, 0, i)
                z_split(0, i + 1)
                z_result(zc[:, DS(i * 2 + 1, 1), :], i * 2 + (R_BC + 1), 1, i)
            with act.Fori(ZC // 2, NT // 2) as i:
                z_split(1, i)
                z_result(zr[:, DS(i * 2 - ZC, 1), :], i * 2 + R_BC, 0, i)
                z_split(0, i + 1)
                z_result(zr[:, DS(i * 2 - (ZC - 1), 1), :], i * 2 + (R_BC + 1), 1, i)
            z_result(zr[:, G0:G0 + 1, :], R_BG, 0, NT // 2, ACT.Sigmoid)

            act.wait_ge(q["maxima_ready"], 1)
            for nh in range(2):
                last = act.activation(pcs[:, nh, :], ps[:, 0, nh * NBLK:(nh + 1) * NBLK], ACT.Exp,
                                      bias=small[:, C_NCM + nh:C_NCM + nh + 1],
                                      accum_out=small[:, C_CSUM + nh:C_CSUM + nh + 1])
            last.then_inc(q["ecmp_ready"], 1)
            act.wait_ge(q["maxima_ready"], 2)
            for k in range(4):
                last = act.activation(pnew[:, k, :], ps[:, 1, k * NS:(k + 1) * NS], ACT.Exp,
                                      bias=small[:, C_NNM + k:C_NNM + k + 1],
                                      accum_out=small[:, C_NSUM + k:C_NSUM + k + 1])
            last.then_inc(q["pnew_ready"], 1)
            act.wait_ge(q["hidp_in_psum"], 1)
            act.activation(hidp[:].rearrange("p h a g -> p (h a g)"), ps[:, 7, 0:2 * QT * G], ACT.Silu,
                           bias=hid_bias[:, 2:3]).then_inc(q["hidp_ready"], 1)
            act.wait_ge(q["spt_in_psum"], 1)
            act.activation(spt[:, 0, :], ps[:, 2, :], ACT.Copy).then_inc(q["spt_by_act"], 1)
            act.wait_ge(q["sp_shifted"], 1)
            act.activation(w_cmp, w_cmp, ACT.Exp).then_inc(q["ep_ready"], 1)
            act.wait_ge(q["op_in_psum"], 1)
            act.activation(po[:], ps[:, 4:8, :], ACT.Copy).then_inc(q["op_ready"], 1)

            units = [(t, br) for t in range(QT) for br in range(2)]
            U = len(units)
            def prompt_head(r):
                act.wait_ge(q["s_pv0"], r + ONE)
                act.wait_ge(q["s_pv1"], r + ONE)
                for j in range(U + 2):
                    if j >= 2:
                        k = j - 2
                        t, br = units[k]
                        act.wait_ge(q["probs_t"], r * U + (k + 1))
                        act.wait_ge(q["pv"], r * U + max(k - 1, 0) + ONE)
                        act.activation(ppt[k % 2][:, :, 0:(t + 1) * 128], ps[:, 4:6, 0:(t + 1) * 128], ACT.Copy
                                       ).then_inc(q["pt_copied"], 1)
                    if j < U:
                        t, br = units[j]
                        act.wait_ge(q["negmax"], r * U + (j + 1))
                        for g in range(G):
                            col = 2 * j + g
                            last = act.activation(pp[j % 2][:, g, 0:(t + 1) * 128], ps[:, 2 * (j % 2) + g, 0:(t + 1) * 128],
                                                  ACT.Exp, bias=small[:, C_PNM + col:C_PNM + col + 1],
                                                  accum_out=small[:, C_PSUM + col:C_PSUM + col + 1])
                        last.then_inc(q["probs"], 1)

            def keys_s(n):
                for m in range(0, 9, 2):
                    act.wait_ge(q["kt_in_psum"], n * 9 + (m + 1))
                    if m == 0:
                        act.wait_ge(q["s_scores"], n + ONE)
                    act.activation(kt[:, 4 * m:4 * m + 4, :].rearrange("p k t -> p (k t)"), ps[:, 0, :], ACT.Copy
                                   ).then_inc(q["kt_by_act"], 1)

            def probs_s(b, n):
                act.wait_ge(q["s_negmax"], n + 1)
                act.wait_ge(q["s_probs_t"], n + ONE)
                act.activation(pw[:, 0:PC, :].rearrange("p k t -> p (k t)"), ps[:, 2:4, :].rearrange("p b t -> p (b t)"),
                               ACT.Exp, bias=cb[:, DS(n, 1), 0, OB - 1], accum_out=cb[:, DS(n, 1), 0, OB - 2])
                act.activation(pw[:, PC, :], ps[:, 4, 0:128], ACT.Exp, bias=cb[:, DS(n, 1), 1, OB - 1],
                               accum_out=cb[:, DS(n, 1), 1, OB - 2]).then_inc(q["s_probs"], 1)

            def probs_t_s(b, i, n):
                act.wait_ge(q["s_probs_t"], n + 1 + ONE)
                act.activation(pwt[:, 4:8, :].rearrange("p k t -> p (k t)"), ps[:, 6, :], ACT.Copy)
                act.activation(pwt[:, 8, :], ps[:, 7, 256:384], ACT.Copy).then_inc(q["s_pt_act"], 1)

            act.wait_ge(q["state_stored"], 16 * (NB + 1))
            with act.Fori(0, R) as r:
                prompt_head(r)
                act.wait_ge(q["pv"], (r + 1) * U + ONE)
                keys_s(r * 2)
                probs_s(0, r * 2)
                keys_s(r * 2 + 1)
                probs_t_s(0, r, r * 2)
                probs_s(1, r * 2 + 1)
                probs_t_s(1, r, r * 2 + 1)

            act.wait_ge(q["s_pv0"], R + ONE)
            act.wait_ge(q["conv_ready"], 1)
            act.activation(xh[:, R:KC, :], yconv[:], ACT.Copy).then_inc(q["at_hi"], 1)
            act.wait_ge(q["o_added"], R)
            act.activation(xh[:, 0:R, 0:SEQ], po[:], ACT.Copy).then_inc(q["at_hi"], 1)

            act.wait_ge(q["exponents_ready"], 1)
            act.activation(chunk_w[:], chunk_w[:], ACT.Exp).then_inc(q["powers_ready"], 1)
            act.wait_ge(q["exponents_ready"], 2)
            act.activation(small[:, C_F:C_F + 8], small[:, C_F:C_F + 8], ACT.Exp).then_inc(q["powers_ready"], 1)

            act.wait_ge(q["os_ready"], 1)
            act.activation(xh[:, 0:R, SEQ:T], os_sum[:].rearrange("p r n q -> p r (n q)"), ACT.Copy
                           ).then_inc(q["at_hi"], 1)

            for t in range(KC):
                s = t % 2
                if t < 2:
                    act.wait_ge(q["at_lo"], 2)
                split_w(s, USES["out"][s] + t // 2, (FILLS["out"][s] + 3 * (t // 2 + 1)) * 16)
            norm_scale(1)
            ffn_gates(1)
            norm_scale(2)
            for t in range(QT + 1):
                w = 128 if t < QT else NS
                act.wait_ge(q["y_in_psum"], t + 1)
                act.activation(yout[0:w, t, 0:512], ps[0:w, 4 + 2 * (t % 2), :], ACT.Copy).then_inc(q["y_by_act"], 1)

        @block.vector
        def _(dve):
            count_from_one(dve, (*w_lo, *d_lo, *y_added, ht_ready, hl_ready, q["kt_by_dve"], q["s_o"], q["s_pt_dve"]))
            steps = Steps(dve, dve_step)
            def split_w(s, use):
                dve.wait_ge(w_hi[s], use + 1)
                dve.tensor_tensor(glo[s][:], graw[s][:], ghi[s][:].bitcast(F32), ALU.subtract).then_inc(w_lo[s], 1)

            def split_d(s, use):
                dve.wait_ge(d_hi[s], use + 1)
                dve.tensor_tensor(dlo[s][:], draw[s][:], dhi[s][:].bitcast(F32), ALU.subtract).then_inc(d_lo[s], 1)

            dve.memset(wbd[:, 0], 0.0).then_inc(q["zeros_ready"], 1)
            dve.wait_ge(const_ready, 6)
            F = C_F
            by_head = ident[:].rearrange("p (x r q) -> p x q r", r=R, q=NQ)
            steps(dve.tensor_reduce(small[:, F:F + 32].rearrange("p (x q) -> p x q", q=NQ), by_head, AX, ALU.add))
            dve.tensor_reduce(fold[:], ident[:].rearrange("p (c r) -> p r c", c=CH), AX, ALU.add)
            steps.settle()
            dve.tensor_copy(same[:].rearrange("p (x r q) -> p x r q", r=R, q=NQ),
                            small[:, F:F + 32].rearrange("p (x o q) -> p x o q", o=1, q=NQ).broadcast_to([128, 8, R, NQ]))
            steps(dve.tensor_reduce(small[:, 0:NQ], ident[:, 0:NS].rearrange("p (x q) -> p q x", q=NQ), AX, ALU.add))
            steps(dve.tensor_reduce(small[:, 16:32].rearrange("p (n q) -> p n q", q=NQ),
                                    ident[:].rearrange("p (n x q) -> p n q x", n=4, q=NQ), AX, ALU.add))
            steps.settle()
            for k in range(NQ):
                steps(dve.tensor_reduce(small[:, 4 + k:5 + k], small[:, k:NQ], AX, ALU.add))
                steps(dve.tensor_reduce(small[:, 32:48].rearrange("p (n k) -> p n k", k=NQ)[:, :, k],
                                        small[:, 16:32].rearrange("p (n q) -> p n q", q=NQ)[:, :, k:NQ], AX, ALU.add))
            steps.settle()
            dve.tensor_scalar(win_mask[:, 0:NQ], small[:, 4:8], NEG, None, ALU.mult)
            for nh in range(2):
                last = dve.tensor_scalar(new_mask[:, nh, 16 * nh:16 * nh + 16], small[:, 32:48], -1.0, -NEG,
                                         ALU.add, ALU.mult)
            last.then_inc(q["masks_ready"], 1)

            dve.wait_ge(small_in_psum, 1)
            dve.tensor_copy(par[:], ps[:, 7, 0:96]).then_inc(par_ready, 1)
            for k in range(1, KC, 2):
                dve.wait_ge(xt_in_psum, k + 1)
                b = 2 * (k % 4)
                dve.tensor_copy(x[:, k, 0:SEQ], ps[:, b, :])
                dve.tensor_copy(x[:, k, SEQ:T], ps[:, b + 1, 0:NS]).then_inc(q["x_by_dve"], 1)
            dve.wait_ge(q["dma_cmp_w"], 16 * 4)
            dve.wait_ge(q["zeros_ready"], 4)
            dve.tensor_copy(wbd[0:BLK, :, :, 0, :], w1[0:BLK]).then_inc(q["wbd_by_dve"], 1)
            dve.wait_ge(q["dma_first"], 16 * 5)
            dve.wait_ge(q["wbd_by_dve"], 1)
            dve.wait_ge(q["wbd_by_act"], 1)
            steps(dve.tensor_tensor(w1, w1, pe_sb[:].rearrange("p c (d o) -> p c d o", o=1).broadcast_to(
                [128, 2, HD, HD]), ALU.mult)); steps.settle()
            for c in range(2):
                last = dve.tensor_reduce(pe_sum[:, c, :], w1[:, c].rearrange("p d h -> p h d"), AX, ALU.add)
            last.then_inc(q["pe_summed"], 1)
            dve.wait_ge(small_in_psum, 2)
            dve.tensor_scalar(hid_bias[:, 0:2], ps[:, 7, 0:2], float(D), None, ALU.mult)
            dve.tensor_scalar(hid_bias[0:HD, 2:3], ps[0:HD, 7, 0:1], float(D), None, ALU.mult)
            dve.tensor_scalar(hid_bias[HD:128, 2:3], ps[HD:128, 7, 1:2], float(D), None, ALU.mult
                              ).then_inc(q["bias_ready"], 1)
            for p in range(GROUPS):
                dve.wait_ge(q["kc_in_psum"], p + 1)
                for k, n in enumerate(PARTS[p]):
                    n, part = divmod(n, 2)
                    rows = slice(part * 32, part * 32 + 32)
                    dve.tensor_copy(kc_all[:, n, rows], ps[:, 4 + p % 2, k * 32:(k + 1) * 32])
                    last = dve.tensor_copy(vc_all[rows, n, :], ps[rows, 6 + p % 2, k * 128:(k + 1) * 128])
                last.then_inc(q["kc_ready"], 1)
                if p == GROUPS - 3:
                    dve.wait_ge(q["x_by_act"], KC // 2)
                    dve.wait_ge(q["x_by_dve"], KC // 2)
                    for j in range(KC // 2):
                        part = slice(2 * j, 2 * j + 2)
                        dve.wait_ge(q["x_hi"], j + 1)
                        dve.tensor_tensor(xl[:, part, :], x[:, part, :], xh[:, part, :].bitcast(F32), ALU.subtract
                                          ).then_inc(q["x_lo"], 1)
                        dve.wait_ge(q["x_lo"], j + 1)
                        steps(dve.tensor_scalar(x[:, part, :], x[:, part, :], ALPHA, None, ALU.mult))
                    steps.settle()

            def ffn_values(n):
                uses = USES[("ffa", "ffb")[n]]
                for half in range(2):
                    before = n * FT + half * FH

                    def gated(j):
                        dve.wait_ge(w_used[1], j + (uses[1] + half * FH + 1))
                        dve.wait_ge(sg_ready, j + (before + 1) + ONE)
                        dve.wait_ge(hh_ready, j + before + ONE)
                        dve.wait_ge(hl_ready, j + before + ONE)
                        dve.tensor_tensor(ht[:].rearrange("p (h t) -> p h t", h=2), ps[:, 2:4, 0:HALF],
                                          sg[:].rearrange("p (h t) -> p h t", h=2), ALU.mult).then_inc(ht_ready, 1)
                        dve.wait_ge(ht_ready, j + (before + 1) + ONE)
                        dve.wait_ge(hh_ready, j + (before + 1) + ONE)
                        dve.tensor_tensor(hl[:, DS(j, 1), :], ht[:], hh[:, DS(j, 1), :].bitcast(F32),
                                          ALU.subtract).then_inc(hl_ready, 1)

                    if n == 0 and half == 0:
                        split_w(0, uses[0])
                        split_w(1, uses[1])
                    with dve.Fori(1, FH) as i:
                        split_w(0, i + (uses[0] + half * FH))
                        gated(i - 1)
                        split_w(1, i + (uses[1] + half * FH))
                    use = (2 * n + half) * (KC // 2)
                    split_d(0, use)
                    gated(FH - 1)

                    if half == 1:
                        dve.memset(csum[:], 0.0).then_inc(csum_step, 1)

                    def add_y(s, i):
                        dve.wait_ge(d_used[s], i + (use + 1) + ONE)
                        xt = x[:, DS(i * 2 + s, 1), :].rearrange("p o (h t) -> p (o h) t", h=2)
                        dve.scalar_tensor_tensor(xt, ps[:, 4 + 2 * s:6 + 2 * s, 0:HALF], 0.5, xt, ALU.mult, ALU.add
                                                 ).then_inc(y_added[s], 1)
                        if half == 1:
                            dve.wait_ge(y_added[s], i + (use + 1) + ONE)
                            dve.wait_ge(csum_step, i * 2 + ((2 * n) * (KC + 1) + s + 1))
                            dve.tensor_tensor(csum[:].rearrange("p (o t) -> p o t", o=1), x[:, DS(i * 2 + s, 1), :],
                                              csum[:].rearrange("p (o t) -> p o t", o=1), ALU.add
                                              ).then_inc(csum_step, 1)

                    if n == 1 and half == 0:
                        dve.wait_ge(q["residual"], 2 * KC)
                    with dve.Fori(0, KC // 2 - 1) as i:
                        split_d(1, i + use)
                        add_y(0, i)
                        split_d(0, i + (use + 1))
                        add_y(1, i)
                    split_d(1, use + KC // 2 - 1)
                    if half == 0:
                        split_w(0, uses[0] + FH)
                        split_w(1, uses[1] + FH)
                    add_y(0, KC // 2 - 1)
                    add_y(1, KC // 2 - 1)

            def norm_values(n):
                for h in range(2):
                    hs = slice(h * HALF, (h + 1) * HALF)
                    dve.wait_ge(mean_ready, 2 * n + h + 1)
                    for k in range(0, KC, 4):
                        dve.tensor_tensor(x[:, k:k + 4, hs], x[:, k:k + 4, hs],
                                          ps[:, h:h + 1, 0:HALF].broadcast_to([128, 4, HALF]), ALU.subtract
                                          ).then_inc(centered, 1)
                for s in ((0,), (0, 1), ())[n]:
                    split_w(s, USES[("proj", "ffb")[n]][s])
                dve.wait_ge(centered, 4 * n + 4)
                for h in range(2):
                    hs = slice(h * HALF, (h + 1) * HALF)
                    dve.wait_ge(std_ready, 2 * n + h + 1)
                    steps(dve.reciprocal(rstd[:, hs], rstd[:, hs]))
                    if n == 2:
                        steps.settle()
                        wide = rstd[:, hs].rearrange("p (o t) -> p o t", o=1).broadcast_to([128, 4, HALF])
                        for k in range(0, KC, 4):
                            dve.tensor_tensor(x[:, k:k + 4, hs], x[:, k:k + 4, hs], wide, ALU.mult).then_inc(scaled, 1)
                if n < 2:
                    steps.settle()

                    def low(k):
                        dve.wait_ge(norm_hi, KC * n + k + 1)
                        dve.wait_ge(normed, KC * n + k + 1)
                        dve.tensor_tensor(xl[:, k, :], x[:, k, :], xh[:, k, :].bitcast(F32), ALU.subtract
                                          ).then_inc(norm_lo, 1)

                    for k in range(KC):
                        dve.tensor_tensor(x[:, k, :], x[:, k, :], rstd[:], ALU.mult).then_inc(scaled, 1)
                        if k >= 2:
                            low(k - 2)
                    low(KC - 2)
                    low(KC - 1)

            ffn_values(0)
            norm_values(0)
            with dve.Fori(0, NT // 2) as i:
                split_w(1, i + USES["proj"][1])
                split_w(0, i + (USES["proj"][0] + 1))

            for t in range(QT + 1):
                w = 128 if t < QT else NS
                dve.wait_ge(tok_in_psum, t + 1)
                b = 4 + 2 * (t % 2)
                dve.tensor_copy(kvtok[0:w, t, 0:4, :], ps[0:w, b, :].rearrange("p (j c) -> p j c", j=4))
                dve.tensor_copy(kvtok[0:w, t, 4:6, :], ps[0:w, b + 1, 0:256].rearrange("p (j c) -> p j c", j=2)
                                ).then_inc(tok_out, 1)

            dve.wait_ge(tok_out, QT)
            dve.wait_ge(q["pads_ready"], 1)
            for h in range(2):
                rows = slice(h * BLK, (h + 1) * BLK)
                for c in range(2):
                    last = dve.tensor_copy(kd[rows, h, c].rearrange("p d (a g) -> p d a g", g=G),
                                           kvtok[rows, 0:QT, c, :].rearrange("p a (g d) -> p d a g", g=G))
            last.then_inc(q["hid_operand_ready"], 1)
            dve.tensor_copy(rep8[:], ident[0:8, 0:8].rearrange("p (o b) -> p o b", o=1).broadcast_to([8, NH, 8]))
            for br in range(BR):
                dve.tensor_copy(
                    gate_sel[br // 2][:, br % 2 * R:(br % 2 + 1) * R, :].rearrange("p r (g d) -> p r g d", g=G),
                    ident[0:BR * NH, br * NH:(br + 1) * NH].rearrange("p (g r o) -> p r g o", g=G, o=1).broadcast_to(
                        [BR * NH, R, G, HD]))
            for g in range(G):
                gp = slice(g * HD, (g + 1) * HD)
                last = dve.tensor_scalar(
                    qbd[gp, :, g * 16:(g + 1) * 16].rearrange("p n (r q) -> p n r q", q=NQ),
                    zr[gp, 0:R, SEQ:T].rearrange("p r (n q) -> p n r q", q=NQ), SCALE, None, ALU.mult)
            last.then_inc(q["qbd_ready"], 1)

            dve.wait_ge(q["ctok_in_psum"], 1)
            dve.tensor_copy(ctok[:, 0, :], ps[0:NS, 2, :])
            dve.tensor_copy(ctok[:, 1, :], ps[0:NS, 3, :]).then_inc(q["ctok_ready"], 1)
            dve.wait_ge(q["s_small_in_psum"], 1)
            dve.tensor_reduce(small[:, C_NCM:C_NCM + 2], ps[:, 0, 0:128].rearrange("p (n b) -> p n b", b=NBLK), AX,
                              ALU.max, negate=True).then_inc(q["maxima_ready"], 1)
            dve.wait_ge(q["s_small_in_psum"], 2)
            dve.tensor_reduce(small[:, C_NNM:C_NNM + 4], ps[:, 1, 0:128].rearrange("p (n b) -> p n b", b=NS), AX,
                              ALU.max, negate=True).then_inc(q["maxima_ready"], 1)
            dve.memset(one[:], 1.0)
            dve.wait_ge(q["ecmp_ready"], 1)
            steps(dve.reciprocal(small[:, C_CSUM:C_CSUM + 2], small[:, C_CSUM:C_CSUM + 2]))
            steps.settle()
            for nh in range(2):
                last = dve.tensor_scalar(pcs[:, nh, :], pcs[:, nh, :], small[:, C_CSUM + nh:C_CSUM + nh + 1], None,
                                         ALU.mult)
            last.then_inc(q["pcs_ready"], 1)
            dve.wait_ge(q["gates_in_psum"], 1)
            dve.tensor_copy(gate_s[:].rearrange("p k n -> p (k n)"), ps[:, 2, 0:BR * R * NS])
            dve.tensor_copy(sext[:, :, :, 0:2], ps[:, 3, 128:192].rearrange("p (t n i) -> p t n i", t=4, i=2))
            steps(dve.tensor_copy(gate_p[:], ps[:, 3, 0:128].rearrange("p (t k) -> p t k", t=QT)[:, :, 0:BR * NH]))
            steps.settle()
            dve.engine_nop().then_inc(q["gates_ready"], 1)

            dve.wait_ge(q["imp_in_psum"], 1)
            dve.tensor_copy(pct[:].rearrange("p n r -> p (n r)"), ps[0:NBLK, 5, 0:256]).then_inc(q["pct_ready"], 1)
            for nh in range(2):
                steps(dve.tensor_copy(imp[:, nh, :].rearrange("p (j a h) -> p j h a", j=2, h=2),
                                      ps[:, 4, nh * NBLK:(nh + 1) * NBLK].rearrange("p (j h a) -> p j h a", j=2, h=2)))

            steps.settle()
            mid_blocks = slice(1, NBLK - 1)
            picks = N_SEL - 3
            both = range(2)
            cand = [imp[:, nh, mid_blocks] for nh in both]
            others = [rest[:, nh, mid_blocks] for nh in both]
            m1 = [small[:, C_M1 + 8 * nh:C_M1 + 8 * nh + 8] for nh in both]
            m2 = [small[:, C_M2 + 8 * nh:C_M2 + 8 * nh + 8] for nh in both]
            cnt = [small[:, C_CNT + nh:C_CNT + nh + 1] for nh in both]
            last_in = [m2[nh][:, picks - 9:picks - 8] for nh in both]
            for nh in both:
                steps(dve.max(m1[nh], cand[nh]))
            steps.settle()
            for nh in both:
                steps(dve.match_replace(others[nh], m1[nh], cand[nh], -1.0))
            steps.settle()
            for nh in both:
                steps(dve.max(m2[nh], others[nh]))
            steps.settle()
            for nh in both:
                steps(dve.tensor_scalar(gt[:, nh, mid_blocks], cand[nh], last_in[nh], None, ALU.is_gt, ALU.add,
                                        accum_out=cnt[nh]))
                steps(dve.tensor_scalar(eq[:, nh, mid_blocks], cand[nh], last_in[nh], None, ALU.is_equal))
            steps.settle()
            for nh in both:
                steps(dve.tensor_scalar(cnt[nh], cnt[nh], -1.0, float(picks), ALU.mult, ALU.add))
                steps(dve.tensor_tensor_scan(pre[:, nh, mid_blocks], one[:, mid_blocks], eq[:, nh, mid_blocks], 0.0,
                                             ALU.mult, ALU.add))
            steps.settle()
            for nh in both:
                steps(dve.scalar_tensor_tensor(others[nh], pre[:, nh, mid_blocks], cnt[nh], eq[:, nh, mid_blocks],
                                               ALU.is_le, ALU.mult))
            steps.settle()
            steps(dve.tensor_tensor(gt[:, :, mid_blocks], gt[:, :, mid_blocks], rest[:, :, mid_blocks], ALU.add))
            steps.settle()
            dve.memset(selneg[:, :, 0:NBLK:NBLK - 1], 0.0)
            dve.tensor_scalar(selneg[:, :, mid_blocks], gt[:, :, mid_blocks], -1.0, -NEG, ALU.add, ALU.mult
                              ).then_inc(q["sel_ready"], 1)

            dve.wait_ge(q["hidx_in_psum"], 1)
            dve.tensor_copy(hidx, ps[:, 6, 0:4 * HD]).then_inc(q["hid_operand_ready"], 1)
            dve.wait_ge(q["selt_in_psum"], 1)
            dve.tensor_copy(selt[:].rearrange("p n b -> p (n b)"), ps[:, 5, 0:128]).then_inc(q["selt_ready"], 1)

            dve.wait_ge(q["kcp_in_psum"], 1)
            for g in range(G):
                gp = slice(g * HD, (g + 1) * HD)
                dve.tensor_scalar(kcp[gp, g, 0:8], ps[gp, 6, 0:8], SCALE, None, ALU.mult)
            dve.tensor_copy(vcp[:], ps[0:8, 7, 0:128]).then_inc(q["kcp_ready"], 1)
            dve.wait_ge(q["ocs_in_psum"], 1)
            dve.tensor_copy(ocs[:].rearrange("p n d -> p (n d)"), ps[:, 0, 0:256]).then_inc(q["ocs_ready"], 1)
            dve.wait_ge(q["pnewt_in_psum"], 1)
            dve.tensor_copy(pnt[:].rearrange("p k r -> p (k r)"), ps[0:NS, 1, :]).then_inc(q["pnewt_ready"], 1)
            dve.wait_ge(q["rep_in_psum"], 1)
            dve.tensor_tensor(vbd[0:64], ps[0:64, 7, 0:128].rearrange("p (o g d) -> p o g d", o=1, g=G).broadcast_to(
                [64, R, G, HD]), diag[:].rearrange("p r (g o) -> p r g o", o=1).broadcast_to([64, R, G, HD]), ALU.mult
                ).then_inc(q["vbd_ready"], 1)

            dve.wait_ge(q["spt_in_psum"], 1)
            dve.tensor_copy(spt[:, 1, :], ps[:, 3, :]).then_inc(q["spt_by_dve"], 1)
            dve.wait_ge(q["sp_in_psum"], 1)
            w_p = w_cmp
            by_row = w_p.rearrange("p (x b) -> p x b", b=8)
            for g in range(G):
                steps(dve.tensor_tensor(
                    w_p.rearrange("p (t g r b) -> p t g r b", t=QT, g=G, r=R)[:, :, g, :, :],
                    ps[:, 2 + g, :].rearrange("p (t r b) -> p t r b", t=QT, r=R)[:, :, :, 0:8],
                    blk_neg[:].rearrange("p t (o b) -> p t o b", o=1).broadcast_to([128, QT, R, 8]), ALU.add))
            steps.settle()
            mx = small[:, C_MX:C_MX + 32]
            wide = mx.rearrange("p (x o) -> p x o", o=1).broadcast_to([128, 32, 8])
            steps(dve.tensor_reduce(mx, by_row, AX, ALU.max)); steps.settle()
            dve.tensor_tensor(by_row, by_row, wide, ALU.subtract).then_inc(q["sp_shifted"], 1)
            dve.wait_ge(q["ep_ready"], 1)
            steps(dve.tensor_tensor(w_p.rearrange("p (t x b) -> p t x b", t=QT, b=8),
                                    w_p.rearrange("p (t x b) -> p t x b", t=QT, b=8),
                                    blk_ok[:].rearrange("p t (o b) -> p t o b", o=1).broadcast_to([128, QT, NH, 8]),
                                    ALU.mult)); steps.settle()
            steps(dve.tensor_reduce(mx, by_row, AX, ALU.add)); steps.settle()
            steps(dve.tensor_scalar(mx, mx, 0.5, None, ALU.max)); steps.settle()
            steps(dve.reciprocal(mx, mx)); steps.settle()
            steps(dve.tensor_tensor(mx.rearrange("p (t x) -> p t x", t=QT), mx.rearrange("p (t x) -> p t x", t=QT),
                                    gate_p[:, :, 0:NH], ALU.mult)); steps.settle()
            dve.tensor_tensor(by_row, by_row, wide, ALU.mult).then_inc(q["pp_ready"], 1)
            dve.wait_ge(q["onew_in_psum"], 1)
            dve.tensor_copy(onew[:].rearrange("p x d -> p (x d)"), ps[:, 4, :]).then_inc(q["onew_ready"], 1)
            dve.wait_ge(q["ptp_in_psum"], 1)
            dve.tensor_copy(ptp[0:64].rearrange("p t c -> p (t c)"), ps[0:64, 6, :]).then_inc(q["ptp_ready"], 1)



            units = [(t, br) for t in range(QT) for br in range(2)]
            U = len(units)
            dve.wait_ge(q["pads_ready"], 2)
            def prompt_queries(r):
                for g in range(G):
                    gp = slice(g * HD, (g + 1) * HD)
                    last = dve.tensor_scalar(qs[gp, g:g + 1, :], zr[gp, DS(r, 1), 0:SEQ], SCALE, None, ALU.mult)
                last.then_inc(q["qs_ready"], 1)

            def prompt_head(r):
                steps(dve.tensor_copy(gate_r[:].rearrange("p t (x o) -> p t x o", o=1),
                                      gate_p[:, :, NH:BR * NH].rearrange("p t (x r) -> p t x r", r=R)[:, :, :, DS(r, 1)]))
                for j in range(U + 1):
                    if j < U:
                        t, br = units[j]
                        dve.wait_ge(q["scores"], r * U + (j + 1))
                        dve.tensor_reduce(small[:, C_PNM + 2 * j:C_PNM + 2 * j + 2],
                                          ps[:, 2 * (j % 2):2 * (j % 2) + 2, 0:(t + 1) * 128], AX, ALU.max,
                                          negate=True).then_inc(q["negmax"], 1)
                    if j >= 1:
                        k = j - 1
                        t, br = units[k]
                        dve.wait_ge(q["probs"], r * U + (k + 1))
                        if k >= 2:
                            dve.wait_ge(q["probs_t"], r * U + (k - 1))
                        steps(dve.reciprocal(small[:, C_REC + 2 * k:C_REC + 2 * k + 2],
                                             small[:, C_PSUM + 2 * k:C_PSUM + 2 * k + 2])); steps.settle()
                        for g in range(G):
                            last = dve.tensor_scalar(norm_diag[k % 2][:, g, :], ident[:], small[:, C_REC + 2 * k + g:C_REC + 2 * k + g + 1],
                                                     gate_r[:, t, 2 * br + g:2 * br + g + 1], ALU.mult, ALU.mult)
                        last.then_inc(q["diag_ready"], 1)
                dve.wait_ge(q["op_ready"], 1)
                dve.wait_ge(q["pv"], (r + 1) * U + ONE)
                dve.tensor_tensor(po[:, DS(r, 1), :], ps[:, 6:7, :], po[:, DS(r, 1), :], ALU.add).then_inc(q["o_added"], 1)

            def queries(b, n, scored):
                dve.wait_ge(q["s_scores"], scored + ONE)
                dve.tensor_copy(qn[b][:].rearrange("p (o r) -> p o r", o=1), qbd[:, DS(n, 1), :]
                                ).then_inc(q["qn_ready"], 1)

            def keys_s(n):
                for m in range(1, 9, 2):
                    dve.wait_ge(q["kt_in_psum"], n * 9 + (m + 1))
                    if m == 1:
                        dve.wait_ge(q["s_scores"], n + ONE)
                    dve.tensor_copy(kt[:, 4 * m:4 * m + 4, :].rearrange("p k t -> p (k t)"), ps[:, 1, :]
                                    ).then_inc(q["kt_by_dve"], 1)

            def negmax_s(n):
                dve.wait_ge(q["s_scores"], n + 1 + ONE)
                dve.tensor_reduce(cb[:, DS(n, 1), 0, OB - 1], ps[:, 2:4, :].rearrange("p b t -> p (b t)"), AX, ALU.max,
                                  negate=True)
                dve.tensor_reduce(cb[:, DS(n, 1), 1, OB - 1], ps[:, 4, 0:128], AX, ALU.max, negate=True
                                  ).then_inc(q["s_negmax"], 1)

            def probs_t_s(n):
                dve.wait_ge(q["s_probs_t"], n + 1 + ONE)
                dve.tensor_copy(pwt[:, 0:4, :].rearrange("p k t -> p (k t)"), ps[:, 5, :]).then_inc(q["s_pt_dve"], 1)

            def out_s(b, i, n):
                dve.wait_ge(q[f"s_pv{b}"], i + 1 + ONE)
                dve.tensor_copy(cb[:, DS(n, 1), :, 0:128].rearrange("p o b d -> p (o b) d"),
                                ps[:, 7, 0:256].rearrange("p (b d) -> p b d", b=2)).then_inc(q["s_o"], 1)

            dve.wait_ge(q["state_stored"], 16 * (NB + 1))
            prompt_queries(0)
            with dve.Fori(0, R) as r:
                steps.enter(r, 0, U + 1)
                prompt_head(r)
                queries(0, r * 2, r * 2)
                queries(1, r * 2 + 1, r * 2)
                keys_s(r * 2)
                negmax_s(r * 2)
                dve.wait_ge(q["pv"], (r + 1) * U + ONE)
                keys_s(r * 2 + 1)
                negmax_s(r * 2 + 1)
                probs_t_s(r * 2)
                out_s(0, r, r * 2)
                dve.wait_ge(q["scores"], (r + 1) * U)
                prompt_queries(r + 1)
                probs_t_s(r * 2 + 1)
                out_s(1, r, r * 2 + 1)
            steps.leave(R)

            dve.wait_ge(q["maxima_in_psum"], 1)
            steps(dve.tensor_reduce(neg_row[:], ps[0:16, 0, 0:128].rearrange("p (c r) -> p r c", c=CH), AX, ALU.min))
            steps.settle()
            dve.tensor_copy(neg_rep[:], neg_row[:].rearrange("p (o r) -> p o r", o=1).broadcast_to([16, CH, NS])
                            ).then_inc(q["m_ready"], 1)
            dve.wait_ge(q["maxima_in_psum"], 2)
            steps(dve.tensor_copy(neg_all[:], ps[:, 1, 0:16])); steps.settle()
            cbf = cb[:].rearrange("p n b o -> p (n b) o")
            dve.tensor_tensor(chunk_w[:], neg_all[:], cbf[:, :, OB - 1], ALU.subtract).then_inc(q["exponents_ready"], 1)
            dve.wait_ge(q["powers_ready"], 1)
            dve.tensor_tensor(cbf[:, :, 0:OB - 1], cbf[:, :, 0:OB - 1],
                              chunk_w[:].rearrange("p (x o) -> p x o", o=1).broadcast_to([128, 16, OB - 1]), ALU.mult)
            dve.tensor_scalar(cbf[:, :, OB - 1], neg_all[:], 1.0 / CH, None, ALU.mult).then_inc(q["cb_scaled"], 1)
            dve.wait_ge(q["at_hi"], 1)
            dve.tensor_tensor(xl[:, R:KC, :], yconv[:], xh[:, R:KC, :].bitcast(F32), ALU.subtract
                              ).then_inc(q["at_lo"], 1)
            dve.wait_ge(q["comb_in_psum"], 1)
            steps(dve.tensor_copy(comb[:].rearrange("p n b o -> p n (b o)"), ps[:, 2:4, 0:2 * OB]))
            steps.settle()
            F = C_F
            four = lambda c: small[:, c:c + 4].rearrange("p (b n) -> p b n", b=2)
            neg_c = comb[:, :, :, OB - 1].rearrange("p n b -> p b n")
            sum_c = comb[:, :, :, OB - 2].rearrange("p n b -> p b n")
            steps(dve.tensor_tensor(four(F + 8), neg_c, four(C_NNM), ALU.min)); steps.settle()
            dve.tensor_tensor(four(F), four(F + 8), neg_c, ALU.subtract)
            dve.tensor_tensor(four(F + 4), four(F + 8), four(C_NNM), ALU.subtract).then_inc(q["exponents_ready"], 1)
            dve.wait_ge(q["powers_ready"], 2)
            steps(dve.tensor_tensor(four(F + 12), four(F), sum_c, ALU.mult))
            steps(dve.tensor_tensor(four(F + 16), four(F + 4), four(C_NSUM), ALU.mult)); steps.settle()
            steps(dve.tensor_tensor(four(F + 20), four(F + 12), four(F + 16), ALU.add)); steps.settle()
            steps(dve.reciprocal(four(F + 24), four(F + 20))); steps.settle()
            steps(dve.tensor_tensor(four(F + 28), four(F), four(F + 24), ALU.mult))
            steps(dve.tensor_tensor(four(F + 32), four(F + 4), four(F + 24), ALU.mult)); steps.settle()
            for k in range(4):
                steps(dve.tensor_scalar(onew[:, k, :], onew[:, k, :], small[:, F + 32 + k:F + 33 + k], None, ALU.mult))
            steps.settle()
            for k in range(4):
                br, nh = k // 2, k % 2
                last = dve.scalar_tensor_tensor(ofin[:, nh, br, :], comb[:, nh, br, 0:128], small[:, F + 28 + k:F + 29 + k],
                                                onew[:, k, :], ALU.mult, ALU.add)
            last.then_inc(q["ofin_ready"], 1)
            dve.wait_ge(q["at_hi"], 2)
            dve.tensor_tensor(xl[:, 0:R, 0:SEQ], po[:], xh[:, 0:R, 0:SEQ].bitcast(F32), ALU.subtract
                              ).then_inc(q["at_lo"], 1)
            dve.wait_ge(q["ofin_in_psum"], 1)
            for g in range(G):
                gp = slice(g * HD, (g + 1) * HD)
                for br in range(BR):
                    for nh in range(2):
                        steps(dve.tensor_tensor(
                            os_all[gp, br, nh, :, :, :],
                            ps[gp, 4 + br, nh * 128:(nh + 1) * 128].rearrange(
                                "p (n g r q) -> p n g r q", n=4, g=G, r=R)[:, :, g, :, :],
                            gate_s[gp, br * R:(br + 1) * R, nh * 16:(nh + 1) * 16].rearrange(
                                "p r (n q) -> p n r q", q=NQ), ALU.mult))
            steps.settle()
            sum_o = os_all[:].rearrange("p b h n r q -> p b (h n) r q")
            out_o = os_sum[:].rearrange("p r n q -> p n r q")
            steps(dve.tensor_tensor(out_o, sum_o[:, 0], sum_o[:, 1], ALU.add)); steps.settle()
            dve.tensor_tensor(out_o, out_o, sum_o[:, 2], ALU.add).then_inc(q["os_ready"], 1)
            dve.wait_ge(q["at_hi"], 3)
            dve.tensor_tensor(xl[:, 0:R, SEQ:T], os_sum[:].rearrange("p r n q -> p r (n q)"),
                              xh[:, 0:R, SEQ:T].bitcast(F32), ALU.subtract).then_inc(q["at_lo"], 1)

            def add_out(t):
                s = t % 2
                dve.wait_ge(w_used[s], USES["out"][s] + t // 2 + 1)
                xt = x[:, t, :].rearrange("p (h t) -> p h t", h=2)
                dve.tensor_tensor(xt, ps[:, 2 * s:2 * s + 2, 0:HALF], xt, ALU.add).then_inc(q["out_added"], 1)
                dve.wait_ge(q["out_added"], t + 1)
                dve.wait_ge(csum_step, KC + 1 + t + 1)
                dve.tensor_tensor(csum[:], x[:, t, :], csum[:], ALU.add).then_inc(csum_step, 1)

            split_w(0, USES["out"][0])
            dve.wait_ge(q["residual"], KC)
            dve.wait_ge(q["at_lo"], 3)
            dve.memset(csum[:], 0.0).then_inc(csum_step, 1)
            for t in range(1, KC):
                split_w(t % 2, USES["out"][t % 2] + t // 2)
                add_out(t - 1)
            add_out(KC - 1)
            norm_values(1)
            ffn_values(1)
            norm_values(2)
            for t in range(QT + 1):
                w = 128 if t < QT else NS
                dve.wait_ge(q["y_in_psum"], t + 1)
                dve.tensor_copy(yout[0:w, t, 512:1024], ps[0:w, 5 + 2 * (t % 2), :]).then_inc(q["y_by_dve"], 1)


_INS = ["x_prompt", "x_sample", "cache_cmp_kv", "cache_sel_kv", "state_win_kv", "state_conv", "page_table",
        "ffa_gate", "ffa_up", "ffa_down", "ln1_g", "ln1_b", "w_in", "b_in", "w_conv", "cmp_w1", "cmp_w2", "cmp_pe",
        "w_out", "ln2_g", "ln2_b", "ffb_gate", "ffb_up", "ffb_down", "ln3_g", "ln3_b"]
_OUTS = [(1, SEQ, D), (NB, NQ, D), (1, 1, SEQ, 2, G, HD), (1, 1, SEQ, 2, G, HD), (1, 1, WIN, 2, G, HD),
         (1, 1, 2, DC), (1, NB, NQ, 2, G, HD), (1, NB, NQ, 2, G, HD), (1, NB, WIN, 2, G, HD), (1, NB, 2, DC)]


def kernel(**inputs):
    import numpy as _np
    import concourse.bacc as _bacc
    from concourse import mybir as _mybir
    from concourse.bass_utils import run_bass_kernel_spmd as _run

    nc = _bacc.Bacc("TRN2", target_bir_lowering=False, num_devices=1)
    arrays, args = {}, []
    for name in _INS:
        a = _np.ascontiguousarray(inputs[name])
        arrays[f"in_{name}_dram"] = a
        args.append(nc.dram_tensor(f"in_{name}_dram", a.shape, _mybir.dt.from_np(a.dtype), kind="ExternalInput").ap())
    for i, shape in enumerate(_OUTS):
        args.append(nc.dram_tensor(f"out_{i}_dram", shape, _mybir.dt.float32, kind="ExternalOutput").ap())
    trunk(nc, *args)
    r = _run(nc, [arrays], core_ids=[0])
    return tuple(r.results[0][f"out_{i}_dram"] for i in range(len(_OUTS)))
```
